# Optimizing a Trainium2 kernel written in Bass

```python
import jax, jax.numpy as jnp
from jax import lax
import numpy as np

D_MODEL = 1024
BATCH = 1
SEQ = 512
DEPTH = 2

N_MIXERS = 2
N_HEADS = 8
QK_NOPE_DIM = 128
QK_ROPE_DIM = 64
V_HEAD_DIM = 128
Q_LORA_RANK = 512
KV_LORA_RANK = 256
ROPE_THETA = 10000.0
Q_BLOCK = 128
POOL_WINDOWS = (2, 4, 8, 16)
N_POOL_GROUPS = len(POOL_WINDOWS)
POOL_GROUP_DIM = D_MODEL // N_POOL_GROUPS
D_FF_DENSE = 2688
N_EXPERTS = 8
TOP_K = 2
D_FF_EXPERT = 1344
MOE_BLOCK = 256
RMS_EPS = 1e-6
N_MLA_LAYERS = (DEPTH + 1) // 2
N_POOL_LAYERS = DEPTH // 2

kernel_name = "hybrid_mla_pool_moe_decoder"

def rms_norm(x, g):
    xf = x.astype(jnp.float32)
    y = xf * lax.rsqrt(jnp.mean(xf * xf, axis=-1, keepdims=True) + RMS_EPS)
    return (y * g.astype(jnp.float32)).astype(x.dtype)

def rope_tables(positions):
    inv_freq = ROPE_THETA ** (-jnp.arange(0, QK_ROPE_DIM, 2, dtype=jnp.float32) / QK_ROPE_DIM)
    ang = positions.astype(jnp.float32)[..., None] * inv_freq
    return jnp.cos(ang), jnp.sin(ang)

def apply_rope(x, cos, sin):
    xf = x.astype(jnp.float32)
    x1, x2 = jnp.split(xf, 2, axis=-1)
    return jnp.concatenate([x1 * cos - x2 * sin, x2 * cos + x1 * sin], axis=-1).astype(x.dtype)

def mla(h, cos, sin, w_down, q_norm, w_uq, kv_norm, w_ukv, w_o):
    B, S, _ = h.shape
    down = h @ w_down
    c_q, c_kv, k_rope = jnp.split(down, [Q_LORA_RANK, Q_LORA_RANK + KV_LORA_RANK], axis=-1)
    q = (rms_norm(c_q, q_norm) @ w_uq).reshape(B, S, N_HEADS, QK_NOPE_DIM + QK_ROPE_DIM)
    q_nope, q_rope = q[..., :QK_NOPE_DIM], q[..., QK_NOPE_DIM:]
    q_rope = apply_rope(q_rope, cos[:, :, None, :], sin[:, :, None, :])
    k_rope = apply_rope(k_rope, cos, sin)
    kv = (rms_norm(c_kv, kv_norm) @ w_ukv).reshape(B, S, N_HEADS, QK_NOPE_DIM + V_HEAD_DIM)
    k_nope, v = kv[..., :QK_NOPE_DIM], kv[..., QK_NOPE_DIM:]
    scale = (QK_NOPE_DIM + QK_ROPE_DIM) ** -0.5
    q_nope = q_nope * scale
    q_rope = q_rope * scale
    outs = []
    for i in range(S // Q_BLOCK):
        q0, q1 = i * Q_BLOCK, (i + 1) * Q_BLOCK
        s = (jnp.einsum('bqhd,bkhd->bhqk', q_nope[:, q0:q1], k_nope[:, :q1])
             + jnp.einsum('bqhr,bkr->bhqk', q_rope[:, q0:q1], k_rope[:, :q1]))
        mask = jnp.arange(q0, q1)[:, None] >= jnp.arange(q1)[None, :]
        s = jnp.where(mask, s.astype(jnp.float32), -jnp.inf)
        p = jax.nn.softmax(s, axis=-1).astype(v.dtype)
        outs.append(jnp.einsum('bhqk,bkhd->bqhd', p, v[:, :q1]))
    o = jnp.concatenate(outs, axis=1).reshape(B, S, N_HEADS * V_HEAD_DIM)
    return o @ w_o

def multiscale_pool(h, pool_w, pool_scale):
    B, S, D = h.shape
    hf = h.astype(jnp.float32)
    t = jnp.arange(1, S + 1, dtype=jnp.float32)
    groups = []
    for g, w in enumerate(POOL_WINDOWS):
        hg = hf[..., g * POOL_GROUP_DIM:(g + 1) * POOL_GROUP_DIM]
        cs = jnp.cumsum(hg, axis=1)
        cs_lag = jnp.pad(cs[:, :S - w], ((0, 0), (w, 0), (0, 0)))
        cnt = jnp.minimum(t, float(w))[None, :, None]
        groups.append((cs - cs_lag) / cnt - hg)
    z = jnp.stack(groups, axis=2).astype(h.dtype)
    y = jnp.einsum('bsgc,gcd->bsgd', z, pool_w).reshape(B, S, D)
    return y * pool_scale

def swiglu(h, w_gate, w_up, w_down):
    return (jax.nn.silu(h @ w_gate) * (h @ w_up)) @ w_down

def moe_swiglu(h, router, w_gate, w_up, w_down):
    B, S, D = h.shape
    N = B * S
    NK = N * TOP_K
    xf = h.reshape(N, D)
    logits = (xf @ router).astype(jnp.float32)
    top_v, top_i = lax.top_k(logits, TOP_K)
    gates = jax.nn.softmax(top_v, axis=-1)
    flat_e = top_i.reshape(-1).astype(jnp.int32)
    flat_tok = jnp.arange(NK, dtype=jnp.int32) // TOP_K
    flat_g = gates.reshape(-1)
    order = jnp.argsort(flat_e)
    sorted_e = flat_e[order]
    counts = jnp.bincount(flat_e, length=N_EXPERTS).astype(jnp.int32)
    padded = (counts + MOE_BLOCK - 1) // MOE_BLOCK * MOE_BLOCK
    pad_end = jnp.cumsum(padded)
    pad_start = pad_end - padded
    start = jnp.cumsum(counts) - counts
    rank = jnp.arange(NK, dtype=jnp.int32) - start[sorted_e]
    dest = pad_start[sorted_e] + rank
    n_blocks = -(-NK // MOE_BLOCK) + N_EXPERTS
    P = n_blocks * MOE_BLOCK
    buf_tok = jnp.zeros((P,), jnp.int32).at[dest].set(flat_tok[order])
    buf_gate = jnp.zeros((P,), jnp.float32).at[dest].set(flat_g[order])
    block_e = jnp.clip(jnp.searchsorted(pad_end, jnp.arange(n_blocks, dtype=jnp.int32) * MOE_BLOCK,
                                        side='right'), 0, N_EXPERTS - 1).astype(jnp.int32)
    xb = xf[buf_tok].reshape(n_blocks, MOE_BLOCK, D)

    def expert_block(args):
        xblk, e = args
        return swiglu(xblk, w_gate[e], w_up[e], w_down[e])

    yb = lax.map(expert_block, (xb, block_e)).reshape(P, D)
    y = jnp.zeros((N, D), h.dtype).at[buf_tok].add(yb * buf_gate[:, None].astype(yb.dtype))
    return y.reshape(B, S, D)

def setup_inputs(seed: int = 0) -> dict:
    key = jax.random.key(seed)
    ks = iter(jax.random.split(key, 32))

    def w(shape, fan_in):
        return jax.random.normal(next(ks), shape, jnp.float32) * (fan_in ** -0.5)

    def gain(shape):
        return 1.0 + 0.05 * jax.random.normal(next(ks), shape, jnp.float32)

    LA, LB = N_MLA_LAYERS, N_POOL_LAYERS
    x = jax.random.normal(next(ks), (BATCH, SEQ, D_MODEL), jnp.float32)
    positions = (jnp.arange(SEQ, dtype=jnp.int32)[None, :]
                 + jax.random.randint(next(ks), (BATCH, 1), 0, 1024, dtype=jnp.int32))
    return {
        "x": x,
        "positions": positions,
        "attn_norm": gain((DEPTH, D_MODEL)),
        "ffn_norm": gain((DEPTH, D_MODEL)),
        "mla_w_down": w((LA, D_MODEL, Q_LORA_RANK + KV_LORA_RANK + QK_ROPE_DIM), D_MODEL),
        "mla_q_norm": gain((LA, Q_LORA_RANK)),
        "mla_w_uq": w((LA, Q_LORA_RANK, N_HEADS * (QK_NOPE_DIM + QK_ROPE_DIM)), Q_LORA_RANK),
        "mla_kv_norm": gain((LA, KV_LORA_RANK)),
        "mla_w_ukv": w((LA, KV_LORA_RANK, N_HEADS * (QK_NOPE_DIM + V_HEAD_DIM)), KV_LORA_RANK),
        "mla_w_o": w((LA, N_HEADS * V_HEAD_DIM, D_MODEL), N_HEADS * V_HEAD_DIM),
        "pool_w": w((LB, N_POOL_GROUPS, POOL_GROUP_DIM, POOL_GROUP_DIM), POOL_GROUP_DIM),
        "pool_scale": gain((LB, D_MODEL)),
        "ffn_w_gate": w((LA, D_MODEL, D_FF_DENSE), D_MODEL),
        "ffn_w_up": w((LA, D_MODEL, D_FF_DENSE), D_MODEL),
        "ffn_w_down": w((LA, D_FF_DENSE, D_MODEL), D_FF_DENSE),
        "moe_router": w((LB, D_MODEL, N_EXPERTS), D_MODEL),
        "moe_w_gate": w((LB, N_EXPERTS, D_MODEL, D_FF_EXPERT), D_MODEL),
        "moe_w_up": w((LB, N_EXPERTS, D_MODEL, D_FF_EXPERT), D_MODEL),
        "moe_w_down": w((LB, N_EXPERTS, D_FF_EXPERT, D_MODEL), D_FF_EXPERT),
        "final_norm": gain((D_MODEL,)),
    }

def reference(x, positions, attn_norm, ffn_norm, mla_w_down, mla_q_norm, mla_w_uq, mla_kv_norm,
              mla_w_ukv, mla_w_o, pool_w, pool_scale, ffn_w_gate, ffn_w_up, ffn_w_down,
              moe_router, moe_w_gate, moe_w_up, moe_w_down, final_norm):
    h = x
    cos, sin = rope_tables(positions)
    for layer in range(DEPTH):
        a = layer // 2
        hn = rms_norm(h, attn_norm[layer])
        if layer % N_MIXERS == 0:
            h = h + mla(hn, cos, sin, mla_w_down[a], mla_q_norm[a], mla_w_uq[a], mla_kv_norm[a],
                        mla_w_ukv[a], mla_w_o[a])
        else:
            h = h + multiscale_pool(hn, pool_w[a], pool_scale[a])
        hn = rms_norm(h, ffn_norm[layer])
        if layer % 2 == 0:
            h = h + swiglu(hn, ffn_w_gate[a], ffn_w_up[a], ffn_w_down[a])
        else:
            h = h + moe_swiglu(hn, moe_router[a], moe_w_gate[a], moe_w_up[a], moe_w_down[a])
    return rms_norm(h, final_norm)


_drawn_inputs = setup_inputs


def setup_inputs(seed=0):
    import zlib

    import numpy as np

    out = dict(_drawn_inputs(seed))
    spreads = {}
    factors = {'mla_q_norm': 2.741}
    for name, (base, spread) in spreads.items():
        noise = np.random.default_rng([zlib.crc32(name.encode()), seed]).standard_normal(out[name].shape)
        drawn = base * np.exp(spread * noise) if base else spread * noise
        out[name] = __import__('jax').numpy.asarray(drawn.astype(out[name].dtype))
    for name, factor in factors.items():
        out[name] = (out[name] * factor).astype(out[name].dtype)
    return out
```

```python
from contextlib import ExitStack

import concourse.bass as bass
import numpy as np
from concourse import mybir

F32 = mybir.dt.float32
F32R = mybir.dt.float32r
BF16 = mybir.dt.bfloat16
I32 = mybir.dt.int32
ACT = mybir.ActivationFunctionType
ALU = mybir.AluOpType
AX = mybir.AxisListType

P = 128
D = 1024
S = 512
T = S // P
KD = D // P
H = 8
NOPE = 128
ROPE = 64
VD = 128
QR = 512
KVR = 256
DOWN = QR + KVR + ROPE
FF = 2688
FT = FF // P
FG = 3
FI = FT // FG
E = 8
FE = 1344
FEF = FE // P
FTAIL = FE - FEF * P
WINDOWS = (2, 4, 8, 16)
WMAX = max(WINDOWS)
GD = D // len(WINDOWS)
EPS = 1e-6
SCALE = (NOPE + ROPE) ** -0.5
NEG = -1e30
THETA = 10000.0

C = 144
CH = C // 2
JMAX = E + 2 * S // (C + 1)
XROWS = (JMAX + 1) * C
ZP = CH
MACTS = FEF + 1
AHEAD = 8
JUNITS = 3 * FEF + 2

ROUND = 1.5 * 2.0 ** 23
TWO_PI = (6.28125, 0.00193500518798828125, 2 * np.pi - 6.28125 - 0.00193500518798828125)
PI_IN = 3.1415925

UNIT = 1024
SLOTS = 8
STAGES = 8
STAGES_OWN = 6


class plan_weights:

    def __init__(self):
        self.at = {}
        flat = []

        def add(name, slots, stages, twice=()):
            for j, (slot, stage) in enumerate(zip(slots, stages)):
                flat.append(((name, j), slot, stage, 2 if j in twice else 1))

        add("down", range(8), (0, 1, 2, 3, 4, 5, 0, 1))
        for _ in range(H // 2):
            add("pair", (0, 1, 2), (2, 3, 4))
        add("wo", (3, 4, 5, 6, 7, 0, 1, 2), (5, 0, 1, 2, 3, 4, 5, 0))
        for _ in range(FI):
            add("ffn", (0, 1, 2, 3, 0, 1, 4, 5, 6), (0, 1, 2, 3, 4, 5, 0, 1, 2))
        add("pool", (7, 2), (3, 4))
        self.split = len(flat)
        add("pre", (None,) * 4, (2, 3, 4, 5))
        for _ in range(3):
            for _ in range((FEF - 2) // 2):
                add("step", (None,) * 6, range(6))
            add("tail", (None,) * 8, (0, 1, 6, 7, 2, 3, 4, 5), twice=(1,))
        last, uses, seen = {}, [0] * STAGES, {}
        for n, (place, slot, stage, dmas) in enumerate(flat):
            uses[stage] += dmas
            back = n - last[stage] if stage in last else None
            last[stage] = n
            seen.setdefault(place, []).append((n, uses[stage], back, slot, stage))
        for place, times in seen.items():
            inner = 4 if place[0] == "step" else 1
            backs = [b for _, _, b, _, _ in times if b is not None]
            n0, u0, _, slot, stage = times[0]
            dn, du = (times[1][0] - n0, times[1][1] - u0) if len(times) > 1 else (0, 0)
            jn, ju = (times[inner][0] - n0, times[inner][1] - u0) if len(times) > inner else (0, 0)
            if place[0] == "tail":
                dn = du = 0
            self.at[place] = (n0, u0, dn, du, jn, ju, min(backs) if backs else None, slot, stage)

    def unit(self, name, j, i=0, job=0):
        n0, _, dn, _, jn, _, _, _, _ = self.at[name, j]
        return i * dn + job * jn + n0

    def landed(self, name, j, i=0, job=0):
        _, u0, _, du, _, ju, _, _, _ = self.at[name, j]
        return (i * du + job * ju + u0) * 16

    def back(self, name, j):
        return self.at[name, j][6]

    def slot(self, name, j):
        return self.at[name, j][7]

    def stage(self, name, j):
        return self.at[name, j][8]


def trunk(nc, a, out):
    plan = plan_weights()
    with ExitStack() as ctx:
        def sb(name, shape, dt=F32):
            return ctx.enter_context(nc.sbuf_tensor(name, shape, dt))

        def sem(name):
            return ctx.enter_context(nc.semaphore(name))

        bank = [ctx.enter_context(nc.psum_tensor(f"bank{b}", [P, 512], F32)) for b in range(8)]
        w_hi = sb("w_hi", [P, SLOTS, UNIT], F32R)
        w_lo = sb("w_lo", [P, SLOTS, UNIT], F32R)
        stage_own = sb("stage_own", [P, STAGES_OWN, UNIT])
        big_hi = sb("big_hi", [P, 8 * S], F32R)
        big_lo = sb("big_lo", [P, 8 * S], F32R)
        act_hi_mem = sb("act_hi_mem", [P, 6 * S], F32R)
        act_lo_mem = sb("act_lo_mem", [P, 6 * S], F32R)
        h = sb("h", [P, T, D])
        scratch = sb("scratch", [P, 9216])
        cos_t = sb("cos_t", [P, T, ROPE])
        sin_t = sb("sin_t", [P, T, ROPE])
        ident = sb("ident", [P, P])
        ident_b = sb("ident_b", [P, P], BF16)
        causal = sb("causal", [P, P], BF16)
        ones_b = sb("ones_b", [P, P], BF16)
        before_b = sb("before_b", [P, P], BF16)
        zeros = sb("zeros", [P, P])
        band = sb("band", [P, 4, P + WMAX])
        band0 = sb("band0", [P, 4, WMAX])
        krT = sb("krT", [P, S])
        e_act = sb("e_act", [P, 2, C])
        router = sb("router", [P, KD, E])
        eps_t = sb("eps_t", [P, 1])
        sumsq = sb("sumsq", [P, 24])
        rms = sb("rms", [P, 24])
        neg_max = sb("neg_max", [P, 8])
        row_sum = sb("row_sum", [P, 8])
        row_inv = sb("row_inv", [P, 8])
        picked = sb("picked", [P, T, E], BF16)
        gate0 = sb("gate0", [P, T])
        gate1 = sb("gate1", [P, T])
        dest = sb("dest", [P, 2 * T], I32)
        table = sb("table", [1, 32], I32)
        posi = sb("posi", [P, T], I32)
        iota_e = sb("iota_e", [P, E])
        iota_j = sb("iota_j", [1, 16])

        hnT_hi, hnT_lo = (m[:, :].rearrange("p (k s) -> p k s", k=8) for m in (big_hi, big_lo))
        oT_hi, oT_lo, zT_hi, zT_lo = hnT_hi, hnT_lo, hnT_hi, hnT_lo
        cqT_hi, cqT_lo = (m[:, 0:4 * S].rearrange("p (k s) -> p k s", k=4) for m in (act_hi_mem, act_lo_mem))
        ckvT_hi, ckvT_lo = (m[:, 4 * S:6 * S].rearrange("p (k s) -> p k s", k=2) for m in (act_hi_mem, act_lo_mem))
        f_hi, f_lo = (m[:, 0:FG * S].rearrange("p (k s) -> p k s", k=FG) for m in (act_hi_mem, act_lo_mem))

        def view(at, n, k=None):
            v = scratch[:, at:at + n]
            return v if k is None else v.rearrange("p (k n) -> p k n", k=k)

        xn = view(0, T * D, T)
        junk = view(4096, 1024)
        cn = view(5120, 1792, 2)
        krope_tmp = view(6912, 128, 2)
        gain_c = view(7040, QR + KVR)
        freq = view(5120, ROPE // 2)
        posf = view(5152, T)
        angle, turns, folded, over = (view(5184 + P * n, P, T) for n in range(4))
        trig_arg = view(7808, 384).rearrange("p (a t n) -> p a t n", a=3, t=T)
        gain = view(8192, D)
        qn = view(0, 1024, 2)
        kn = view(1024, 1024, 2)
        v_nat = view(2048, 1024, T)
        qrT = view(3072, 512)
        qr_nat = view(3584, 512)
        rope_tmp = view(4096, 1024, 2)
        probs = view(5120, 2560, 2)
        probsT = view(7680, 1280)
        f_silu = view(4096, 1024, 2)
        f_act = view(5120, 1024, 2)
        xnT = view(5120, 1024, 8)
        pscale = view(6144, 1024)
        ptmp = view(7168, 512)
        route = view(7168, 1024)
        stage_more = view(0, 2048, 2)
        yn = scratch[0:CH, 2048:4096].rearrange("p (k n) -> p k n", k=2)
        xg = scratch[0:CH, 4096:6144].rearrange("p (k n) -> p k n", k=2)
        yT = view(6144, KD * C, KD)
        xT = view(6144 + KD * C, KD * C, KD)
        e_silu = krT[:, 0:2 * C].rearrange("p (k n) -> p k n", k=2)
        e_up = e_silu[:, 1, :]
        y_in = view(0, 4096, 4)
        final = view(4096, 2048, 2)
        fjunk = view(6144, 1024)

        def stage(s):
            return stage_own[:, s, :] if s < STAGES_OWN else stage_more[:, s - STAGES_OWN, :]

        xbuf = nc.dram_tensor("xbuf", (XROWS, D), F32, kind="Internal").ap()
        ybuf = nc.dram_tensor("ybuf", (JMAX * C, D), F32, kind="Internal").ap()

        landed = [sem(f"landed{s}") for s in range(STAGES)]
        x_landed = [sem(f"x_landed{t}") for t in range(T)]
        gain_landed = sem("gain_landed")
        gainc_landed = sem("gainc_landed")
        freq_landed = sem("freq_landed")
        pos_landed = sem("pos_landed")
        router_landed = sem("router_landed")
        pscale_landed = sem("pscale_landed")
        xg_landed = sem("xg_landed")
        zero_stored = sem("zero_stored")
        scattered = sem("scattered")
        y_stored = sem("y_stored")
        y_gathered = [sem(f"y_gathered{t}") for t in range(2)]
        out_stored = [sem(f"out_stored{t}") for t in range(2)]
        consts_ready = sem("consts_ready")
        counts_ready = sem("counts_ready")
        counts_inv = sem("counts_inv")
        pool_step = sem("pool_step")
        yn_free = sem("yn_free")

        weight_hi = sem("weight_hi")
        weight_lo = sem("weight_lo")
        std_ready = sem("std_ready")
        act_step = sem("act_step")
        xnT_hi = sem("xnT_hi")
        xnT_lo = sem("xnT_lo")
        xn_ready = sem("xn_ready")
        dve_step = sem("dve_step")
        trig_ready = sem("trig_ready")
        trig_done = sem("trig_done")
        roped = sem("roped")
        iotas_ready = sem("iotas_ready")
        xnT_done = sem("xnT_done")
        c_done = sem("c_done")
        c_std = sem("c_std")
        c_ready = sem("c_ready")
        cT_done = sem("cT_done")
        cT_hi = sem("cT_hi")
        cT_lo = sem("cT_lo")
        down_freed = sem("down_freed")
        proj_done = sem("proj_done")
        proj_act = sem("proj_act")
        proj_dve = sem("proj_dve")
        scores_done = sem("scores_done")
        max_ready = sem("max_ready")
        exp_ready = sem("exp_ready")
        inv_ready = sem("inv_ready")
        probs_ready = sem("probs_ready")
        pT_done = sem("pT_done")
        pT_act = sem("pT_act")
        pT_dve = sem("pT_dve")
        pv_done = sem("pv_done")
        o_hi = sem("o_hi")
        o_lo = sem("o_lo")
        wo_done = sem("wo_done")
        wo_freed = sem("wo_freed")
        h_attn = sem("h_attn")
        gu_done = sem("gu_done")
        silu_ready = sem("silu_ready")
        prod_ready = sem("prod_ready")
        act_hi = sem("act_hi")
        act_lo = sem("act_lo")
        ffn_done = sem("ffn_done")
        h_ffn = sem("h_ffn")
        z_done = sem("z_done")
        z_hi = sem("z_hi")
        z_lo = sem("z_lo")
        mix_done = sem("mix_done")
        h_mix = sem("h_mix")
        logits_done = sem("logits_done")
        chosen = sem("chosen")
        exp_gate = sem("exp_gate")
        rank_done = sem("rank_done")
        routed = sem("routed")
        xT_done = sem("xT_done")
        xT_ready = sem("xT_ready")
        expert_used = sem("expert_used")
        yT_ready = sem("yT_ready")
        y_nat_done = sem("y_nat_done")
        y_ready = sem("y_ready")
        h_final = sem("h_final")
        out_ready = sem("out_ready")

        block = ctx.enter_context(nc.Block())

        gains = {"attn0": a["attn_norm"][0:1], "ffn0": a["ffn_norm"][0:1], "attn1": a["attn_norm"][1:2],
                 "ffn1": a["ffn_norm"][1:2], "final": a["final_norm"].rearrange("(o d) -> o d", o=1)}
        rows_of = {"down": a["mla_w_down"][0], "wo": a["mla_w_o"][0]}
        w_uq = a["mla_w_uq"][0].rearrange("(k p) n -> p k n", p=P)
        w_ukv = a["mla_w_ukv"][0].rearrange("(k p) n -> p k n", p=P)
        f_gate, f_up = (a[n][0].rearrange("(k p) n -> p k n", p=P) for n in ("ffn_w_gate", "ffn_w_up"))
        pool_w = a["pool_w"][0].rearrange("g (k p) n -> p (g k) n", p=P)
        m_gate, m_up = (a[n][0].rearrange("e (k p) n -> e p k n", p=P) for n in ("moe_w_gate", "moe_w_up"))
        m_down = a["moe_w_down"][0]

        @block.sync
        def _(sp):
            def load(name, j, pieces, i=0, job=0):
                back = plan.back(name, j)
                if name in ("step", "tail"):
                    sp.wait_ge(expert_used, plan.unit(name, j, i, job) - (back - 1) + (AHEAD - plan.split))
                elif name == "pre":
                    sp.wait_ge(weight_lo, plan.split)
                elif back is not None:
                    sp.wait_ge(weight_lo, plan.unit(name, j, i, job) - (back - 1))
                s = plan.stage(name, j)
                for dst, src in pieces(stage(s)):
                    sp.dma_start(dst, src).then_inc(landed[s], 16)

            def cols(st, k, n):
                return st[:, 0:k * n].rearrange("p (k n) -> p k n", k=k)

            def x_in(t):
                sp.dma_start(h[:, t, :], a["x"][0, t * P:(t + 1) * P, :]).then_inc(x_landed[t], 16)

            def rows(name, k):
                load(name, k, lambda st: [(st[:, 0:rows_of[name].shape[1]], rows_of[name][k * P:(k + 1) * P, :])])

            x_in(0)
            for k in range(4):
                rows("down", k)
            x_in(1)
            for k in range(4, 6):
                rows("down", k)
            x_in(2)
            x_in(3)
            for k in range(6, 8):
                rows("down", k)

            with sp.Fori(0, H // 2) as pair:
                for j in range(2):
                    load("pair", j, lambda st: [(cols(st, 2, 384), w_uq[:, 2 * j:2 * j + 2, bass.ds(pair * 384, 384)])], pair)
                load("pair", 2, lambda st: [(cols(st, 2, 512), w_ukv[:, :, bass.ds(pair * 512, 512)])], pair)
            for k in range(8):
                rows("wo", k)

            with sp.Fori(0, FI) as i:
                for j in range(FG):
                    for q, w in enumerate((f_gate, f_up)):
                        load("ffn", 2 * j + q, lambda st: [(cols(st, 8, P), w[:, :, bass.ds(i * (FG * P) + j * P, P)])], i)
                for j in range(FG):
                    load("ffn", 2 * FG + j,
                         lambda st: [(st, a["ffn_w_down"][0, bass.ds(i * (FG * P) + j * P, P), :])], i)
            for j in range(2):
                load("pool", j, lambda st: [(cols(st, 4, GD), pool_w[:, 4 * j:4 * j + 4, :])])

            def expert_cols(w, e, f, n=P):
                return w[bass.ds(e, 1), :, :, f * P:f * P + n].rearrange("o p k n -> p (o k) n")

            for j, (w, f) in enumerate(((m_gate, 0), (m_up, 0), (m_gate, 1), (m_up, 1))):
                load("pre", j, lambda st: [(cols(st, 8, P), w[0, :, :, f * P:(f + 1) * P])])

            sp.wait_ge(routed, 1)
            sp.wait_ge(scattered, 16 * 2 * T)
            jobs = sp.value_load(table[0:1, 0:1], min_val=E, max_val=JMAX)
            with sp.Fori(0, jobs) as job:
                e = sp.value_load(table[0:1, bass.ds(job + 1, 1)], min_val=0, max_val=E - 1)
                e_next = sp.value_load(table[0:1, bass.ds(job + 2, 1)], min_val=0, max_val=E - 1)

                def columns(w, ee, off):
                    return w[bass.ds(ee, 1), :, :, bass.ds(off, P)].rearrange("o p k n -> p (o k) n")

                def down_rows(off, n=P):
                    return m_down[bass.ds(e, 1), bass.ds(off, n), :].rearrange("o p n -> p (o n)")

                with sp.Fori(0, (FEF - 2) // 2) as i:
                    for s in range(2):
                        off = i * (2 * P) + s * P
                        load("step", 3 * s, lambda st: [(st, down_rows(off))], i, job)
                        load("step", 3 * s + 1, lambda st: [(cols(st, 8, P), columns(m_gate, e, off + 2 * P))], i, job)
                        load("step", 3 * s + 2, lambda st: [(cols(st, 8, P), columns(m_up, e, off + 2 * P))], i, job)
                load("tail", 0, lambda st: [(st, down_rows((FEF - 2) * P))], 0, job)
                load("tail", 1, lambda st: [(cols(st, 8, P)[:, :, q * FTAIL:(q + 1) * FTAIL],
                                             expert_cols(w, e, FEF, FTAIL)) for q, w in enumerate((m_gate, m_up))], 0, job)
                load("tail", 2, lambda st: [(st, down_rows((FEF - 1) * P))], 0, job)
                load("tail", 3, lambda st: [(st[0:FTAIL, :], down_rows(FEF * P, FTAIL))], 0, job)
                for j, (w, f) in enumerate(((m_gate, 0), (m_up, 0), (m_gate, 1), (m_up, 1))):
                    load("tail", 4 + j, lambda st: [(cols(st, 8, P), expert_cols(w, e_next, f))], 0, job)
            for done in out_stored:
                sp.wait_ge(done, 16 * T // 2)

        @block.gpsimd
        def _(pool):
            steps = [0]

            def link(ins):
                steps[0] += 1
                ins.then_inc(pool_step, 1)
                pool.wait_ge(pool_step, steps[0])

            g = nc.gpsimd
            pool.dma_start(gain, gains["attn0"].partition_broadcast(P).rearrange("p o d -> p (o d)")).then_inc(gain_landed, 16)
            pool.dma_start(posi[:, :], a["positions"].rearrange("o (t p) -> p (o t)", p=P),
                           allow_slow_non_contiguous=True).then_inc(pos_landed, 16)
            pool.dma_start(freq, a["rope_freq"].partition_broadcast(P).rearrange("p o d -> p (o d)")
                           ).then_inc(freq_landed, 16)
            pool.dma_start(gain_c[:, 0:QR], a["mla_q_norm"].partition_broadcast(P).rearrange("p o d -> p (o d)")
                           ).then_inc(gainc_landed, 16)
            pool.dma_start(gain_c[:, QR:], a["mla_kv_norm"].partition_broadcast(P).rearrange("p o d -> p (o d)")
                           ).then_inc(gainc_landed, 16)
            pool.dma_start(router[:, :, :], a["moe_router"][0].rearrange("(k p) e -> p k e", p=P),
                           allow_slow_non_contiguous=True).then_inc(router_landed, 16)
            g.memset(eps_t[:, :], EPS)
            g.memset(ident[:, :], 0.0)
            g.memset(ident_b[:, :], 0.0)
            g.memset(causal[:, :], 0.0)
            g.memset(zeros[:, :], 0.0)
            g.memset(ones_b[:, :], 1.0)
            link(g.memset(before_b[:, :], 1.0))
            for m in (ident, ident_b):
                last = g.affine_select(out=m[:, :], in_=m[:, :], compare_op=ALU.not_equal, fill=1.0, base=0,
                                       pattern=[[-1, P]], channel_multiplier=1)
            last.then_inc(consts_ready, 1)
            g.affine_select(out=causal[:, :], in_=causal[:, :], compare_op=ALU.is_ge, fill=NEG, base=0,
                            pattern=[[-1, P]], channel_multiplier=1)
            g.affine_select(out=before_b[:, :], in_=before_b[:, :], compare_op=ALU.is_ge, fill=0.0, base=-1,
                            pattern=[[1, P]], channel_multiplier=-1).then_inc(consts_ready, 1)
            g.iota(iota_e[:, :], [[1, E]], base=0, channel_multiplier=0, allow_small_or_imprecise_dtypes=True
                   ).then_inc(iotas_ready, 1)
            g.iota(iota_j[:, :], [[1, 16]], base=0, channel_multiplier=0, allow_small_or_imprecise_dtypes=True
                   ).then_inc(iotas_ready, 1)
            for n, w in enumerate(WINDOWS):
                g.memset(band[:, n, :], 1.0 / w)
                g.iota(band0[:, n, :], [[1, WMAX]], base=1, channel_multiplier=0, allow_small_or_imprecise_dtypes=True
                       ).then_inc(pool_step, 1)
                steps[0] += 1
            pool.wait_ge(pool_step, steps[0])
            for n, w in enumerate(WINDOWS):
                g.tensor_scalar(band0[:, n, :], band0[:, n, :], float(w), None, ALU.min).then_inc(counts_ready, 1)
            pool.wait_ge(counts_inv, 1)
            for n, w in enumerate(WINDOWS):
                for m, width in ((band, P + WMAX), (band0, WMAX)):
                    link(g.affine_select(out=m[:, n, :], in_=m[:, n, :], compare_op=ALU.is_ge, fill=0.0, base=0,
                                         pattern=[[1, width]], channel_multiplier=-1))
                    link(g.affine_select(out=m[:, n, :], in_=m[:, n, :], compare_op=ALU.is_ge, fill=0.0, base=w - 1,
                                         pattern=[[-1, width]], channel_multiplier=1))
                link(g.tensor_tensor(band[:, n, 0:P], band[:, n, 0:P], ident[:, :], ALU.subtract))
                link(g.tensor_tensor(band0[:, n, :], band0[:, n, :], ident[:, 0:WMAX], ALU.subtract))
            pool.sem_inc(consts_ready, 1)

            pool.wait_ge(down_freed, KD)
            half = (JMAX + 1) // 2 * C
            for rows in (xbuf[0:half, :], xbuf[half:, :], ybuf[E * C:, :]):
                pool.dma_start(rows.rearrange("(p r) (c n) -> p (r c) n", p=ZP, n=P),
                               zeros[0:ZP, :].unsqueeze(1).broadcast_to([ZP, rows.shape[0] // ZP * (D // P), P])
                               ).then_inc(zero_stored, 16)

            pool.wait_ge(pv_done, H)
            pool.wait_ge(pT_dve, H)
            pool.wait_ge(xn_ready, T)
            pool.dma_start(gain, gains["ffn0"].partition_broadcast(P).rearrange("p o d -> p (o d)")).then_inc(gain_landed, 16)
            pool.wait_ge(xn_ready, 2 * T)
            pool.dma_start(gain, gains["attn1"].partition_broadcast(P).rearrange("p o d -> p (o d)")).then_inc(gain_landed, 16)
            pool.dma_start(pscale, a["pool_scale"].partition_broadcast(P).rearrange("p o d -> p (o d)")
                           ).then_inc(pscale_landed, 16)
            pool.wait_ge(xn_ready, 3 * T)
            pool.dma_start(gain, gains["ffn1"].partition_broadcast(P).rearrange("p o d -> p (o d)")).then_inc(gain_landed, 16)

            pool.wait_ge(routed, 1)
            pool.wait_ge(zero_stored, 48)
            for c in range(2 * T):
                pool.indirect_dma_start(out=xbuf, out_offset=bass.IndirectOffsetOnAxis(ap=dest[:, c:c + 1], axis=0),
                                        in_=xn[:, c % T, :], in_offset=None).then_inc(scattered, 16)
            pool.wait_ge(scattered, 16 * 2 * T)
            pool.sem_inc(yn_free, 1)
            pool.dma_start(xg, xbuf[0:C, :].rearrange("(k p) n -> p k n", p=CH)).then_inc(xg_landed, 16)
            jobs = pool.value_load(table[0:1, 0:1], min_val=E, max_val=JMAX)
            with pool.Fori(0, jobs) as job:
                pool.wait_ge(xT_done, job + 1)
                pool.dma_start(xg, xbuf[bass.ds(job * C + C, C), :].rearrange("(k p) n -> p k n", p=CH)
                               ).then_inc(xg_landed, 16)
                pool.wait_ge(y_ready, job + 2)
                pool.dma_start(ybuf[bass.ds(job * C, C), :].rearrange("(k p) n -> p k n", p=CH), yn
                               ).then_inc(y_stored, 16)
                pool.wait_ge(y_stored, job * 16 + 16)
                pool.sem_inc(yn_free, 1)
            pool.dma_start(gain, gains["final"].partition_broadcast(P).rearrange("p o d -> p (o d)")).then_inc(gain_landed, 16)
            for t in range(T):
                if t >= 2:
                    pool.wait_ge(h_final, t - 1)
                for k in range(2):
                    pool.indirect_dma_start(out=y_in[:, 2 * (t % 2) + k, :], out_offset=None, in_=ybuf,
                                            in_offset=bass.IndirectOffsetOnAxis(ap=dest[:, k * T + t:k * T + t + 1], axis=0)
                                            ).then_inc(y_gathered[t % 2], 16)

        @block.scalar
        def _(act):
            s = nc.scalar
            steps = [0]

            def link(ins):
                steps[0] += 1
                ins.then_inc(act_step, 1)
                act.wait_ge(act_step, steps[0])

            def split(name, j, i=0, job=0, n=UNIT, parts=P):
                st, sl = plan.stage(name, j), plan.slot(name, j)
                act.wait_ge(landed[st], plan.landed(name, j, i, job))
                s.copy(w_hi[0:parts, sl, 0:n], stage(st)[0:parts, 0:n]).then_inc(weight_hi, 1)

            def norm_std(q, t, where=junk):
                link(s.activation(where, h[:, t, :], ACT.Square, scale=D ** -0.5, accum_out=sumsq[:, q:q + 1]))
                s.activation(rms[:, q:q + 1], sumsq[:, q:q + 1], ACT.Sqrt, bias=eps_t[:, 0:1]).then_inc(std_ready, 1)

            def norm_hi(q, t):
                act.wait_ge(xnT_done, q + 1)
                for b in range(2):
                    last = s.copy(hnT_hi[:, 4 * b:4 * b + 4, t * P:(t + 1) * P],
                                  bank[b][:, :].rearrange("p (k n) -> p k n", k=4))
                last.then_inc(xnT_hi, 1)

            act.wait_ge(consts_ready, 1)
            for t in range(T):
                act.wait_ge(x_landed[t], 16)
                norm_std(t, t)

            def c_std_of(t):
                if t < T - 1:
                    act.wait_ge(c_done, t + 1)
                else:
                    act.wait_ge(down_freed, KD)
                b = 4 + 2 * (t % 2)
                s.activation(junk[:, 0:QR], bank[b][:, :], ACT.Square, scale=QR ** -0.5, accum_out=sumsq[:, 16 + t:17 + t])
                link(s.activation(junk[:, QR:QR + KVR], bank[b + 1][:, 0:KVR], ACT.Square, scale=KVR ** -0.5,
                                  accum_out=sumsq[:, 20 + t:21 + t]))
                s.activation(rms[:, 16 + t:17 + t], sumsq[:, 16 + t:17 + t], ACT.Sqrt, bias=eps_t[:, 0:1])
                s.activation(rms[:, 20 + t:21 + t], sumsq[:, 20 + t:21 + t], ACT.Sqrt, bias=eps_t[:, 0:1]).then_inc(c_std, 1)

            def c_hi(t):
                act.wait_ge(cT_done, t + 1)
                tok = slice(t * P, (t + 1) * P)
                s.copy(cqT_hi[:, :, tok], bank[2][:, :].rearrange("p (k n) -> p k n", k=4))
                s.copy(ckvT_hi[:, :, tok], bank[3][:, 0:2 * P].rearrange("p (k n) -> p k n", k=2)).then_inc(cT_hi, 1)

            act.wait_ge(trig_ready, 1)
            s.activation(sin_t[:, :, 32:64], trig_arg[:, 0], ACT.Sin)
            s.activation(cos_t[:, :, 0:32], trig_arg[:, 1], ACT.Sin)
            s.activation(cos_t[:, :, 32:64], trig_arg[:, 1], ACT.Sin)
            s.activation(sin_t[:, :, 0:32], trig_arg[:, 2], ACT.Sin).then_inc(trig_done, 1)

            norm_hi(0, 0)
            for k in range(4):
                split("down", k, n=DOWN)
            norm_hi(1, 1)
            for k in range(4, 8):
                split("down", k, n=DOWN)
            c_std_of(0)
            for t in range(2, T):
                norm_hi(t, t)
                c_hi(t - 2)
                c_std_of(t - 1)
            c_hi(2)
            c_std_of(3)
            c_hi(3)
            for j in range(3):
                act.wait_ge(down_freed, j + 1)
                split("pair", j, n=(768, 768, 1024)[j])

            def attention(pair, following):
                act.wait_ge(proj_done, pair * 7 + 1)
                s.mul(qn[:, 0, :], bank[0][:, :], SCALE).then_inc(proj_act, 1)
                act.wait_ge(proj_done, pair * 7 + 5)
                s.mul(qn[:, 1, :], bank[5][:, :], SCALE).then_inc(proj_act, 1)
                act.wait_ge(proj_done, pair * 7 + 7)
                s.mul(qrT, bank[7][:, :], SCALE).then_inc(proj_act, 1)

                def exps(hd):
                    for qb in range(T):
                        n = (qb + 1) * P
                        at = qb * (qb + 1) // 2 * P
                        col = 4 * hd + qb
                        act.wait_ge(max_ready, pair * 8 + col + 1)
                        s.activation(probs[:, hd, at:at + n], bank[col][:, 0:n], ACT.Exp, bias=neg_max[:, col:col + 1],
                                     accum_out=row_sum[:, col:col + 1]).then_inc(exp_ready, 1)

                def turned(hd):
                    act.wait_ge(pT_done, pair * 2 + hd + 1)
                    if hd:
                        act.wait_ge(pv_done, pair * 2 + 1)
                    s.copy(probsT[:, 0:512], bank[4 * hd][:, :])
                    s.copy(probsT[:, 896:1280], bank[4 * hd + 2][:, 0:384]).then_inc(pT_act, 1)

                def head_out(hd):
                    act.wait_ge(pv_done, pair * 2 + hd + 1)
                    s.copy(oT_hi[:, bass.ds(pair * 2 + hd, 1), :], bank[4 * hd + 3][:, :].unsqueeze(1)).then_inc(o_hi, 1)

                exps(0)
                following(0)
                exps(1)
                turned(0)
                head_out(0)
                following(1)
                turned(1)
                following(2)
                head_out(1)

            with act.Fori(0, H // 2 - 1) as pair:
                attention(pair, lambda part: split("pair", part, pair + 1, n=(768, 768, 1024)[part]))
            attention(H // 2 - 1, lambda part: [split("wo", k) for k in ((0, 1, 2), (3, 4, 5), (6, 7))[part]])

            for t in range(T):
                act.wait_ge(h_attn, t + 1)
                norm_std(T + t, t)
                if t:
                    norm_hi(T + t - 1, t - 1)
            for j in range(4):
                act.wait_ge(wo_freed, (6, 7, 8, 8)[j])
                split("ffn", j)
            norm_hi(2 * T - 1, T - 1)

            def ffn_act(i, j):
                act.wait_ge(gu_done, i * FG + j + 1)
                s.activation(f_silu[:, j % 2, :], bank[2 * (j % 2)][:, :], ACT.Silu).then_inc(silu_ready, 1)
                act.wait_ge(prod_ready, i * FG + j + 1)
                s.copy(f_hi[:, j, :], f_act[:, j % 2, :]).then_inc(act_hi, 1)

            def ffn(i, following):
                ffn_act(i, 0)
                for j in range(4, 9):
                    split("ffn", j, i)
                ffn_act(i, 1)
                ffn_act(i, 2)
                following()

            with act.Fori(0, FI - 1) as i:
                ffn(i, lambda: [split("ffn", j, i + 1) for j in range(4)])
            ffn(FI - 1, lambda: [split("pool", j) for j in range(2)])

            for t in range(T):
                act.wait_ge(h_ffn, 8 * (FI - 1) + 4 + t + 1)
                norm_std(2 * T + t, t)
            for d in range(KD):
                act.wait_ge(z_done, d + 1)
                s.copy(zT_hi[:, d, :], bank[d % 4][:, :]).then_inc(z_hi, 1)

            def rows_T(t):
                act.wait_ge(xnT_done, 2 * T + t + 1)
                s.copy(xnT[:, 0:4, :], bank[0][:, :].rearrange("p (k n) -> p k n", k=4)).then_inc(xnT_hi, 1)

            for t in range(T):
                act.wait_ge(h_mix, t + 1)
                norm_std(3 * T + t, t)
                if t:
                    rows_T(t - 1)
            rows_T(T - 1)
            act.wait_ge(chosen, 1)
            s.activation(gate1[:, :], gate1[:, :], ACT.Exp).then_inc(exp_gate, 1)

            act.wait_ge(routed, 1)
            act.sem_inc(y_ready, 1)
            jobs = act.value_load(table[0:1, 0:1], min_val=E, max_val=JMAX)
            with act.Fori(0, jobs) as job:
                used = job * JUNITS + AHEAD

                def silu(par, count):
                    act.wait_ge(expert_used, used + count)
                    s.activation(e_silu[:, par, :], bank[2 * par][:, 0:C], ACT.Silu).then_inc(silu_ready, 1)

                silu(0, 2)
                with act.Fori(0, (FEF - 2) // 2) as i:
                    silu(1, i * 6 + 4)
                    silu(0, i * 6 + 7)
                silu(1, JUNITS - 4)
                act.wait_ge(expert_used, used + (JUNITS - 2))
                act.wait_ge(prod_ready, job * MACTS + (FT + MACTS - 1))
                s.activation(e_silu[0:FTAIL, 0, :], bank[0][0:FTAIL, 0:C], ACT.Silu)
                s.copy(e_up[0:FTAIL, :], bank[0][FTAIL:P, 0:C]).then_inc(silu_ready, 1)
                act.wait_ge(expert_used, used + JUNITS)
                for b, k0, k1 in ((4, 0, 3), (5, 3, 6), (6, 6, 8)):
                    last = s.copy(yT[:, k0:k1, :], bank[b][:, 0:(k1 - k0) * C].rearrange("p (k n) -> p k n", n=C))
                last.then_inc(yT_ready, 1)
                act.wait_ge(y_nat_done, job + 1)
                act.wait_ge(yn_free, job + 1)
                for b in range(4):
                    last = s.copy(yn[:, b // 2, (b % 2) * 512:(b % 2) * 512 + 512], bank[4 + b][0:CH, :])
                last.then_inc(y_ready, 1)

            for t in range(T):
                act.wait_ge(h_final, t + 1)
                link(s.activation(fjunk, h[:, t, :], ACT.Square, scale=D ** -0.5, accum_out=sumsq[:, t:t + 1]))
                s.activation(rms[:, t:t + 1], sumsq[:, t:t + 1], ACT.Sqrt, bias=eps_t[:, 0:1]).then_inc(std_ready, 1)
                act.wait_ge(out_ready, t + 1)
                act.dma_start(out[0, t * P:(t + 1) * P, :], final[:, t % 2, :]).then_inc(out_stored[t % 2], 16)
            for done in out_stored:
                act.wait_ge(done, 16 * T // 2)

        @block.tensor
        def _(pe):
            t_ = nc.tensor

            def mm3(dst, st_hi, st_lo, mv_hi, mv_lo, start, stop, check=False):
                t_.matmul(dst, st_lo, mv_hi, start=start, stop=False, skip_group_check=check)
                t_.matmul(dst, st_hi, mv_lo, start=False, stop=False, skip_group_check=check)
                return t_.matmul(dst, st_hi, mv_hi, start=False, stop=stop, skip_group_check=check)

            def weights(name, j, i=0, job=0):
                pe.wait_ge(weight_lo, plan.unit(name, j, i, job) + 1)
                return plan.slot(name, j)

            def transposes(src, banks):
                for k in range(8):
                    last = t_.transpose(bank[banks[k // 4]][:, k % 4 * P:k % 4 * P + P], src[:, k * P:(k + 1) * P], ident[:, :])
                return last

            def norm_T(q, t):
                pe.wait_ge(xn_ready, q + 1)
                if q:
                    pe.wait_ge(xnT_hi, q)
                    pe.wait_ge(xnT_lo, q)
                transposes(xn[:, t, :], (0, 1)).then_inc(xnT_done, 1)

            def tok(t):
                return slice(t * P, (t + 1) * P)

            def down(t):
                pe.wait_ge(xnT_lo, t + 1)
                if t >= 2:
                    pe.wait_ge(c_ready, t - 1)
                b = 4 + 2 * (t % 2)

                def part(k, half):
                    lo, hi = ((0, QR), (QR, DOWN))[half]
                    sl = weights("down", k)
                    return mm3(bank[b + half][:, 0:hi - lo], hnT_hi[:, k, tok(t)], hnT_lo[:, k, tok(t)],
                               w_hi[:, sl, lo:hi], w_lo[:, sl, lo:hi], k == 0, k == KD - 1)

                for k in range(KD):
                    for half in range(2):
                        last = part(k, half)
                    if t == T - 1:
                        last.then_inc(down_freed, 1)
                if t < T - 1:
                    last.then_inc(c_done, 1)

            def latents_T(t):
                pe.wait_ge(c_ready, t + 1)
                if t:
                    pe.wait_ge(cT_lo, t)
                for k in range(7):
                    last = t_.transpose(bank[2 + k // 4][:, k % 4 * P:k % 4 * P + P], cn[:, t % 2, k * P:(k + 1) * P],
                                        ident[:, :])
                last.then_inc(cT_done, 1)

            pe.wait_ge(consts_ready, 2)
            norm_T(0, 0)
            norm_T(1, 1)
            down(0)
            for t in range(2, T):
                norm_T(t, t)
                latents_T(t - 2)
                down(t - 1)
            latents_T(2)
            down(3)
            latents_T(3)

            def attention(pair):
                sl = [weights("pair", j, pair) for j in range(3)]

                def wq(part, k, lo, hi):
                    m = (w_hi, w_lo)[part][:, sl[k // 2], 0:768].rearrange("p (k n) -> p k n", k=2)
                    return m[:, k % 2, lo:hi]

                def wq_rope(part, k):
                    m = (w_hi, w_lo)[part][:, sl[k // 2], 0:768].rearrange("p (k h n) -> p k h n", k=2, h=2)
                    return m[:, k % 2, :, NOPE:NOPE + ROPE]

                def wkv(part, k, lo, hi):
                    m = (w_hi, w_lo)[part][:, sl[2], :].rearrange("p (k n) -> p k n", k=2)
                    return m[:, k, lo:hi]

                def wv(part, k):
                    m = (w_hi, w_lo)[part][:, sl[2], :].rearrange("p (k h n) -> p k h n", k=2, h=2)
                    return m[:, k, :, NOPE:NOPE + VD]

                def q_head(hd, b):
                    for k in range(4):
                        last = mm3(bank[b][:, :], wq(0, k, hd * 192, hd * 192 + NOPE), wq(1, k, hd * 192, hd * 192 + NOPE),
                                   cqT_hi[:, k, :], cqT_lo[:, k, :], k == 0, k == 3)
                    last.then_inc(proj_done, 1)

                def k_head(hd, b):
                    for k in range(2):
                        last = mm3(bank[b][:, :], wkv(0, k, hd * 256, hd * 256 + NOPE), wkv(1, k, hd * 256, hd * 256 + NOPE),
                                   ckvT_hi[:, k, :], ckvT_lo[:, k, :], k == 0, k == 1)
                    last.then_inc(proj_done, 1)

                q_head(0, 0)
                k_head(0, 1)
                pe.wait_ge(o_lo, pair * 2 + 1)
                for t in range(T):
                    for k in range(2):
                        last = mm3(bank[2 + t // 2][:, t % 2 * 256:t % 2 * 256 + 256].rearrange("p (h n) -> p h n", h=2),
                                   ckvT_hi[:, k, tok(t)], ckvT_lo[:, k, tok(t)], wv(0, k), wv(1, k), k == 0, k == 1)
                last.then_inc(proj_done, 1)
                for t in range(T):
                    for k in range(4):
                        last = mm3(bank[4][:, tok(t)].rearrange("p (h n) -> p h n", h=2),
                                   cqT_hi[:, k, tok(t)], cqT_lo[:, k, tok(t)], wq_rope(0, k), wq_rope(1, k), k == 0, k == 3)
                last.then_inc(proj_done, 1)
                q_head(1, 5)
                k_head(1, 6)
                pe.wait_ge(proj_dve, pair * 4 + 3)
                pe.wait_ge(o_lo, pair * 2 + 2)
                for t in range(T):
                    last = t_.transpose(bank[7][:, tok(t)], qr_nat[:, tok(t)], ident[:, :])
                last.then_inc(proj_done, 1)

                def scores(hd):
                    pe.wait_ge(proj_act, pair * 3 + 3)
                    pe.wait_ge(proj_dve, pair * 4 + (4 if hd else 2))
                    r = slice(ROPE * hd, ROPE * hd + ROPE)
                    for qb in range(T):
                        dst, n = bank[4 * hd + qb], (qb + 1) * P
                        t_.matmul(dst[:, 0:n], qn[:, hd, tok(qb)], kn[:, hd, 0:n], start=True, stop=False)
                        t_.matmul(dst[:, 0:n], qrT[r, tok(qb)], krT[r, 0:n], start=False, stop=False)
                        t_.matmul(dst[:, tok(qb)], ident_b[:, :], causal[:, :], start=False, stop=True
                                  ).then_inc(scores_done, 1)

                def turn(hd):
                    for qb in range(T):
                        pe.wait_ge(probs_ready, pair * 8 + 4 * hd + qb + 1)
                        at = qb * (qb + 1) // 2 * P
                        for kb in range(qb + 1):
                            col = (qb - kb) * P + (256 if kb == 3 else 0)
                            last = t_.transpose(bank[4 * hd + min(kb, 2)][:, col:col + P],
                                                probs[:, hd, at + kb * P:at + kb * P + P], ident[:, :])
                    last.then_inc(pT_done, 1)

                def head_out(hd):
                    pe.wait_ge(pT_act, pair * 2 + hd + 1)
                    pe.wait_ge(pT_dve, pair * 2 + hd + 1)
                    for kb, at in enumerate((0, 512, 896, 1152)):
                        last = t_.matmul(bank[4 * hd + 3][:, kb * P:S],
                                         v_nat[:, kb, hd * VD:(hd + 1) * VD],
                                         probsT[:, at:at + S - kb * P], start=kb == 0, stop=kb == T - 1)
                    last.then_inc(pv_done, 1)

                scores(0)
                scores(1)
                turn(0)
                head_out(0)
                turn(1)
                head_out(1)

            pe.wait_ge(cT_lo, T)
            with pe.Fori(0, H // 2) as pair:
                attention(pair)

            pe.wait_ge(o_lo, 2 + H)

            def project(t):
                if t >= 2:
                    pe.wait_ge(h_attn, t - 1)
                b = 4 + 2 * (t % 2)

                def part(k, half):
                    sl = weights("wo", k)
                    at = slice(512 * half, 512 * half + 512)
                    return mm3(bank[b + half][:, :], oT_hi[:, k, tok(t)], oT_lo[:, k, tok(t)],
                               w_hi[:, sl, at], w_lo[:, sl, at], k == 0, k == H - 1)

                for k in range(H):
                    for half in range(2):
                        last = part(k, half)
                    if t == T - 1:
                        last.then_inc(wo_freed, 1)
                if t < T - 1:
                    last.then_inc(wo_done, 1)

            project(0)
            for t in range(1, T):
                project(t)
                norm_T(T + t - 1, t - 1)
            norm_T(2 * T - 1, T - 1)

            pe.wait_ge(xnT_lo, 2 * T)
            with pe.Fori(0, FI) as i:
                for j in range(FG):
                    if j == 2:
                        pe.wait_ge(prod_ready, i * FG + 1)
                    for q in range(2):
                        sl = weights("ffn", 2 * j + q, i)
                        for k in range(KD):
                            last = mm3(bank[2 * (j % 2) + q][:, :], w_hi[:, sl, k * P:(k + 1) * P], w_lo[:, sl, k * P:(k + 1) * P],
                                       hnT_hi[:, k, :], hnT_lo[:, k, :], k == 0, k == KD - 1)
                    last.then_inc(gu_done, 1)
                sl = [weights("ffn", 2 * FG + j, i) for j in range(FG)]
                pe.wait_ge(act_lo, i * FG + 2)
                for half in range(2):
                    at = slice(512 * half, 512 * half + 512)
                    for j in range(FG):
                        if j == 2 and half == 0:
                            pe.wait_ge(act_lo, i * FG + 3)
                        for t in range(T):
                            if j == 0 and half:
                                pe.wait_ge(h_ffn, i * 8 + t + 1)
                            last = mm3(bank[4 + t][:, :], f_hi[:, j, tok(t)], f_lo[:, j, tok(t)],
                                       w_hi[:, sl[j], at], w_lo[:, sl[j], at], j == 0, j == FG - 1)
                            if j == FG - 1:
                                last.then_inc(ffn_done, 1)

            pe.wait_ge(consts_ready, 3)
            pe.wait_ge(xn_ready, 3 * T)
            for d in range(KD):
                if d >= 4:
                    pe.wait_ge(z_lo, d - 3)
                g = d // 2
                dst = bank[d % 4]
                chunk = [xn[:, t, d * P:(d + 1) * P] for t in range(T)]
                t_.matmul(dst[:, 0:WMAX], chunk[0], band0[:, g, :], start=True, stop=False, skip_group_check=True)
                t_.matmul(dst[:, WMAX:P + WMAX], chunk[0], band[:, g, WMAX:], start=False, stop=False, skip_group_check=True)
                for t in range(1, T):
                    n = P + WMAX if t < T - 1 else P
                    last = t_.matmul(dst[:, t * P:t * P + n], chunk[t], band[:, g, 0:n], start=False, stop=t == T - 1,
                                     skip_group_check=True)
                last.then_inc(z_done, 1)

            def mix(t):
                if t >= 2:
                    pe.wait_ge(h_mix, t - 1)
                for g in range(4):
                    sl = weights("pool", g // 2)
                    for k in range(2):
                        at = ((g % 2) * 2 + k) * GD
                        last = mm3(bank[4 + 2 * (t % 2) + g // 2][:, g % 2 * GD:g % 2 * GD + GD],
                                   zT_hi[:, 2 * g + k, tok(t)], zT_lo[:, 2 * g + k, tok(t)],
                                   w_hi[:, sl, at:at + GD], w_lo[:, sl, at:at + GD], k == 0, k == 1)
                last.then_inc(mix_done, 1)

            def logits(t):
                norm_T_at = 2 * T + t
                pe.wait_ge(xn_ready, 3 * T + t + 1)
                pe.wait_ge(xnT_hi, norm_T_at)
                pe.wait_ge(xnT_lo, norm_T_at)
                transposes(xn[:, t, :], (0, 1)).then_inc(xnT_done, 1)
                pe.wait_ge(xnT_hi, norm_T_at + 1)
                pe.wait_ge(xnT_lo, norm_T_at + 1)
                for k in range(KD):
                    last = t_.matmul(bank[2][:, t * E:(t + 1) * E], xnT[:, k, :], router[:, k, :], start=k == 0, stop=k == KD - 1)
                if t == T - 1:
                    last.then_inc(logits_done, 1)

            pe.wait_ge(router_landed, 16)
            pe.wait_ge(z_lo, KD)
            mix(0)
            for t in range(1, T):
                mix(t)
                logits(t - 1)
            logits(T - 1)

            pe.wait_ge(chosen, 1)
            for t in range(T):
                for c in range(t + 1):
                    last = t_.matmul(bank[3][:, t * E:(t + 1) * E], (before_b if c == t else ones_b)[:, :], picked[:, c, :],
                                     start=c == 0, stop=c == t)
            for c in range(T):
                last = t_.matmul(bank[3][:, T * E:(T + 1) * E], ones_b[:, :], picked[:, c, :], start=c == 0, stop=c == T - 1)
            last.then_inc(rank_done, 1)

            def x_T(at):
                pe.wait_ge(xg_landed, at * 16)
                for k in range(KD):
                    b, k0 = ((1, 0), (7, 3), (3, 6))[k // 3]
                    for q in range(2):
                        col = (k - k0) * C + q * CH
                        last = t_.transpose(bank[b][:, col:col + CH], xg[:, q, k * P:(k + 1) * P], ident[0:CH, 0:CH])
                last.then_inc(xT_done, 1)

            def landed_unit(name, j, i=0, job=0):
                st = plan.stage(name, j)
                pe.wait_ge(landed[st], plan.landed(name, j, i, job))
                return stage(st)

            def columns(dst, w):
                for k in range(KD):
                    last = t_.matmul(dst[:, 0:C], w[:, k * P:(k + 1) * P], xT[:, k, :], start=k == 0, stop=k == KD - 1)
                return last.then_inc(expert_used, 1)

            def gate_up(name, j, par, i=0, job=0):
                for q in range(2):
                    columns(bank[2 * par + q], landed_unit(name, j + q, i, job))

            def down_tile(name, j, par, prod, i=0, job=0, first=False, final=False):
                pe.wait_ge(prod_ready, prod)
                w = landed_unit(name, j, i, job)
                n = FTAIL if final else P
                for k in range(KD):
                    col = k % 3 * C
                    last = t_.matmul(bank[4 + k // 3][:, col:col + C], w[0:n, k * P:(k + 1) * P], e_act[0:n, par, :],
                                     start=first and k % 3 == 0, stop=final, skip_group_check=True)
                last.then_inc(expert_used, 1)

            pe.wait_ge(routed, 1)
            pe.sem_inc(expert_used, AHEAD)
            x_T(1)
            pe.wait_ge(xT_ready, 1)
            gate_up("pre", 0, 0)
            for q in range(2):
                landed_unit("pre", 2 + q)
            jobs = pe.value_load(table[0:1, 0:1], min_val=E, max_val=JMAX)
            with pe.Fori(0, jobs) as job:
                acts = job * MACTS + FT
                turns = (FEF - 2) // 2 - 1
                for q in range(2):
                    columns(bank[2 + q], stage(plan.stage("pre", 2 + q)))
                pe.wait_ge(y_ready, job + 1)
                down_tile("step", 0, 0, acts + 1, 0, job, first=True)
                gate_up("step", 1, 0, 0, job)
                with pe.Fori(0, turns) as i:
                    down_tile("step", 3, 1, acts + i * 2 + 2, i, job)
                    gate_up("step", 4, 1, i, job)
                    down_tile("step", 0, 0, acts + i * 2 + 3, i + 1, job)
                    gate_up("step", 1, 0, i + 1, job)
                down_tile("step", 3, 1, acts + (2 * turns + 2), turns, job)
                gate_up("step", 4, 1, turns, job)
                down_tile("tail", 0, 0, acts + FEF - 1, 0, job)
                columns(bank[0], landed_unit("tail", 1, 0, job))
                pe.wait_ge(prod_ready, acts + FEF)
                x_T(job + 2)
                down_tile("tail", 2, 1, acts + FEF, 0, job)
                down_tile("tail", 3, 0, acts + MACTS, 0, job, final=True)
                pe.wait_ge(xT_ready, job + 2)
                gate_up("tail", 4, 0, 0, job)
                for q in range(2):
                    landed_unit("tail", 6 + q, 0, job)
                pe.wait_ge(yT_ready, job + 1)
                for q in range(2):
                    for k in range(KD):
                        last = t_.transpose(bank[4 + 2 * q + k // 4][0:CH, k % 4 * P:k % 4 * P + P], yT[:, k, q * CH:(q + 1) * CH],
                                            ident[:, :])
                last.then_inc(y_nat_done, 1)

        @block.vector
        def _(dve):
            v = nc.vector
            steps = [0]

            def link(ins):
                steps[0] += 1
                ins.then_inc(dve_step, 1)
                dve.wait_ge(dve_step, steps[0])

            def split(name, j, i=0, job=0, n=UNIT, parts=P):
                st, sl = plan.stage(name, j), plan.slot(name, j)
                dve.wait_ge(weight_hi, plan.unit(name, j, i, job) + 1)
                v.tensor_tensor(w_lo[0:parts, sl, 0:n], stage(st)[0:parts, 0:n], w_hi[0:parts, sl, 0:n],
                                ALU.subtract).then_inc(weight_lo, 1)

            dve.wait_ge(pos_landed, 16)
            dve.wait_ge(freq_landed, 16)
            link(v.tensor_copy(posf, posi[:, :]))
            link(v.tensor_tensor(angle, posf.unsqueeze(2).broadcast_to([P, T, 32]),
                                 freq.unsqueeze(1).broadcast_to([P, T, 32]), ALU.mult))
            link(v.tensor_scalar(turns, angle, 1 / (2 * np.pi), ROUND, ALU.mult, ALU.add))
            link(v.tensor_scalar(turns, turns, ROUND, None, ALU.subtract))
            for part in TWO_PI:
                link(v.scalar_tensor_tensor(angle, turns, -part, angle, ALU.mult, ALU.add))
            link(v.tensor_scalar(over, angle, np.pi / 2, 2 * np.pi, ALU.is_gt, ALU.mult))
            link(v.scalar_tensor_tensor(folded, angle, np.pi / 2, over, ALU.add, ALU.subtract))
            v.tensor_scalar(trig_arg[:, 0], angle, PI_IN, -PI_IN, ALU.min, ALU.max)
            v.tensor_scalar(trig_arg[:, 1], folded, PI_IN, -PI_IN, ALU.min, ALU.max)
            link(v.tensor_scalar(over, angle, -1.0, None, ALU.mult))
            v.tensor_scalar(trig_arg[:, 2], over, PI_IN, -PI_IN, ALU.min, ALU.max).then_inc(trig_ready, 1)
            dve.wait_ge(counts_ready, len(WINDOWS))
            v.reciprocal(band0[:, :, :], band0[:, :, :]).then_inc(counts_inv, 1)

            def norm_rows(q, t):
                dve.wait_ge(std_ready, q + 1)
                col = q if q < 4 * T else q - 4 * T
                link(v.reciprocal(rms[:, col:col + 1], rms[:, col:col + 1]))
                dve.wait_ge(gain_landed, 16 * (q // T + 1))
                v.scalar_tensor_tensor(xn[:, t, :], h[:, t, :], rms[:, col:col + 1], gain, ALU.mult, ALU.mult
                                       ).then_inc(xn_ready, 1)

            def norm_lo(q, t):
                dve.wait_ge(xnT_hi, q + 1)
                for b in range(2):
                    at = (slice(None), slice(4 * b, 4 * b + 4), slice(t * P, (t + 1) * P))
                    last = v.tensor_tensor(hnT_lo[at], bank[b][:, :].rearrange("p (k n) -> p k n", k=4), hnT_hi[at],
                                           ALU.subtract)
                last.then_inc(xnT_lo, 1)

            def rotate(out_, tmp, q, heads, t):
                n = len(range(*t.indices(T)))
                shape = [P, n, heads, ROPE]
                half = [P, n, heads, ROPE // 2]
                v.tensor_tensor(out_, q, cos_t[:, t, :].unsqueeze(2).broadcast_to(shape), ALU.mult)
                v.tensor_tensor(tmp[..., 0:32], q[..., 32:64], sin_t[:, t, 0:32].unsqueeze(2).broadcast_to(half), ALU.mult)
                link(v.tensor_tensor(tmp[..., 32:64], q[..., 0:32], sin_t[:, t, 32:64].unsqueeze(2).broadcast_to(half),
                                     ALU.mult))
                return v.tensor_tensor(out_, out_, tmp, ALU.add)

            def latents(t):
                dve.wait_ge(c_std, t + 1)
                v.reciprocal(rms[:, 16 + t:17 + t], rms[:, 16 + t:17 + t])
                link(v.reciprocal(rms[:, 20 + t:21 + t], rms[:, 20 + t:21 + t]))
                b = 4 + 2 * (t % 2)
                c = cn[:, t % 2, :]
                v.scalar_tensor_tensor(c[:, 0:QR], bank[b][:, :], rms[:, 16 + t:17 + t], gain_c[:, 0:QR], ALU.mult, ALU.mult)
                v.scalar_tensor_tensor(c[:, QR:QR + KVR], bank[b + 1][:, 0:KVR], rms[:, 20 + t:21 + t], gain_c[:, QR:],
                                       ALU.mult, ALU.mult)
                kr = c[:, QR + KVR:DOWN]
                link(rotate(kr.unsqueeze(1).unsqueeze(1), krope_tmp[:, 0, :].unsqueeze(1).unsqueeze(1),
                            bank[b + 1][:, KVR:KVR + ROPE].unsqueeze(1).unsqueeze(1), 1, slice(t, t + 1)))
                v.tensor_copy(c[:, DOWN:DOWN + ROPE], kr).then_inc(c_ready, 1)

            def latents_lo(t):
                dve.wait_ge(cT_hi, t + 1)
                tok = slice(t * P, (t + 1) * P)
                v.tensor_tensor(cqT_lo[:, :, tok], bank[2][:, :].rearrange("p (k n) -> p k n", k=4), cqT_hi[:, :, tok],
                                ALU.subtract)
                v.tensor_copy(krT[:, tok], bank[3][:, 2 * P:3 * P])
                v.tensor_tensor(ckvT_lo[:, :, tok], bank[3][:, 0:2 * P].rearrange("p (k n) -> p k n", k=2),
                                ckvT_hi[:, :, tok], ALU.subtract).then_inc(cT_lo, 1)

            norm_rows(0, 0)
            norm_rows(1, 1)
            norm_lo(0, 0)
            for k in range(4):
                split("down", k, n=DOWN)
            norm_lo(1, 1)
            for k in range(4, 8):
                split("down", k, n=DOWN)
            norm_rows(2, 2)
            norm_rows(3, 3)
            dve.wait_ge(trig_done, 1)
            dve.wait_ge(gainc_landed, 32)
            latents(0)
            for t in range(2, T):
                norm_lo(t, t)
                latents_lo(t - 2)
                latents(t - 1)
            latents_lo(2)
            latents(3)
            latents_lo(3)
            for j in range(3):
                split("pair", j, n=(768, 768, 1024)[j])
            dve.sem_inc(o_lo, 2)

            def attention(pair, following, first):
                dve.wait_ge(proj_done, pair * 7 + 2)
                v.tensor_copy(kn[:, 0, :], bank[1][:, :]).then_inc(proj_dve, 1)
                dve.wait_ge(proj_done, pair * 7 + 3)
                v.tensor_copy(v_nat[:, 0:2, :], bank[2][:, :].rearrange("p (k n) -> p k n", k=2))
                v.tensor_copy(v_nat[:, 2:4, :], bank[3][:, :].rearrange("p (k n) -> p k n", k=2)).then_inc(proj_dve, 1)
                dve.wait_ge(proj_done, pair * 7 + 4)
                shape = "p (t h n) -> p t h n"
                every = slice(0, T)
                q = bank[4][:, :].rearrange(shape, t=T, h=2)
                out_ = qr_nat.rearrange(shape, t=T, h=2)
                tmp = rope_tmp[:, 0, :].rearrange(shape, t=T, h=2)
                for t in range(T):
                    cs = cos_t[:, t, :].unsqueeze(1).broadcast_to([P, 2, ROPE])
                    v.tensor_tensor(out_[:, t], q[:, t], cs, ALU.mult)
                    for lo, hi in ((0, 32), (32, 0)):
                        sn = sin_t[:, t, lo:lo + 32].unsqueeze(1).broadcast_to([P, 2, 32])
                        last = v.tensor_tensor(tmp[:, t, :, lo:lo + 32], q[:, t, :, hi:hi + 32], sn, ALU.mult)
                last.then_inc(roped, 1)
                dve.wait_ge(roped, pair + 1)
                v.tensor_tensor(qr_nat, qr_nat, rope_tmp[:, 0, :], ALU.add).then_inc(proj_dve, 1)
                dve.wait_ge(proj_done, pair * 7 + 6)
                v.tensor_copy(kn[:, 1, :], bank[6][:, :]).then_inc(proj_dve, 1)

                def softmax(hd):
                    def largest(qb):
                        col = 4 * hd + qb
                        dve.wait_ge(scores_done, pair * 8 + col + 1)
                        v.tensor_reduce(neg_max[:, col:col + 1], bank[col][:, 0:(qb + 1) * P], AX.X, ALU.max, negate=True
                                        ).then_inc(max_ready, 1)

                    def divide(qb):
                        col = 4 * hd + qb
                        at, n = qb * (qb + 1) // 2 * P, (qb + 1) * P
                        dve.wait_ge(exp_ready, pair * 8 + col + 1)
                        v.reciprocal(row_inv[:, col:col + 1], row_sum[:, col:col + 1]).then_inc(inv_ready, 1)
                        dve.wait_ge(inv_ready, pair * 8 + col + 1)
                        v.tensor_scalar(probs[:, hd, at:at + n], probs[:, hd, at:at + n], row_inv[:, col:col + 1], None,
                                        ALU.mult).then_inc(probs_ready, 1)

                    largest(0)
                    largest(1)
                    for qb in range(T):
                        divide(qb)
                        if qb + 2 < T:
                            largest(qb + 2)

                def turned(hd):
                    dve.wait_ge(pT_done, pair * 2 + hd + 1)
                    if hd:
                        dve.wait_ge(pv_done, pair * 2 + 1)
                    v.tensor_copy(probsT[:, 512:896], bank[4 * hd + 1][:, 0:384]).then_inc(pT_dve, 1)

                def head_out(hd):
                    dve.wait_ge(o_hi, pair * 2 + hd + 1)
                    at = bass.ds(pair * 2 + hd, 1)
                    v.tensor_tensor(oT_lo[:, at, :], bank[4 * hd + 3][:, :].unsqueeze(1), oT_hi[:, at, :],
                                    ALU.subtract).then_inc(o_lo, 1)

                softmax(0)
                following(0)
                softmax(1)
                turned(0)
                head_out(0)
                following(1)
                turned(1)
                following(2)
                head_out(1)

            with dve.Fori(0, H // 2 - 1) as pair:
                attention(pair, lambda part: split("pair", part, pair + 1, n=(768, 768, 1024)[part]), None)
            attention(H // 2 - 1, lambda part: [split("wo", k) for k in ((0, 1, 2), (3, 4, 5), (6, 7))[part]], None)

            def add_attention(t):
                if t < T - 1:
                    dve.wait_ge(wo_done, t + 1)
                else:
                    dve.wait_ge(wo_freed, H)
                for half in range(2):
                    at = slice(512 * half, 512 * half + 512)
                    last = v.tensor_tensor(h[:, t, at], bank[4 + 2 * (t % 2) + half][:, :], h[:, t, at], ALU.add)
                last.then_inc(h_attn, 1)

            for t in range(T):
                add_attention(t)
                norm_rows(T + t, t)
                if t:
                    norm_lo(T + t - 1, t - 1)
            for j in range(4):
                split("ffn", j)
            norm_lo(2 * T - 1, T - 1)

            def ffn_act(i, j):
                n = i * FG + j + 1
                dve.wait_ge(silu_ready, n)
                v.tensor_tensor(f_act[:, j % 2, :], f_silu[:, j % 2, :], bank[2 * (j % 2) + 1][:, :], ALU.mult
                                ).then_inc(prod_ready, 1)
                dve.wait_ge(act_hi, n)
                v.tensor_tensor(f_lo[:, j, :], f_act[:, j % 2, :], f_hi[:, j, :], ALU.subtract).then_inc(act_lo, 1)

            def ffn(i, following):
                ffn_act(i, 0)
                for j in range(4, 9):
                    split("ffn", j, i)
                ffn_act(i, 1)
                ffn_act(i, 2)
                for half in range(2):
                    following(half)
                    at = slice(512 * half, 512 * half + 512)
                    for t in range(T):
                        dve.wait_ge(ffn_done, i * 8 + 4 * half + t + 1)
                        v.tensor_tensor(h[:, t, at], bank[4 + t][:, :], h[:, t, at], ALU.add).then_inc(h_ffn, 1)

            with dve.Fori(0, FI - 1) as i:
                ffn(i, lambda half: [split("ffn", 2 * half + j, i + 1) for j in range(2)])
            ffn(FI - 1, lambda half: split("pool", half))

            for t in range(T):
                norm_rows(2 * T + t, t)
            for d in range(KD):
                dve.wait_ge(z_hi, d + 1)
                v.tensor_tensor(zT_lo[:, d, :], bank[d % 4][:, :], zT_hi[:, d, :], ALU.subtract).then_inc(z_lo, 1)

            def rows_T(t):
                dve.wait_ge(xnT_done, 2 * T + t + 1)
                v.tensor_copy(xnT[:, 4:8, :], bank[1][:, :].rearrange("p (k n) -> p k n", k=4)).then_inc(xnT_lo, 1)

            def add_mix(t):
                dve.wait_ge(mix_done, t + 1)
                for half in range(2):
                    at = slice(512 * half, 512 * half + 512)
                    link(v.tensor_tensor(ptmp, bank[4 + 2 * (t % 2) + half][:, :], pscale[:, at], ALU.mult))
                    last = v.tensor_tensor(h[:, t, at], h[:, t, at], ptmp, ALU.add)
                    if half == 0:
                        link(last)
                last.then_inc(h_mix, 1)

            dve.wait_ge(pscale_landed, 16)
            for t in range(T):
                add_mix(t)
                norm_rows(3 * T + t, t)
                if t:
                    rows_T(t - 1)
            rows_T(T - 1)

            def tab(n, width=T * E):
                return route[:, n * 32:n * 32 + width]

            def by_expert(n):
                return tab(n).rearrange("p (t e) -> p t e", t=T)

            def per_token(x):
                return x.unsqueeze(2).broadcast_to([P, T, E])

            def per_expert(x):
                return x.unsqueeze(1).broadcast_to([P, T, E])

            logit, eq, first, second, spare = (by_expert(n) for n in range(5))
            best = [tab(5 + n, T) for n in range(4)]
            index, ends, starts, tmp8, count = (tab(9 + n, E) for n in range(5))
            job_no = route[0:1, 640:768].rearrange("p (j e) -> p j e", e=E)
            job_end = route[0:1, 768:896].rearrange("p (j e) -> p j e", e=E)
            job_exp = route[0:1, 896:912]
            place_f = route[:, 912:912 + 2 * T]
            dve.wait_ge(logits_done, 1)
            dve.wait_ge(iotas_ready, 2)
            v.tensor_scalar(index, iota_e[:, :], -float(E), None, ALU.add)
            link(v.tensor_copy(tab(0), bank[2][:, 0:T * E]))

            def pick(logits, top, at, onehot):
                link(v.tensor_reduce(top, logits, AX.X, ALU.max))
                link(v.tensor_tensor(eq, logits, per_token(top), ALU.is_equal))
                link(v.tensor_tensor(eq, eq, per_expert(index), ALU.mult))
                link(v.tensor_reduce(at, eq, AX.X, ALU.min))
                link(v.tensor_tensor(onehot, per_expert(index), per_token(at), ALU.is_equal))

            pick(logit, best[0], best[1], first)
            link(v.scalar_tensor_tensor(spare, first, -1e38, logit, ALU.mult, ALU.add))
            pick(spare, best[2], best[3], second)
            link(v.tensor_tensor(gate1[:, :], best[2], best[0], ALU.subtract))
            v.tensor_tensor(picked[:, :, :], first, second, ALU.add).then_inc(chosen, 1)
            dve.wait_ge(exp_gate, 1)
            link(v.tensor_scalar(gate0[:, :], gate1[:, :], 1.0, None, ALU.add))
            link(v.reciprocal(gate0[:, :], gate0[:, :]))
            link(v.tensor_tensor(gate1[:, :], gate1[:, :], gate0[:, :], ALU.mult))

            dve.wait_ge(rank_done, 1)
            link(v.tensor_copy(count, bank[3][:, T * E:(T + 1) * E]))
            link(v.tensor_scalar(starts, count, float(C), 1.0, ALU.is_gt, ALU.add))
            for more in range(2, -(-S // C)):
                link(v.scalar_tensor_tensor(starts, count, float(more * C), starts, ALU.is_gt, ALU.add))
            link(v.tensor_copy(ends, starts))
            for shift in (1, 2, 4):
                link(v.tensor_copy(tmp8, ends))
                link(v.tensor_tensor(ends[:, shift:], tmp8[:, shift:], tmp8[:, 0:E - shift], ALU.add))
            link(v.tensor_tensor(starts, ends, starts, ALU.subtract))
            link(v.tensor_scalar(starts, starts, float(C), None, ALU.mult))
            link(v.tensor_tensor(spare, bank[3][:, 0:T * E].rearrange("p (t e) -> p t e", t=T), per_expert(starts), ALU.add))
            for n, onehot in enumerate((first, second)):
                link(v.tensor_tensor(eq, onehot, spare, ALU.mult))
                link(v.tensor_reduce(place_f[:, n * T:(n + 1) * T], eq, AX.X, ALU.add))
            link(v.tensor_copy(dest[:, :], place_f))
            link(v.tensor_copy(job_end, ends[0:1, :].unsqueeze(1).broadcast_to([1, 16, E])))
            link(v.tensor_copy(job_no, iota_j[0:1, :].unsqueeze(2).broadcast_to([1, 16, E])))
            link(v.tensor_tensor(job_end, job_end, job_no, ALU.is_le))
            link(v.tensor_reduce(job_exp, job_end, AX.X, ALU.add))
            link(v.tensor_scalar(job_exp, job_exp, float(E - 1), None, ALU.min))
            link(v.tensor_copy(table[0:1, 0:1], ends[0:1, E - 1:E]))
            v.tensor_copy(table[0:1, 1:17], job_exp).then_inc(routed, 1)

            def x_out(at):
                dve.wait_ge(xT_done, at)
                for b, k0, k1 in ((1, 0, 3), (7, 3, 6), (3, 6, 8)):
                    last = v.tensor_copy(xT[:, k0:k1, :], bank[b][:, 0:(k1 - k0) * C].rearrange("p (k n) -> p k n", n=C))
                last.then_inc(xT_ready, 1)

            x_out(1)
            dve.wait_ge(routed, 1)
            jobs = dve.value_load(table[0:1, 0:1], min_val=E, max_val=JMAX)
            with dve.Fori(0, jobs) as job:
                def product(f, par):
                    dve.wait_ge(silu_ready, job * MACTS + f + (FT + 1))
                    v.tensor_tensor(e_act[:, par, :], e_silu[:, par, :], bank[2 * par + 1][:, 0:C], ALU.mult
                                    ).then_inc(prod_ready, 1)

                with dve.Fori(0, FEF // 2) as i:
                    for q in range(2):
                        product(i * 2 + q, q)
                dve.wait_ge(silu_ready, job * MACTS + (FT + MACTS))
                v.tensor_tensor(e_act[0:FTAIL, 0, :], e_silu[0:FTAIL, 0, :], e_up[0:FTAIL, :], ALU.mult
                                ).then_inc(prod_ready, 1)
                x_out(job + 2)

            for t in range(T):
                dve.wait_ge(y_gathered[t % 2], 32 * (t // 2 + 1))
                link(v.scalar_tensor_tensor(h[:, t, :], y_in[:, 2 * (t % 2), :], gate0[:, t:t + 1], h[:, t, :],
                                            ALU.mult, ALU.add))
                v.scalar_tensor_tensor(h[:, t, :], y_in[:, 2 * (t % 2) + 1, :], gate1[:, t:t + 1], h[:, t, :],
                                       ALU.mult, ALU.add).then_inc(h_final, 1)
                dve.wait_ge(std_ready, 4 * T + t + 1)
                link(v.reciprocal(rms[:, t:t + 1], rms[:, t:t + 1]))
                dve.wait_ge(gain_landed, 16 * 5)
                if t >= 2:
                    dve.wait_ge(out_stored[t % 2], 16 * (t // 2))
                v.scalar_tensor_tensor(final[:, t % 2, :], h[:, t, :], rms[:, t:t + 1], gain, ALU.mult, ALU.mult
                                       ).then_inc(out_ready, 1)


_INS = ["x", "positions", "attn_norm", "ffn_norm", "mla_w_down", "mla_q_norm", "mla_w_uq", "mla_kv_norm", "mla_w_ukv",
        "mla_w_o", "pool_w", "pool_scale", "ffn_w_gate", "ffn_w_up", "ffn_w_down", "moe_router", "moe_w_gate", "moe_w_up",
        "moe_w_down", "final_norm"]


def kernel(**inputs):
    import concourse.bacc as _bacc
    from concourse.bass_utils import run_bass_kernel_spmd as _run

    nc = _bacc.Bacc("TRN2", target_bir_lowering=False, num_devices=1)
    arrays = {name: np.ascontiguousarray(inputs[name]) for name in _INS}
    arrays["rope_freq"] = (THETA ** (-np.arange(0, ROPE, 2, dtype=np.float64) / ROPE)).astype(np.float32)[None, :]
    args = {name: nc.dram_tensor(f"in_{name}", v.shape, mybir.dt.from_np(v.dtype), kind="ExternalInput").ap()
            for name, v in arrays.items()}
    out = nc.dram_tensor("out_0", (1, S, D), F32, kind="ExternalOutput").ap()
    trunk(nc, args, out)
    r = _run(nc, [{f"in_{name}": v for name, v in arrays.items()}], core_ids=[0])
    return r.results[0]["out_0"]
```

```python
from contextlib import ExitStack

import concourse.bass as bass
import numpy as np
from concourse import mybir

F32 = mybir.dt.float32
F32R = mybir.dt.float32r
BF16 = mybir.dt.bfloat16
I32 = mybir.dt.int32
ACT = mybir.ActivationFunctionType
ALU = mybir.AluOpType
AX = mybir.AxisListType

P = 128
D = 1024
S = 512
T = S // P
KD = D // P
H = 8
NOPE = 128
ROPE = 64
VD = 128
QR = 512
KVR = 256
DOWN = QR + KVR + ROPE
FF = 2688
FT = FF // P
FG = 3
FI = FT // FG
E = 8
FE = 1344
FEF = FE // P
FTAIL = FE - FEF * P
WINDOWS = (2, 4, 8, 16)
WMAX = max(WINDOWS)
GD = D // len(WINDOWS)
EPS = 1e-6
SCALE = (NOPE + ROPE) ** -0.5
NEG = -1e30
THETA = 10000.0

C = 144
CH = C // 2
JMAX = E + 2 * S // (C + 1)
XROWS = (JMAX + 1) * C
ZP = CH
MACTS = FEF + 1
AHEAD = 8
JUNITS = 3 * FEF + 2

ROUND = 1.5 * 2.0 ** 23
TWO_PI = (6.28125, 0.00193500518798828125, 2 * np.pi - 6.28125 - 0.00193500518798828125)
PI_IN = 3.1415925

UNIT = 1024
SLOTS = 8
STAGES = 8
STAGES_OWN = 6


class plan_weights:

    def __init__(self):
        self.at = {}
        flat = []

        def add(name, slots, stages, twice=()):
            for j, (slot, stage) in enumerate(zip(slots, stages)):
                flat.append(((name, j), slot, stage, 2 if j in twice else 1))

        add("down", range(8), (0, 1, 2, 3, 4, 5, 0, 1))
        add("rope", (0, 1), (2, 3), twice=(0, 1))
        for _ in range(H // 2):
            add("pair", (2, 3), (4, 5), twice=(0,))
        add("wo", (4, 5, 6, 7, 0, 1, 2, 3), (0, 1, 2, 3, 4, 5, 0, 1))
        for _ in range(FI):
            add("ffn", (0, 1, 2, 3, 0, 1, 4, 5, 6), (2, 3, 4, 5, 0, 1, 2, 3, 4))
        add("pool", (7, 2), (5, 0))
        self.split = len(flat)
        add("pre", (None,) * 4, (2, 3, 4, 5))
        for _ in range(3):
            for _ in range((FEF - 2) // 2):
                add("step", (None,) * 6, range(6))
            add("tail", (None,) * 8, (0, 1, 6, 7, 2, 3, 4, 5), twice=(1,))
        last, uses, seen = {}, [0] * STAGES, {}
        for n, (place, slot, stage, dmas) in enumerate(flat):
            uses[stage] += dmas
            back = n - last[stage] if stage in last else None
            last[stage] = n
            seen.setdefault(place, []).append((n, uses[stage], back, slot, stage))
        for place, times in seen.items():
            inner = 4 if place[0] == "step" else 1
            backs = [b for _, _, b, _, _ in times if b is not None]
            n0, u0, _, slot, stage = times[0]
            dn, du = (times[1][0] - n0, times[1][1] - u0) if len(times) > 1 else (0, 0)
            jn, ju = (times[inner][0] - n0, times[inner][1] - u0) if len(times) > inner else (0, 0)
            if place[0] == "tail":
                dn = du = 0
            self.at[place] = (n0, u0, dn, du, jn, ju, min(backs) if backs else None, slot, stage)

    def unit(self, name, j, i=0, job=0):
        n0, _, dn, _, jn, _, _, _, _ = self.at[name, j]
        return i * dn + job * jn + n0

    def landed(self, name, j, i=0, job=0):
        _, u0, _, du, _, ju, _, _, _ = self.at[name, j]
        return (i * du + job * ju + u0) * 16

    def back(self, name, j):
        return self.at[name, j][6]

    def slot(self, name, j):
        return self.at[name, j][7]

    def stage(self, name, j):
        return self.at[name, j][8]


def trunk(nc, a, out):
    plan = plan_weights()
    with ExitStack() as ctx:
        def sb(name, shape, dt=F32):
            return ctx.enter_context(nc.sbuf_tensor(name, shape, dt))

        def sem(name):
            return ctx.enter_context(nc.semaphore(name))

        bank = [ctx.enter_context(nc.psum_tensor(f"bank{b}", [P, 512], F32)) for b in range(8)]
        w_hi = sb("w_hi", [P, SLOTS, UNIT], F32R)
        w_lo = sb("w_lo", [P, SLOTS, UNIT], F32R)
        stage_own = sb("stage_own", [P, STAGES_OWN, UNIT])
        big_hi = sb("big_hi", [P, 8 * S], F32R)
        big_lo = sb("big_lo", [P, 8 * S], F32R)
        act_hi_mem = sb("act_hi_mem", [P, 6 * S], F32R)
        act_lo_mem = sb("act_lo_mem", [P, 6 * S], F32R)
        h = sb("h", [P, T, D])
        scratch = sb("scratch", [P, 9216])
        cos_t = sb("cos_t", [P, T, ROPE])
        sin_t = sb("sin_t", [P, T, ROPE])
        ident = sb("ident", [P, P])
        ident_b = sb("ident_b", [P, P], BF16)
        causal = sb("causal", [P, P], BF16)
        ones_b = sb("ones_b", [P, P], BF16)
        before_b = sb("before_b", [P, P], BF16)
        zeros = sb("zeros", [P, P])
        band = sb("band", [P, 4, P + WMAX])
        band0 = sb("band0", [P, 4, WMAX])
        krT = sb("krT", [P, S])
        qr_now = sb("qr_now", [P, S])
        router = sb("router", [P, KD, E])
        eps_t = sb("eps_t", [P, 1])
        sumsq = sb("sumsq", [P, 24])
        rms = sb("rms", [P, 24])
        neg_max = sb("neg_max", [P, 8])
        row_sum = sb("row_sum", [P, 8])
        row_inv = sb("row_inv", [P, 8])
        picked = sb("picked", [P, T, E], BF16)
        gate0 = sb("gate0", [P, T])
        gate1 = sb("gate1", [P, T])
        dest = sb("dest", [P, 2 * T], I32)
        table = sb("table", [1, 32], I32)
        posi = sb("posi", [P, T], I32)
        iota_e = sb("iota_e", [P, E])
        iota_j = sb("iota_j", [1, 16])

        hnT_hi, hnT_lo = (m[:, :].rearrange("p (k s) -> p k s", k=8) for m in (big_hi, big_lo))
        oT_hi, oT_lo, zT_hi, zT_lo = hnT_hi, hnT_lo, hnT_hi, hnT_lo
        cqT_hi, cqT_lo = (m[:, 0:4 * S].rearrange("p (k s) -> p k s", k=4) for m in (act_hi_mem, act_lo_mem))
        ckvT_hi, ckvT_lo = (m[:, 4 * S:6 * S].rearrange("p (k s) -> p k s", k=2) for m in (act_hi_mem, act_lo_mem))
        f_hi, f_lo = (m[:, 0:FG * S].rearrange("p (k s) -> p k s", k=FG) for m in (act_hi_mem, act_lo_mem))

        def view(at, n, k=None):
            v = scratch[:, at:at + n]
            return v if k is None else v.rearrange("p (k n) -> p k n", k=k)

        xn = view(0, T * D, T)
        cn = view(5120, 1792, 2)
        krope_tmp = view(6912, 128, 2)
        gain_c = view(7040, QR + KVR)
        freq = view(5120, ROPE // 2)
        posf = view(5152, T)
        angle, turns, folded, over = (view(5184 + P * n, P, T) for n in range(4))
        trig_arg = view(7808, 384).rearrange("p (a t n) -> p a t n", a=3, t=T)
        gain = view(8192, D)
        qn = view(0, 1024, 2)
        kn = view(1024, 1024, 2)
        v_nat = view(2048, 1024, T)
        qrT = view(3072, 2048, H // 2)
        rotated, rope_tmp = ([view(1024 + (t % 2) * 1024 + 512 * n, 512) for t in range(T)] for n in range(2))
        probs = view(5120, 2560, 2)
        probsT = view(7680, 1280)
        f_silu = view(4096, 1024, 2)
        f_act = view(5120, 1024, 2)
        xnT = view(5120, 1024, 8)
        pscale = view(6144, 1024)
        ptmp = view(7168, 512)
        route = view(7168, 1024)
        stage_more = view(0, 2048, 2)
        yn = scratch[0:CH, 2048:4096].rearrange("p (k n) -> p k n", k=2)
        xg = scratch[0:CH, 4096:6144].rearrange("p (k n) -> p k n", k=2)
        yT = view(6144, KD * C, KD)
        xT = view(6144 + KD * C, KD * C, KD)
        e_silu = krT[:, 0:2 * C].rearrange("p (k n) -> p k n", k=2)
        e_act = qr_now[:, 0:2 * C].rearrange("p (k n) -> p k n", k=2)
        e_up = e_silu[:, 1, :]
        y_in = view(0, 4096, 4)
        final = view(4096, 2048, 2)
        fjunk = view(6144, 1024)

        def stage(s):
            return stage_own[:, s, :] if s < STAGES_OWN else stage_more[:, s - STAGES_OWN, :]

        xbuf = nc.dram_tensor("xbuf", (XROWS, D), F32, kind="Internal").ap()
        ybuf = nc.dram_tensor("ybuf", (JMAX * C, D), F32, kind="Internal").ap()

        landed = [sem(f"landed{s}") for s in range(STAGES)]
        x_landed = [sem(f"x_landed{t}") for t in range(T)]
        gain_landed = sem("gain_landed")
        gainc_landed = sem("gainc_landed")
        freq_landed = sem("freq_landed")
        pos_landed = sem("pos_landed")
        router_landed = sem("router_landed")
        pscale_landed = sem("pscale_landed")
        xg_landed = sem("xg_landed")
        zero_stored = sem("zero_stored")
        scattered = sem("scattered")
        y_stored = sem("y_stored")
        y_gathered = [sem(f"y_gathered{t}") for t in range(2)]
        out_stored = [sem(f"out_stored{t}") for t in range(2)]
        eps_ready = sem("eps_ready")
        consts_ready = sem("consts_ready")
        counts_ready = sem("counts_ready")
        counts_inv = sem("counts_inv")
        pool_step = sem("pool_step")
        yn_free = sem("yn_free")

        weight_hi = sem("weight_hi")
        weight_lo = sem("weight_lo")
        std_ready = sem("std_ready")
        act_step = sem("act_step")
        xnT_hi = sem("xnT_hi")
        xnT_lo = sem("xnT_lo")
        xn_ready = sem("xn_ready")
        dve_step = sem("dve_step")
        trig_ready = sem("trig_ready")
        trig_done = sem("trig_done")
        iotas_ready = sem("iotas_ready")
        xnT_done = sem("xnT_done")
        c_done = sem("c_done")
        c_std = sem("c_std")
        c_ready = sem("c_ready")
        cT_done = sem("cT_done")
        cT_hi = sem("cT_hi")
        cT_lo = sem("cT_lo")
        down_freed = sem("down_freed")
        rope_done = sem("rope_done")
        rope_ready = sem("rope_ready")
        ropeT_done = sem("ropeT_done")
        qr_ready = sem("qr_ready")
        q_done = sem("q_done")
        k_done = sem("k_done")
        v_done = sem("v_done")
        q_ready = sem("q_ready")
        k_ready = sem("k_ready")
        v_ready = sem("v_ready")
        scores_done = sem("scores_done")
        max_ready = sem("max_ready")
        exp_ready = sem("exp_ready")
        inv_ready = sem("inv_ready")
        probs_ready = sem("probs_ready")
        pT_done = sem("pT_done")
        pT_act = sem("pT_act")
        pT_dve = sem("pT_dve")
        pv_done = sem("pv_done")
        o_hi = sem("o_hi")
        o_lo = sem("o_lo")
        wo_done = sem("wo_done")
        wo_freed = sem("wo_freed")
        h_attn = sem("h_attn")
        gu_done = sem("gu_done")
        silu_ready = sem("silu_ready")
        prod_ready = sem("prod_ready")
        act_hi = sem("act_hi")
        act_lo = sem("act_lo")
        ffn_done = sem("ffn_done")
        h_ffn = sem("h_ffn")
        z_done = sem("z_done")
        z_hi = sem("z_hi")
        z_lo = sem("z_lo")
        mix_done = sem("mix_done")
        h_mix = sem("h_mix")
        logits_done = sem("logits_done")
        chosen = sem("chosen")
        exp_gate = sem("exp_gate")
        rank_done = sem("rank_done")
        routed = sem("routed")
        xT_done = sem("xT_done")
        xT_ready = sem("xT_ready")
        expert_used = sem("expert_used")
        yT_ready = sem("yT_ready")
        y_nat_done = sem("y_nat_done")
        y_ready = sem("y_ready")
        h_final = sem("h_final")
        out_ready = sem("out_ready")

        block = ctx.enter_context(nc.Block())

        gains = {"attn0": a["attn_norm"][0:1], "ffn0": a["ffn_norm"][0:1], "attn1": a["attn_norm"][1:2],
                 "ffn1": a["ffn_norm"][1:2], "final": a["final_norm"].rearrange("(o d) -> o d", o=1)}
        rows_of = {"down": a["mla_w_down"][0], "wo": a["mla_w_o"][0]}
        w_uq = a["mla_w_uq"][0].rearrange("(k p) n -> p k n", p=P)
        w_ukv = a["mla_w_ukv"][0].rearrange("(k p) n -> p k n", p=P)
        f_gate, f_up = (a[n][0].rearrange("(k p) n -> p k n", p=P) for n in ("ffn_w_gate", "ffn_w_up"))
        pool_w = a["pool_w"][0].rearrange("g (k p) n -> p (g k) n", p=P)
        m_gate, m_up = (a[n][0].rearrange("e (k p) n -> e p k n", p=P) for n in ("moe_w_gate", "moe_w_up"))
        m_down = a["moe_w_down"][0]

        @block.sync
        def _(sp):
            def load(name, j, pieces, i=0, job=0):
                back = plan.back(name, j)
                if name in ("step", "tail"):
                    sp.wait_ge(expert_used, plan.unit(name, j, i, job) - (back - 1) + (AHEAD - plan.split))
                elif name == "pre":
                    sp.wait_ge(weight_lo, plan.split)
                elif back is not None:
                    sp.wait_ge(weight_lo, plan.unit(name, j, i, job) - (back - 1))
                s = plan.stage(name, j)
                for dst, src in pieces(stage(s)):
                    sp.dma_start(dst, src).then_inc(landed[s], 16)

            def cols(st, k, n):
                return st[:, 0:k * n].rearrange("p (k n) -> p k n", k=k)

            def x_in(t):
                sp.dma_start(h[:, t, :], a["x"][0, t * P:(t + 1) * P, :]).then_inc(x_landed[t], 16)

            def rows(name, k):
                load(name, k, lambda st: [(st[:, 0:rows_of[name].shape[1]], rows_of[name][k * P:(k + 1) * P, :])])

            x_in(0)
            for k in range(4):
                rows("down", k)
            x_in(1)
            for k in range(4, 6):
                rows("down", k)
            x_in(2)
            x_in(3)
            for k in range(6, 8):
                rows("down", k)

            for j in range(2):
                load("rope", j, lambda st: [(st[:, m * 512:m * 512 + 512].rearrange("p (h n) -> p h n", h=H),
                                             w_uq[:, 2 * j + m, :].rearrange("p (h n) -> p h n", h=H)[:, :, NOPE:])
                                            for m in range(2)])
            with sp.Fori(0, H // 2) as pair:
                load("pair", 0, lambda st: [(st.rearrange("p (k h n) -> p k h n", k=4, h=2)[:, :, hd, :],
                                             w_uq[:, :, bass.ds(pair * 384 + hd * 192, NOPE)]) for hd in range(2)], pair)
                load("pair", 1, lambda st: [(cols(st, 2, 512), w_ukv[:, :, bass.ds(pair * 512, 512)])], pair)
            for k in range(8):
                rows("wo", k)

            with sp.Fori(0, FI) as i:
                for j in range(FG):
                    for q, w in enumerate((f_gate, f_up)):
                        load("ffn", 2 * j + q, lambda st: [(cols(st, 8, P), w[:, :, bass.ds(i * (FG * P) + j * P, P)])], i)
                for j in range(FG):
                    load("ffn", 2 * FG + j,
                         lambda st: [(st, a["ffn_w_down"][0, bass.ds(i * (FG * P) + j * P, P), :])], i)
            for j in range(2):
                load("pool", j, lambda st: [(cols(st, 4, GD), pool_w[:, 4 * j:4 * j + 4, :])])

            def expert_cols(w, e, f, n=P):
                return w[bass.ds(e, 1), :, :, f * P:f * P + n].rearrange("o p k n -> p (o k) n")

            for j, (w, f) in enumerate(((m_gate, 0), (m_up, 0), (m_gate, 1), (m_up, 1))):
                load("pre", j, lambda st: [(cols(st, 8, P), w[0, :, :, f * P:(f + 1) * P])])

            sp.wait_ge(routed, 1)
            sp.wait_ge(scattered, 16 * 2 * T)
            jobs = sp.value_load(table[0:1, 0:1], min_val=E, max_val=JMAX)
            with sp.Fori(0, jobs) as job:
                e = sp.value_load(table[0:1, bass.ds(job + 1, 1)], min_val=0, max_val=E - 1)
                e_next = sp.value_load(table[0:1, bass.ds(job + 2, 1)], min_val=0, max_val=E - 1)

                def columns(w, ee, off):
                    return w[bass.ds(ee, 1), :, :, bass.ds(off, P)].rearrange("o p k n -> p (o k) n")

                def down_rows(off, n=P):
                    return m_down[bass.ds(e, 1), bass.ds(off, n), :].rearrange("o p n -> p (o n)")

                with sp.Fori(0, (FEF - 2) // 2) as i:
                    for s in range(2):
                        off = i * (2 * P) + s * P
                        load("step", 3 * s, lambda st: [(st, down_rows(off))], i, job)
                        load("step", 3 * s + 1, lambda st: [(cols(st, 8, P), columns(m_gate, e, off + 2 * P))], i, job)
                        load("step", 3 * s + 2, lambda st: [(cols(st, 8, P), columns(m_up, e, off + 2 * P))], i, job)
                load("tail", 0, lambda st: [(st, down_rows((FEF - 2) * P))], 0, job)
                load("tail", 1, lambda st: [(cols(st, 8, P)[:, :, q * FTAIL:(q + 1) * FTAIL],
                                             expert_cols(w, e, FEF, FTAIL)) for q, w in enumerate((m_gate, m_up))], 0, job)
                load("tail", 2, lambda st: [(st, down_rows((FEF - 1) * P))], 0, job)
                load("tail", 3, lambda st: [(st[0:FTAIL, :], down_rows(FEF * P, FTAIL))], 0, job)
                for j, (w, f) in enumerate(((m_gate, 0), (m_up, 0), (m_gate, 1), (m_up, 1))):
                    load("tail", 4 + j, lambda st: [(cols(st, 8, P), expert_cols(w, e_next, f))], 0, job)
            for done in out_stored:
                sp.wait_ge(done, 16 * T // 2)

        @block.gpsimd
        def _(pool):
            steps = [0]

            def link(ins):
                steps[0] += 1
                ins.then_inc(pool_step, 1)
                pool.wait_ge(pool_step, steps[0])

            g = nc.gpsimd
            g.memset(eps_t[:, :], EPS).then_inc(eps_ready, 1)
            g.memset(ident[:, :], 0.0)
            link(g.memset(ident_b[:, :], 0.0))
            for m in (ident, ident_b):
                last = g.affine_select(out=m[:, :], in_=m[:, :], compare_op=ALU.not_equal, fill=1.0, base=0,
                                       pattern=[[-1, P]], channel_multiplier=1)
            last.then_inc(consts_ready, 1)
            pool.dma_start(gain, gains["attn0"].partition_broadcast(P).rearrange("p o d -> p (o d)")).then_inc(gain_landed, 16)
            g.memset(causal[:, :], 0.0)
            g.memset(zeros[:, :], 0.0)
            g.memset(ones_b[:, :], 1.0)
            link(g.memset(before_b[:, :], 1.0))
            g.affine_select(out=causal[:, :], in_=causal[:, :], compare_op=ALU.is_ge, fill=NEG, base=0,
                            pattern=[[-1, P]], channel_multiplier=1)
            g.affine_select(out=before_b[:, :], in_=before_b[:, :], compare_op=ALU.is_ge, fill=0.0, base=-1,
                            pattern=[[1, P]], channel_multiplier=-1).then_inc(consts_ready, 1)
            pool.dma_start(gain_c[:, 0:QR], a["mla_q_norm"].partition_broadcast(P).rearrange("p o d -> p (o d)")
                           ).then_inc(gainc_landed, 16)
            pool.dma_start(gain_c[:, QR:], a["mla_kv_norm"].partition_broadcast(P).rearrange("p o d -> p (o d)")
                           ).then_inc(gainc_landed, 16)
            pool.dma_start(router[:, :, :], a["moe_router"][0].rearrange("(k p) e -> p k e", p=P),
                           allow_slow_non_contiguous=True).then_inc(router_landed, 16)
            g.iota(iota_e[:, :], [[1, E]], base=0, channel_multiplier=0, allow_small_or_imprecise_dtypes=True
                   ).then_inc(iotas_ready, 1)
            g.iota(iota_j[:, :], [[1, 16]], base=0, channel_multiplier=0, allow_small_or_imprecise_dtypes=True
                   ).then_inc(iotas_ready, 1)
            for n, w in enumerate(WINDOWS):
                g.memset(band[:, n, :], 1.0 / w)
                g.iota(band0[:, n, :], [[1, WMAX]], base=1, channel_multiplier=0, allow_small_or_imprecise_dtypes=True
                       ).then_inc(pool_step, 1)
                steps[0] += 1
            pool.wait_ge(pool_step, steps[0])
            for n, w in enumerate(WINDOWS):
                g.tensor_scalar(band0[:, n, :], band0[:, n, :], float(w), None, ALU.min).then_inc(counts_ready, 1)
            pool.wait_ge(counts_inv, 1)
            for n, w in enumerate(WINDOWS):
                for m, width in ((band, P + WMAX), (band0, WMAX)):
                    link(g.affine_select(out=m[:, n, :], in_=m[:, n, :], compare_op=ALU.is_ge, fill=0.0, base=0,
                                         pattern=[[1, width]], channel_multiplier=-1))
                    link(g.affine_select(out=m[:, n, :], in_=m[:, n, :], compare_op=ALU.is_ge, fill=0.0, base=w - 1,
                                         pattern=[[-1, width]], channel_multiplier=1))
                link(g.tensor_tensor(band[:, n, 0:P], band[:, n, 0:P], ident[:, :], ALU.subtract))
                link(g.tensor_tensor(band0[:, n, :], band0[:, n, :], ident[:, 0:WMAX], ALU.subtract))
            pool.sem_inc(consts_ready, 1)

            pool.wait_ge(down_freed, KD)
            half = (JMAX + 1) // 2 * C
            for rows in (xbuf[0:half, :], xbuf[half:, :], ybuf[E * C:, :]):
                pool.dma_start(rows.rearrange("(p r) (c n) -> p (r c) n", p=ZP, n=P),
                               zeros[0:ZP, :].unsqueeze(1).broadcast_to([ZP, rows.shape[0] // ZP * (D // P), P])
                               ).then_inc(zero_stored, 16)

            pool.wait_ge(pv_done, H)
            pool.wait_ge(pT_dve, H)
            pool.wait_ge(xn_ready, T)
            pool.dma_start(gain, gains["ffn0"].partition_broadcast(P).rearrange("p o d -> p (o d)")).then_inc(gain_landed, 16)
            pool.wait_ge(xn_ready, 2 * T)
            pool.dma_start(gain, gains["attn1"].partition_broadcast(P).rearrange("p o d -> p (o d)")).then_inc(gain_landed, 16)
            pool.dma_start(pscale, a["pool_scale"].partition_broadcast(P).rearrange("p o d -> p (o d)")
                           ).then_inc(pscale_landed, 16)
            pool.wait_ge(xn_ready, 3 * T)
            pool.dma_start(gain, gains["ffn1"].partition_broadcast(P).rearrange("p o d -> p (o d)")).then_inc(gain_landed, 16)

            pool.wait_ge(routed, 1)
            pool.wait_ge(zero_stored, 48)
            for c in range(2 * T):
                pool.indirect_dma_start(out=xbuf, out_offset=bass.IndirectOffsetOnAxis(ap=dest[:, c:c + 1], axis=0),
                                        in_=xn[:, c % T, :], in_offset=None).then_inc(scattered, 16)
            pool.wait_ge(scattered, 16 * 2 * T)
            pool.sem_inc(yn_free, 1)
            pool.dma_start(xg, xbuf[0:C, :].rearrange("(k p) n -> p k n", p=CH)).then_inc(xg_landed, 16)
            jobs = pool.value_load(table[0:1, 0:1], min_val=E, max_val=JMAX)
            with pool.Fori(0, jobs) as job:
                pool.wait_ge(xT_done, job + 1)
                pool.dma_start(xg, xbuf[bass.ds(job * C + C, C), :].rearrange("(k p) n -> p k n", p=CH)
                               ).then_inc(xg_landed, 16)
                pool.wait_ge(y_ready, job + 2)
                pool.dma_start(ybuf[bass.ds(job * C, C), :].rearrange("(k p) n -> p k n", p=CH), yn
                               ).then_inc(y_stored, 16)
                pool.wait_ge(y_stored, job * 16 + 16)
                pool.sem_inc(yn_free, 1)
            pool.dma_start(gain, gains["final"].partition_broadcast(P).rearrange("p o d -> p (o d)")).then_inc(gain_landed, 16)
            for t in range(T):
                if t >= 2:
                    pool.wait_ge(h_final, t - 1)
                for k in range(2):
                    pool.indirect_dma_start(out=y_in[:, 2 * (t % 2) + k, :], out_offset=None, in_=ybuf,
                                            in_offset=bass.IndirectOffsetOnAxis(ap=dest[:, k * T + t:k * T + t + 1], axis=0)
                                            ).then_inc(y_gathered[t % 2], 16)

        @block.scalar
        def _(act):
            s = nc.scalar
            steps = [0]

            def link(ins):
                steps[0] += 1
                ins.then_inc(act_step, 1)
                act.wait_ge(act_step, steps[0])

            def split(name, j, i=0, job=0, n=UNIT, parts=P):
                st, sl = plan.stage(name, j), plan.slot(name, j)
                act.wait_ge(landed[st], plan.landed(name, j, i, job))
                s.copy(w_hi[0:parts, sl, 0:n], stage(st)[0:parts, 0:n]).then_inc(weight_hi, 1)

            def norm_std(q, t):
                link(s.activation(xn[:, t, :], h[:, t, :], ACT.Square, scale=D ** -0.5, accum_out=sumsq[:, q:q + 1]))
                s.activation(rms[:, q:q + 1], sumsq[:, q:q + 1], ACT.Sqrt, bias=eps_t[:, 0:1]).then_inc(std_ready, 1)

            def norm_hi(q, t):
                act.wait_ge(xnT_done, q + 1)
                for b in range(2):
                    last = s.copy(hnT_hi[:, 4 * b:4 * b + 4, t * P:(t + 1) * P],
                                  bank[b][:, :].rearrange("p (k n) -> p k n", k=4))
                last.then_inc(xnT_hi, 1)

            act.dma_start(posi[:, :], a["positions"].rearrange("o (t p) -> p (o t)", p=P),
                          allow_slow_non_contiguous=True).then_inc(pos_landed, 16)
            act.dma_start(freq, a["rope_freq"].partition_broadcast(P).rearrange("p o d -> p (o d)")
                          ).then_inc(freq_landed, 16)
            act.wait_ge(eps_ready, 1)
            s.activation(rms[:, 23:24], eps_t[:, 0:1], ACT.Sqrt)
            for t in range(T):
                act.wait_ge(x_landed[t], 16)
                norm_std(t, t)

            def c_std_of(t):
                if t < T - 1:
                    act.wait_ge(c_done, t + 1)
                else:
                    act.wait_ge(down_freed, KD)
                b = 4 + 2 * (t % 2)
                s.activation(cn[:, t % 2, 0:QR], bank[b][:, :], ACT.Square, scale=QR ** -0.5, accum_out=sumsq[:, 16 + t:17 + t])
                link(s.activation(cn[:, t % 2, QR:QR + KVR], bank[b + 1][:, 0:KVR], ACT.Square, scale=KVR ** -0.5,
                                  accum_out=sumsq[:, 20 + t:21 + t]))
                s.activation(rms[:, 16 + t:17 + t], sumsq[:, 16 + t:17 + t], ACT.Sqrt, bias=eps_t[:, 0:1])
                s.activation(rms[:, 20 + t:21 + t], sumsq[:, 20 + t:21 + t], ACT.Sqrt, bias=eps_t[:, 0:1]).then_inc(c_std, 1)

            def c_hi(t):
                act.wait_ge(cT_done, t + 1)
                tok = slice(t * P, (t + 1) * P)
                s.copy(cqT_hi[:, :, tok], bank[2][:, :].rearrange("p (k n) -> p k n", k=4))
                s.copy(ckvT_hi[:, :, tok], bank[3][:, 0:2 * P].rearrange("p (k n) -> p k n", k=2)).then_inc(cT_hi, 1)

            norm_hi(0, 0)
            for k in range(4):
                split("down", k, n=DOWN)
            norm_hi(1, 1)
            for k in range(4, 8):
                split("down", k, n=DOWN)
            act.wait_ge(trig_ready, 1)
            s.activation(sin_t[:, :, 32:64], trig_arg[:, 0], ACT.Sin)
            s.activation(cos_t[:, :, 0:32], trig_arg[:, 1], ACT.Sin)
            s.activation(cos_t[:, :, 32:64], trig_arg[:, 1], ACT.Sin)
            s.activation(sin_t[:, :, 0:32], trig_arg[:, 2], ACT.Sin).then_inc(trig_done, 1)
            norm_hi(2, 2)
            c_std_of(0)
            norm_hi(3, 3)
            c_hi(0)
            c_std_of(1)
            c_hi(1)
            c_std_of(2)
            for j in range(4):
                act.wait_ge(down_freed, j + 1)
                split(("rope", "pair")[j // 2], j % 2)

            def qr_out(t):
                act.wait_ge(ropeT_done, t + 1)
                s.mul(qrT[:, :, t * P:(t + 1) * P], bank[t % 2][:, :].rearrange("p (k n) -> p k n", k=4), SCALE
                      ).then_inc(qr_ready, 1)

            def q_out(pair, hd):
                act.wait_ge(q_done, 2 * pair + (hd + 1))
                s.mul(qn[:, hd, :], bank[4][:, :], SCALE).then_inc(q_ready, 1)

            c_hi(2)
            c_std_of(3)
            qr_out(0)
            c_hi(3)
            qr_out(1)
            q_out(0, 0)
            qr_out(2)
            qr_out(3)
            act.wait_ge(qr_ready, T)
            s.copy(qr_now[:, :], qrT[:, 0, :])
            q_out(0, 1)
            act.wait_ge(k_done, 2)
            for j in range(2):
                split("pair", j, 1)

            def attention(pair, more, between):
                def exps(hd):
                    for qb in range(T):
                        n = (qb + 1) * P
                        at = qb * (qb + 1) // 2 * P
                        col = 4 * hd + qb
                        act.wait_ge(max_ready, pair * 8 + col + 1)
                        s.activation(probs[:, hd, at:at + n], bank[qb][:, 0:n], ACT.Exp, bias=neg_max[:, col:col + 1],
                                     accum_out=row_sum[:, col:col + 1]).then_inc(exp_ready, 1)

                def turned(hd):
                    act.wait_ge(pT_done, pair * 2 + hd + 1)
                    s.copy(probsT[:, 0:512], bank[0][:, :])
                    s.copy(probsT[:, 896:1280], bank[2][:, 0:384]).then_inc(pT_act, 1)

                def head_out(hd):
                    act.wait_ge(pv_done, pair * 2 + hd + 1)
                    s.copy(oT_hi[:, bass.ds(pair * 2 + hd, 1), :], bank[3][:, :].unsqueeze(1)).then_inc(o_hi, 1)

                exps(0)
                between(0)
                if more:
                    q_out(pair + 1, 0)
                turned(0)
                head_out(0)
                exps(1)
                if more:
                    s.copy(qr_now[:, :].unsqueeze(1), qrT[:, bass.ds(pair + 1, 1), :])
                between(1)
                if more:
                    q_out(pair + 1, 1)
                turned(1)
                between(2)
                head_out(1)
                between(3)

            def next_pair(pair):
                def between(place):
                    if place >= 2:
                        act.wait_ge(k_done, pair * 2 + 4)
                        split("pair", place - 2, pair + 2)
                return between

            with act.Fori(0, H // 2 - 2) as pair:
                attention(pair, True, next_pair(pair))
            attention(H // 2 - 2, True, lambda place: [split("wo", k) for k in ((0,), (1, 2), (3,), (4, 5))[place]])
            act.wait_ge(k_done, H)
            attention(H // 2 - 1, False, lambda place: [split("wo", k) for k in ((6,), (7,), (), ())[place]])

            for t in range(T):
                act.wait_ge(h_attn, t + 1)
                norm_std(T + t, t)
                if t:
                    norm_hi(T + t - 1, t - 1)
            for j in range(4):
                act.wait_ge(wo_freed, 5 + j)
                split("ffn", j)
            norm_hi(2 * T - 1, T - 1)

            def ffn_act(i, j):
                act.wait_ge(gu_done, i * FG + j + 1)
                s.activation(f_silu[:, j % 2, :], bank[2 * (j % 2)][:, :], ACT.Silu).then_inc(silu_ready, 1)
                act.wait_ge(prod_ready, i * FG + j + 1)
                s.copy(f_hi[:, j, :], f_act[:, j % 2, :]).then_inc(act_hi, 1)

            def ffn(i, following):
                ffn_act(i, 0)
                for j in range(4, 9):
                    split("ffn", j, i)
                ffn_act(i, 1)
                ffn_act(i, 2)
                following()

            with act.Fori(0, FI - 1) as i:
                ffn(i, lambda: [split("ffn", j, i + 1) for j in range(4)])
            ffn(FI - 1, lambda: [split("pool", j) for j in range(2)])

            for t in range(T):
                act.wait_ge(h_ffn, 8 * (FI - 1) + 4 + t + 1)
                norm_std(2 * T + t, t)
            for d in range(KD):
                act.wait_ge(z_done, d + 1)
                s.copy(zT_hi[:, d, :], bank[d % 4][:, :]).then_inc(z_hi, 1)

            def rows_T(t):
                act.wait_ge(xnT_done, 2 * T + t + 1)
                s.copy(xnT[:, 0:4, :], bank[0][:, :].rearrange("p (k n) -> p k n", k=4)).then_inc(xnT_hi, 1)

            for t in range(T):
                act.wait_ge(h_mix, t + 1)
                norm_std(3 * T + t, t)
                if t:
                    rows_T(t - 1)
            rows_T(T - 1)
            act.wait_ge(chosen, 1)
            s.activation(gate1[:, :], gate1[:, :], ACT.Exp).then_inc(exp_gate, 1)

            act.wait_ge(routed, 1)
            act.sem_inc(y_ready, 1)
            jobs = act.value_load(table[0:1, 0:1], min_val=E, max_val=JMAX)
            with act.Fori(0, jobs) as job:
                used = job * JUNITS + AHEAD

                def silu(par, count):
                    act.wait_ge(expert_used, used + count)
                    s.activation(e_silu[:, par, :], bank[2 * par][:, 0:C], ACT.Silu).then_inc(silu_ready, 1)

                silu(0, 2)
                with act.Fori(0, (FEF - 2) // 2) as i:
                    silu(1, i * 6 + 4)
                    silu(0, i * 6 + 7)
                silu(1, JUNITS - 4)
                act.wait_ge(expert_used, used + (JUNITS - 2))
                act.wait_ge(prod_ready, job * MACTS + (FT + MACTS - 1))
                s.activation(e_silu[0:FTAIL, 0, :], bank[0][0:FTAIL, 0:C], ACT.Silu)
                s.copy(e_up[0:FTAIL, :], bank[0][FTAIL:P, 0:C]).then_inc(silu_ready, 1)
                act.wait_ge(expert_used, used + JUNITS)
                for b, k0, k1 in ((4, 0, 3), (5, 3, 6), (6, 6, 8)):
                    last = s.copy(yT[:, k0:k1, :], bank[b][:, 0:(k1 - k0) * C].rearrange("p (k n) -> p k n", n=C))
                last.then_inc(yT_ready, 1)
                act.wait_ge(y_nat_done, job + 1)
                act.wait_ge(yn_free, job + 1)
                for b in range(4):
                    last = s.copy(yn[:, b // 2, (b % 2) * 512:(b % 2) * 512 + 512], bank[4 + b][0:CH, :])
                last.then_inc(y_ready, 1)

            for t in range(T):
                act.wait_ge(h_final, t + 1)
                link(s.activation(fjunk, h[:, t, :], ACT.Square, scale=D ** -0.5, accum_out=sumsq[:, t:t + 1]))
                s.activation(rms[:, t:t + 1], sumsq[:, t:t + 1], ACT.Sqrt, bias=eps_t[:, 0:1]).then_inc(std_ready, 1)
                act.wait_ge(out_ready, t + 1)
                act.dma_start(out[0, t * P:(t + 1) * P, :], final[:, t % 2, :]).then_inc(out_stored[t % 2], 16)
            for done in out_stored:
                act.wait_ge(done, 16 * T // 2)

        @block.tensor
        def _(pe):
            t_ = nc.tensor

            def mm3(dst, st_hi, st_lo, mv_hi, mv_lo, start, stop, check=False):
                t_.matmul(dst, st_lo, mv_hi, start=start, stop=False, skip_group_check=check)
                t_.matmul(dst, st_hi, mv_lo, start=False, stop=False, skip_group_check=check)
                return t_.matmul(dst, st_hi, mv_hi, start=False, stop=stop, skip_group_check=check)

            def weights(name, j, i=0, job=0):
                pe.wait_ge(weight_lo, plan.unit(name, j, i, job) + 1)
                return plan.slot(name, j)

            def transposes(src, banks):
                for k in range(8):
                    last = t_.transpose(bank[banks[k // 4]][:, k % 4 * P:k % 4 * P + P], src[:, k * P:(k + 1) * P], ident[:, :])
                return last

            def norm_T(q, t):
                pe.wait_ge(xn_ready, q + 1)
                if q:
                    pe.wait_ge(xnT_hi, q)
                    pe.wait_ge(xnT_lo, q)
                transposes(xn[:, t, :], (0, 1)).then_inc(xnT_done, 1)

            def tok(t):
                return slice(t * P, (t + 1) * P)

            def down(t):
                pe.wait_ge(xnT_lo, t + 1)
                if t >= 2:
                    pe.wait_ge(c_ready, t - 1)
                b = 4 + 2 * (t % 2)

                def part(k, half):
                    lo, hi = ((0, QR), (QR, DOWN))[half]
                    sl = weights("down", k)
                    return mm3(bank[b + half][:, 0:hi - lo], hnT_hi[:, k, tok(t)], hnT_lo[:, k, tok(t)],
                               w_hi[:, sl, lo:hi], w_lo[:, sl, lo:hi], k == 0, k == KD - 1)

                for k in range(KD):
                    for half in range(2):
                        last = part(k, half)
                    if t == T - 1:
                        last.then_inc(down_freed, 1)
                if t < T - 1:
                    last.then_inc(c_done, 1)

            def latents_T(t):
                pe.wait_ge(c_ready, t + 1)
                if t:
                    pe.wait_ge(cT_lo, t)
                for k in range(7):
                    last = t_.transpose(bank[2 + k // 4][:, k % 4 * P:k % 4 * P + P], cn[:, t % 2, k * P:(k + 1) * P],
                                        ident[:, :])
                last.then_inc(cT_done, 1)

            pe.wait_ge(consts_ready, 2)
            norm_T(0, 0)
            norm_T(1, 1)
            down(0)
            norm_T(2, 2)
            down(1)
            norm_T(3, 3)
            latents_T(0)
            down(2)
            latents_T(1)
            down(3)
            latents_T(2)

            def rope_q(t):
                if t < 2:
                    pe.wait_ge(cT_lo, t + 1)
                else:
                    pe.wait_ge(qr_ready, t - 1)
                for k in range(4):
                    sl = weights("rope", k // 2)
                    at = slice(k % 2 * 512, k % 2 * 512 + 512)
                    last = mm3(bank[t % 2][:, :], cqT_hi[:, k, tok(t)], cqT_lo[:, k, tok(t)], w_hi[:, sl, at], w_lo[:, sl, at],
                               k == 0, k == 3)
                last.then_inc(rope_done, 1)

            def rope_T(t):
                pe.wait_ge(rope_ready, t + 1)
                for k in range(4):
                    last = t_.transpose(bank[t % 2][:, tok(k)], rotated[t][:, tok(k)], ident[:, :])
                last.then_inc(ropeT_done, 1)

            def wq(part, k, hd):
                m = (w_hi, w_lo)[part][:, plan.slot("pair", 0), :].rearrange("p (k h n) -> p k h n", k=4, h=2)
                return m[:, k, hd, :]

            def wkv(part, k):
                m = (w_hi, w_lo)[part][:, plan.slot("pair", 1), :].rearrange("p (k h n) -> p k h n", k=2, h=2)
                return m[:, k]

            def q_head(pair, hd, first=False):
                if not first:
                    pe.wait_ge(q_ready, 2 * pair + hd)
                weights("pair", 0, pair)
                for k in range(4):
                    last = mm3(bank[4][:, :], wq(0, k, hd), wq(1, k, hd), cqT_hi[:, k, :], cqT_lo[:, k, :], k == 0, k == 3)
                last.then_inc(q_done, 1)

            def k_head(pair, hd, first=False):
                if not first:
                    pe.wait_ge(k_ready, 2 * pair + hd)
                weights("pair", 1, pair)
                for k in range(2):
                    last = mm3(bank[5][:, :], wkv(0, k)[:, hd, 0:NOPE], wkv(1, k)[:, hd, 0:NOPE],
                               ckvT_hi[:, k, :], ckvT_lo[:, k, :], k == 0, k == 1)
                last.then_inc(k_done, 1)

            def values(pair, first=False):
                if not first:
                    pe.wait_ge(v_ready, 2 * pair)
                weights("pair", 1, pair)
                for t in range(T):
                    for k in range(2):
                        last = mm3(bank[6 + t // 2][:, t % 2 * 256:t % 2 * 256 + 256].rearrange("p (h n) -> p h n", h=2),
                                   ckvT_hi[:, k, tok(t)], ckvT_lo[:, k, tok(t)], wkv(0, k)[:, :, NOPE:], wkv(1, k)[:, :, NOPE:],
                                   k == 0, k == 1)
                last.then_inc(v_done, 1)

            rope_q(0)
            rope_q(1)
            rope_T(0)
            latents_T(3)
            pe.wait_ge(cT_lo, 3)
            rope_q(2)
            rope_T(1)
            pe.wait_ge(cT_lo, T)
            q_head(0, 0, True)
            rope_q(3)
            rope_T(2)
            k_head(0, 0, True)
            values(0, True)
            rope_T(3)
            q_head(0, 1)
            k_head(0, 1)

            def attention(pair, filler):
                def scores(hd):
                    if hd == 0:
                        pe.wait_ge(q_ready, pair * 2 + 2)
                        pe.wait_ge(k_ready, pair * 2 + 2)
                    r = slice(ROPE * hd, ROPE * hd + ROPE)
                    for qb in range(T):
                        if qb == T - 1:
                            pe.wait_ge(o_lo, pair * 2 + hd + 1)
                        dst, n = bank[qb], (qb + 1) * P
                        t_.matmul(dst[:, 0:n], qn[:, hd, tok(qb)], kn[:, hd, 0:n], start=True, stop=False)
                        t_.matmul(dst[:, 0:n], qr_now[r, tok(qb)], krT[r, 0:n], start=False, stop=False)
                        t_.matmul(dst[:, tok(qb)], ident_b[:, :], causal[:, :], start=False, stop=True
                                  ).then_inc(scores_done, 1)

                def turn(hd):
                    for qb in range(T):
                        pe.wait_ge(probs_ready, pair * 8 + 4 * hd + qb + 1)
                        at = qb * (qb + 1) // 2 * P
                        for kb in range(qb + 1):
                            col = (qb - kb) * P + (256 if kb == 3 else 0)
                            last = t_.transpose(bank[min(kb, 2)][:, col:col + P],
                                                probs[:, hd, at + kb * P:at + kb * P + P], ident[:, :])
                    last.then_inc(pT_done, 1)

                def head_out(hd):
                    pe.wait_ge(pT_act, pair * 2 + hd + 1)
                    pe.wait_ge(pT_dve, pair * 2 + hd + 1)
                    pe.wait_ge(v_ready, pair * 2 + hd + 1)
                    for kb, at in enumerate((0, 512, 896, 1152)):
                        last = t_.matmul(bank[3][:, kb * P:S], v_nat[:, kb, hd * VD:(hd + 1) * VD],
                                         probsT[:, at:at + S - kb * P], start=kb == 0, stop=kb == T - 1)
                    last.then_inc(pv_done, 1)

                for hd in range(2):
                    scores(hd)
                    filler(2 * hd)
                    turn(hd)
                    filler(2 * hd + 1)
                    head_out(hd)

            def next_pair(pair):
                def filler(place):
                    if place == 0:
                        q_head(pair + 1, 0)
                    elif place == 1:
                        k_head(pair + 1, 0)
                    elif place == 2:
                        values(pair + 1)
                        q_head(pair + 1, 1)
                    else:
                        k_head(pair + 1, 1)
                return filler

            with pe.Fori(0, H // 2 - 1) as pair:
                attention(pair, next_pair(pair))

            def wo_part(t, k):
                sl = weights("wo", k)
                for half in range(2):
                    at = slice(512 * half, 512 * half + 512)
                    last = mm3(bank[4 + 2 * (t % 2) + half][:, :], oT_hi[:, k, tok(t)], oT_lo[:, k, tok(t)],
                               w_hi[:, sl, at], w_lo[:, sl, at], k == 0, k == H - 1)
                if t == T - 1:
                    last.then_inc(wo_freed, 1)
                elif k == H - 1:
                    last.then_inc(wo_done, 1)

            def first_heads(place):
                if place == 2:
                    pe.wait_ge(v_ready, H)
                for t, k in (((0, 0), (0, 1), (0, 2)), ((0, 3), (0, 4)), ((0, 5), (1, 0), (1, 1)), ((1, 2), (1, 3)))[place]:
                    wo_part(t, k)

            attention(H // 2 - 1, first_heads)
            for k in (4, 5):
                wo_part(1, k)
            for k in (H - 2, H - 1):
                pe.wait_ge(o_lo, 1 + k + 1)
                for t in range(2):
                    wo_part(t, k)
            pe.wait_ge(h_attn, 1)
            for k in range(H):
                wo_part(2, k)
            norm_T(T, 0)
            pe.wait_ge(h_attn, 2)
            for k in range(H):
                if k == 4:
                    norm_T(T + 1, 1)
                wo_part(3, k)
            norm_T(T + 2, 2)
            norm_T(T + 3, 3)

            pe.wait_ge(xnT_lo, 2 * T)
            with pe.Fori(0, FI) as i:
                for j in range(FG):
                    if j == 2:
                        pe.wait_ge(prod_ready, i * FG + 1)
                    for q in range(2):
                        sl = weights("ffn", 2 * j + q, i)
                        for k in range(KD):
                            last = mm3(bank[2 * (j % 2) + q][:, :], w_hi[:, sl, k * P:(k + 1) * P], w_lo[:, sl, k * P:(k + 1) * P],
                                       hnT_hi[:, k, :], hnT_lo[:, k, :], k == 0, k == KD - 1)
                    last.then_inc(gu_done, 1)
                sl = [weights("ffn", 2 * FG + j, i) for j in range(FG)]
                pe.wait_ge(act_lo, i * FG + 2)
                for half in range(2):
                    at = slice(512 * half, 512 * half + 512)
                    for j in range(FG):
                        if j == 2 and half == 0:
                            pe.wait_ge(act_lo, i * FG + 3)
                        for t in range(T):
                            if j == 0 and half:
                                pe.wait_ge(h_ffn, i * 8 + t + 1)
                            last = mm3(bank[4 + t][:, :], f_hi[:, j, tok(t)], f_lo[:, j, tok(t)],
                                       w_hi[:, sl[j], at], w_lo[:, sl[j], at], j == 0, j == FG - 1)
                            if j == FG - 1:
                                last.then_inc(ffn_done, 1)

            pe.wait_ge(consts_ready, 3)
            pe.wait_ge(xn_ready, 3 * T)
            for d in range(KD):
                if d >= 4:
                    pe.wait_ge(z_lo, d - 3)
                g = d // 2
                dst = bank[d % 4]
                chunk = [xn[:, t, d * P:(d + 1) * P] for t in range(T)]
                t_.matmul(dst[:, 0:WMAX], chunk[0], band0[:, g, :], start=True, stop=False, skip_group_check=True)
                t_.matmul(dst[:, WMAX:P + WMAX], chunk[0], band[:, g, WMAX:], start=False, stop=False, skip_group_check=True)
                for t in range(1, T):
                    n = P + WMAX if t < T - 1 else P
                    last = t_.matmul(dst[:, t * P:t * P + n], chunk[t], band[:, g, 0:n], start=False, stop=t == T - 1,
                                     skip_group_check=True)
                last.then_inc(z_done, 1)

            def mix(t):
                if t >= 2:
                    pe.wait_ge(h_mix, t - 1)
                for g in range(4):
                    sl = weights("pool", g // 2)
                    for k in range(2):
                        at = ((g % 2) * 2 + k) * GD
                        last = mm3(bank[4 + 2 * (t % 2) + g // 2][:, g % 2 * GD:g % 2 * GD + GD],
                                   zT_hi[:, 2 * g + k, tok(t)], zT_lo[:, 2 * g + k, tok(t)],
                                   w_hi[:, sl, at:at + GD], w_lo[:, sl, at:at + GD], k == 0, k == 1)
                last.then_inc(mix_done, 1)

            def logits(t):
                norm_T_at = 2 * T + t
                pe.wait_ge(xn_ready, 3 * T + t + 1)
                pe.wait_ge(xnT_hi, norm_T_at)
                pe.wait_ge(xnT_lo, norm_T_at)
                transposes(xn[:, t, :], (0, 1)).then_inc(xnT_done, 1)
                pe.wait_ge(xnT_hi, norm_T_at + 1)
                pe.wait_ge(xnT_lo, norm_T_at + 1)
                for k in range(KD):
                    last = t_.matmul(bank[2][:, t * E:(t + 1) * E], xnT[:, k, :], router[:, k, :], start=k == 0, stop=k == KD - 1)
                if t == T - 1:
                    last.then_inc(logits_done, 1)

            pe.wait_ge(router_landed, 16)
            pe.wait_ge(z_lo, KD)
            mix(0)
            for t in range(1, T):
                mix(t)
                logits(t - 1)
            logits(T - 1)

            pe.wait_ge(chosen, 1)
            for t in range(T):
                for c in range(t + 1):
                    last = t_.matmul(bank[3][:, t * E:(t + 1) * E], (before_b if c == t else ones_b)[:, :], picked[:, c, :],
                                     start=c == 0, stop=c == t)
            for c in range(T):
                last = t_.matmul(bank[3][:, T * E:(T + 1) * E], ones_b[:, :], picked[:, c, :], start=c == 0, stop=c == T - 1)
            last.then_inc(rank_done, 1)

            def x_T(at):
                pe.wait_ge(xg_landed, at * 16)
                for k in range(KD):
                    b, k0 = ((1, 0), (7, 3), (3, 6))[k // 3]
                    for q in range(2):
                        col = (k - k0) * C + q * CH
                        last = t_.transpose(bank[b][:, col:col + CH], xg[:, q, k * P:(k + 1) * P], ident[0:CH, 0:CH])
                last.then_inc(xT_done, 1)

            def landed_unit(name, j, i=0, job=0):
                st = plan.stage(name, j)
                pe.wait_ge(landed[st], plan.landed(name, j, i, job))
                return stage(st)

            def columns(dst, w):
                for k in range(KD):
                    last = t_.matmul(dst[:, 0:C], w[:, k * P:(k + 1) * P], xT[:, k, :], start=k == 0, stop=k == KD - 1)
                return last.then_inc(expert_used, 1)

            def gate_up(name, j, par, i=0, job=0):
                for q in range(2):
                    columns(bank[2 * par + q], landed_unit(name, j + q, i, job))

            def down_tile(name, j, par, prod, i=0, job=0, first=False, final=False):
                pe.wait_ge(prod_ready, prod)
                w = landed_unit(name, j, i, job)
                n = FTAIL if final else P
                for k in range(KD):
                    col = k % 3 * C
                    last = t_.matmul(bank[4 + k // 3][:, col:col + C], w[0:n, k * P:(k + 1) * P], e_act[0:n, par, :],
                                     start=first and k % 3 == 0, stop=final, skip_group_check=True)
                last.then_inc(expert_used, 1)

            pe.wait_ge(routed, 1)
            pe.sem_inc(expert_used, AHEAD)
            x_T(1)
            pe.wait_ge(xT_ready, 1)
            gate_up("pre", 0, 0)
            for q in range(2):
                landed_unit("pre", 2 + q)
            jobs = pe.value_load(table[0:1, 0:1], min_val=E, max_val=JMAX)
            with pe.Fori(0, jobs) as job:
                acts = job * MACTS + FT
                turns = (FEF - 2) // 2 - 1
                for q in range(2):
                    columns(bank[2 + q], stage(plan.stage("pre", 2 + q)))
                pe.wait_ge(y_ready, job + 1)
                down_tile("step", 0, 0, acts + 1, 0, job, first=True)
                gate_up("step", 1, 0, 0, job)
                with pe.Fori(0, turns) as i:
                    down_tile("step", 3, 1, acts + i * 2 + 2, i, job)
                    gate_up("step", 4, 1, i, job)
                    down_tile("step", 0, 0, acts + i * 2 + 3, i + 1, job)
                    gate_up("step", 1, 0, i + 1, job)
                down_tile("step", 3, 1, acts + (2 * turns + 2), turns, job)
                gate_up("step", 4, 1, turns, job)
                down_tile("tail", 0, 0, acts + FEF - 1, 0, job)
                columns(bank[0], landed_unit("tail", 1, 0, job))
                pe.wait_ge(prod_ready, acts + FEF)
                x_T(job + 2)
                down_tile("tail", 2, 1, acts + FEF, 0, job)
                down_tile("tail", 3, 0, acts + MACTS, 0, job, final=True)
                pe.wait_ge(xT_ready, job + 2)
                gate_up("tail", 4, 0, 0, job)
                for q in range(2):
                    landed_unit("tail", 6 + q, 0, job)
                pe.wait_ge(yT_ready, job + 1)
                for q in range(2):
                    for k in range(KD):
                        last = t_.transpose(bank[4 + 2 * q + k // 4][0:CH, k % 4 * P:k % 4 * P + P], yT[:, k, q * CH:(q + 1) * CH],
                                            ident[:, :])
                last.then_inc(y_nat_done, 1)

        @block.vector
        def _(dve):
            v = nc.vector
            steps = [0]

            def link(ins):
                steps[0] += 1
                ins.then_inc(dve_step, 1)
                dve.wait_ge(dve_step, steps[0])

            def split(name, j, i=0, job=0, n=UNIT, parts=P):
                st, sl = plan.stage(name, j), plan.slot(name, j)
                dve.wait_ge(weight_hi, plan.unit(name, j, i, job) + 1)
                v.tensor_tensor(w_lo[0:parts, sl, 0:n], stage(st)[0:parts, 0:n], w_hi[0:parts, sl, 0:n],
                                ALU.subtract).then_inc(weight_lo, 1)

            dve.wait_ge(pos_landed, 16)
            dve.wait_ge(freq_landed, 16)
            link(v.tensor_copy(posf, posi[:, :]))
            link(v.tensor_tensor(angle, posf.unsqueeze(2).broadcast_to([P, T, 32]),
                                 freq.unsqueeze(1).broadcast_to([P, T, 32]), ALU.mult))
            link(v.tensor_scalar(turns, angle, 1 / (2 * np.pi), ROUND, ALU.mult, ALU.add))
            link(v.tensor_scalar(turns, turns, ROUND, None, ALU.subtract))
            for part in TWO_PI:
                link(v.scalar_tensor_tensor(angle, turns, -part, angle, ALU.mult, ALU.add))
            link(v.tensor_scalar(over, angle, np.pi / 2, 2 * np.pi, ALU.is_gt, ALU.mult))
            link(v.scalar_tensor_tensor(folded, angle, np.pi / 2, over, ALU.add, ALU.subtract))
            v.tensor_scalar(trig_arg[:, 0], angle, PI_IN, -PI_IN, ALU.min, ALU.max)
            v.tensor_scalar(trig_arg[:, 1], folded, PI_IN, -PI_IN, ALU.min, ALU.max)
            link(v.tensor_scalar(over, angle, -1.0, None, ALU.mult))
            v.tensor_scalar(trig_arg[:, 2], over, PI_IN, -PI_IN, ALU.min, ALU.max).then_inc(trig_ready, 1)
            dve.wait_ge(counts_ready, len(WINDOWS))
            v.reciprocal(band0[:, :, :], band0[:, :, :]).then_inc(counts_inv, 1)

            def norm_rows(q, t):
                dve.wait_ge(std_ready, q + 1)
                col = q if q < 4 * T else q - 4 * T
                link(v.reciprocal(rms[:, col:col + 1], rms[:, col:col + 1]))
                dve.wait_ge(gain_landed, 16 * (q // T + 1))
                v.scalar_tensor_tensor(xn[:, t, :], h[:, t, :], rms[:, col:col + 1], gain, ALU.mult, ALU.mult
                                       ).then_inc(xn_ready, 1)

            def norm_lo(q, t):
                dve.wait_ge(xnT_hi, q + 1)
                for b in range(2):
                    at = (slice(None), slice(4 * b, 4 * b + 4), slice(t * P, (t + 1) * P))
                    last = v.tensor_tensor(hnT_lo[at], bank[b][:, :].rearrange("p (k n) -> p k n", k=4), hnT_hi[at],
                                           ALU.subtract)
                last.then_inc(xnT_lo, 1)

            def rotate(out_, tmp, q, heads, t):
                n = len(range(*t.indices(T)))
                shape = [P, n, heads, ROPE]
                half = [P, n, heads, ROPE // 2]
                v.tensor_tensor(out_, q, cos_t[:, t, :].unsqueeze(2).broadcast_to(shape), ALU.mult)
                v.tensor_tensor(tmp[..., 0:32], q[..., 32:64], sin_t[:, t, 0:32].unsqueeze(2).broadcast_to(half), ALU.mult)
                link(v.tensor_tensor(tmp[..., 32:64], q[..., 0:32], sin_t[:, t, 32:64].unsqueeze(2).broadcast_to(half),
                                     ALU.mult))
                return v.tensor_tensor(out_, out_, tmp, ALU.add)

            def latents(t):
                dve.wait_ge(c_std, t + 1)
                v.reciprocal(rms[:, 16 + t:17 + t], rms[:, 16 + t:17 + t])
                link(v.reciprocal(rms[:, 20 + t:21 + t], rms[:, 20 + t:21 + t]))
                b = 4 + 2 * (t % 2)
                c = cn[:, t % 2, :]
                v.scalar_tensor_tensor(c[:, 0:QR], bank[b][:, :], rms[:, 16 + t:17 + t], gain_c[:, 0:QR], ALU.mult, ALU.mult)
                v.scalar_tensor_tensor(c[:, QR:QR + KVR], bank[b + 1][:, 0:KVR], rms[:, 20 + t:21 + t], gain_c[:, QR:],
                                       ALU.mult, ALU.mult)
                kr = c[:, QR + KVR:DOWN]
                link(rotate(kr.unsqueeze(1).unsqueeze(1), krope_tmp[:, 0, :].unsqueeze(1).unsqueeze(1),
                            bank[b + 1][:, KVR:KVR + ROPE].unsqueeze(1).unsqueeze(1), 1, slice(t, t + 1)))
                v.tensor_copy(c[:, DOWN:DOWN + ROPE], kr).then_inc(c_ready, 1)

            def latents_lo(t):
                dve.wait_ge(cT_hi, t + 1)
                tok = slice(t * P, (t + 1) * P)
                v.tensor_tensor(cqT_lo[:, :, tok], bank[2][:, :].rearrange("p (k n) -> p k n", k=4), cqT_hi[:, :, tok],
                                ALU.subtract)
                v.tensor_copy(krT[:, tok], bank[3][:, 2 * P:3 * P])
                v.tensor_tensor(ckvT_lo[:, :, tok], bank[3][:, 0:2 * P].rearrange("p (k n) -> p k n", k=2),
                                ckvT_hi[:, :, tok], ALU.subtract).then_inc(cT_lo, 1)

            norm_rows(0, 0)
            norm_rows(1, 1)
            norm_lo(0, 0)
            for k in range(4):
                split("down", k, n=DOWN)
            norm_lo(1, 1)
            for k in range(4, 8):
                split("down", k, n=DOWN)
            norm_rows(2, 2)
            norm_rows(3, 3)
            dve.wait_ge(trig_done, 1)
            dve.wait_ge(gainc_landed, 32)
            norm_lo(2, 2)
            latents(0)
            norm_lo(3, 3)
            latents_lo(0)
            latents(1)
            latents_lo(1)
            latents(2)
            for j in range(4):
                split(("rope", "pair")[j // 2], j % 2)

            def rotate_q(t):
                dve.wait_ge(rope_done, t + 1)
                shape = "p (t h n) -> p t h n"
                q, out_, tmp = (m.rearrange(shape, t=1, h=H) for m in (bank[t % 2][:, :], rotated[t], rope_tmp[t]))
                rotate(out_, tmp, q, H, slice(t, t + 1)).then_inc(rope_ready, 1)

            def k_out(pair, hd):
                dve.wait_ge(k_done, 2 * pair + (hd + 1))
                v.tensor_copy(kn[:, hd, :], bank[5][:, :]).then_inc(k_ready, 1)

            def v_out(hd):
                for b in range(2):
                    last = v.tensor_copy(v_nat[:, 2 * b:2 * b + 2, hd * VD:(hd + 1) * VD],
                                         bank[6 + b][:, :].rearrange("p (t h n) -> p t h n", t=2, h=2)[:, :, hd, :])
                last.then_inc(v_ready, 1)

            latents_lo(2)
            latents(3)
            rotate_q(0)
            rotate_q(1)
            latents_lo(3)
            rotate_q(2)
            rotate_q(3)
            k_out(0, 0)
            dve.wait_ge(ropeT_done, T)
            dve.wait_ge(v_done, 1)
            v_out(0)
            v_out(1)
            k_out(0, 1)
            for j in range(2):
                split("pair", j, 1)
            dve.sem_inc(o_lo, 1)

            def attention(pair, more, between):
                def softmax(hd):
                    def largest(qb):
                        col = 4 * hd + qb
                        dve.wait_ge(scores_done, pair * 8 + col + 1)
                        v.tensor_reduce(neg_max[:, col:col + 1], bank[qb][:, 0:(qb + 1) * P], AX.X, ALU.max, negate=True
                                        ).then_inc(max_ready, 1)

                    def divide(qb):
                        col = 4 * hd + qb
                        at, n = qb * (qb + 1) // 2 * P, (qb + 1) * P
                        dve.wait_ge(exp_ready, pair * 8 + col + 1)
                        v.reciprocal(row_inv[:, col:col + 1], row_sum[:, col:col + 1]).then_inc(inv_ready, 1)
                        dve.wait_ge(inv_ready, pair * 8 + col + 1)
                        v.tensor_scalar(probs[:, hd, at:at + n], probs[:, hd, at:at + n], row_inv[:, col:col + 1], None,
                                        ALU.mult).then_inc(probs_ready, 1)

                    largest(0)
                    largest(1)
                    for qb in range(T):
                        divide(qb)
                        if qb + 2 < T:
                            largest(qb + 2)

                def turned(hd):
                    dve.wait_ge(pT_done, pair * 2 + hd + 1)
                    v.tensor_copy(probsT[:, 512:896], bank[1][:, 0:384]).then_inc(pT_dve, 1)

                def head_out(hd):
                    dve.wait_ge(o_hi, pair * 2 + hd + 1)
                    at = bass.ds(pair * 2 + hd, 1)
                    v.tensor_tensor(oT_lo[:, at, :], bank[3][:, :].unsqueeze(1), oT_hi[:, at, :],
                                    ALU.subtract).then_inc(o_lo, 1)

                softmax(0)
                between(0)
                turned(0)
                if more:
                    k_out(pair + 1, 0)
                head_out(0)
                softmax(1)
                if more:
                    dve.wait_ge(v_done, pair + 2)
                    v_out(0)
                between(1)
                turned(1)
                if more:
                    k_out(pair + 1, 1)
                between(2)
                head_out(1)
                if more:
                    v_out(1)
                between(3)

            def next_pair(pair):
                return lambda place: split("pair", place - 2, pair + 2) if place >= 2 else None

            with dve.Fori(0, H // 2 - 2) as pair:
                attention(pair, True, next_pair(pair))
            attention(H // 2 - 2, True, lambda place: [split("wo", k) for k in ((0,), (1, 2), (3,), (4, 5))[place]])
            attention(H // 2 - 1, False, lambda place: [split("wo", k) for k in ((6,), (7,), (), ())[place]])

            def add_attention(t):
                if t < T - 1:
                    dve.wait_ge(wo_done, t + 1)
                else:
                    dve.wait_ge(wo_freed, H)
                for half in range(2):
                    at = slice(512 * half, 512 * half + 512)
                    last = v.tensor_tensor(h[:, t, at], bank[4 + 2 * (t % 2) + half][:, :], h[:, t, at], ALU.add)
                last.then_inc(h_attn, 1)

            for t in range(T):
                add_attention(t)
                norm_rows(T + t, t)
                if t:
                    norm_lo(T + t - 1, t - 1)
            for j in range(4):
                split("ffn", j)
            norm_lo(2 * T - 1, T - 1)

            def ffn_act(i, j):
                n = i * FG + j + 1
                dve.wait_ge(silu_ready, n)
                v.tensor_tensor(f_act[:, j % 2, :], f_silu[:, j % 2, :], bank[2 * (j % 2) + 1][:, :], ALU.mult
                                ).then_inc(prod_ready, 1)
                dve.wait_ge(act_hi, n)
                v.tensor_tensor(f_lo[:, j, :], f_act[:, j % 2, :], f_hi[:, j, :], ALU.subtract).then_inc(act_lo, 1)

            def ffn(i, following):
                ffn_act(i, 0)
                for j in range(4, 9):
                    split("ffn", j, i)
                ffn_act(i, 1)
                ffn_act(i, 2)
                for half in range(2):
                    following(half)
                    at = slice(512 * half, 512 * half + 512)
                    for t in range(T):
                        dve.wait_ge(ffn_done, i * 8 + 4 * half + t + 1)
                        v.tensor_tensor(h[:, t, at], bank[4 + t][:, :], h[:, t, at], ALU.add).then_inc(h_ffn, 1)

            with dve.Fori(0, FI - 1) as i:
                ffn(i, lambda half: [split("ffn", 2 * half + j, i + 1) for j in range(2)])
            ffn(FI - 1, lambda half: split("pool", half))

            for t in range(T):
                norm_rows(2 * T + t, t)
            for d in range(KD):
                dve.wait_ge(z_hi, d + 1)
                v.tensor_tensor(zT_lo[:, d, :], bank[d % 4][:, :], zT_hi[:, d, :], ALU.subtract).then_inc(z_lo, 1)

            def rows_T(t):
                dve.wait_ge(xnT_done, 2 * T + t + 1)
                v.tensor_copy(xnT[:, 4:8, :], bank[1][:, :].rearrange("p (k n) -> p k n", k=4)).then_inc(xnT_lo, 1)

            def add_mix(t):
                dve.wait_ge(mix_done, t + 1)
                for half in range(2):
                    at = slice(512 * half, 512 * half + 512)
                    link(v.tensor_tensor(ptmp, bank[4 + 2 * (t % 2) + half][:, :], pscale[:, at], ALU.mult))
                    last = v.tensor_tensor(h[:, t, at], h[:, t, at], ptmp, ALU.add)
                    if half == 0:
                        link(last)
                last.then_inc(h_mix, 1)

            dve.wait_ge(pscale_landed, 16)
            for t in range(T):
                add_mix(t)
                norm_rows(3 * T + t, t)
                if t:
                    rows_T(t - 1)
            rows_T(T - 1)

            def tab(n, width=T * E):
                return route[:, n * 32:n * 32 + width]

            def by_expert(n):
                return tab(n).rearrange("p (t e) -> p t e", t=T)

            def per_token(x):
                return x.unsqueeze(2).broadcast_to([P, T, E])

            def per_expert(x):
                return x.unsqueeze(1).broadcast_to([P, T, E])

            logit, eq, first, second, spare = (by_expert(n) for n in range(5))
            best = [tab(5 + n, T) for n in range(4)]
            index, ends, starts, tmp8, count = (tab(9 + n, E) for n in range(5))
            job_no = route[0:1, 640:768].rearrange("p (j e) -> p j e", e=E)
            job_end = route[0:1, 768:896].rearrange("p (j e) -> p j e", e=E)
            job_exp = route[0:1, 896:912]
            place_f = route[:, 912:912 + 2 * T]
            dve.wait_ge(logits_done, 1)
            dve.wait_ge(iotas_ready, 2)
            v.tensor_scalar(index, iota_e[:, :], -float(E), None, ALU.add)
            link(v.tensor_copy(tab(0), bank[2][:, 0:T * E]))

            def pick(logits, top, at, onehot):
                link(v.tensor_reduce(top, logits, AX.X, ALU.max))
                link(v.tensor_tensor(eq, logits, per_token(top), ALU.is_equal))
                link(v.tensor_tensor(eq, eq, per_expert(index), ALU.mult))
                link(v.tensor_reduce(at, eq, AX.X, ALU.min))
                link(v.tensor_tensor(onehot, per_expert(index), per_token(at), ALU.is_equal))

            pick(logit, best[0], best[1], first)
            link(v.scalar_tensor_tensor(spare, first, -1e38, logit, ALU.mult, ALU.add))
            pick(spare, best[2], best[3], second)
            link(v.tensor_tensor(gate1[:, :], best[2], best[0], ALU.subtract))
            v.tensor_tensor(picked[:, :, :], first, second, ALU.add).then_inc(chosen, 1)
            dve.wait_ge(exp_gate, 1)
            link(v.tensor_scalar(gate0[:, :], gate1[:, :], 1.0, None, ALU.add))
            link(v.reciprocal(gate0[:, :], gate0[:, :]))
            link(v.tensor_tensor(gate1[:, :], gate1[:, :], gate0[:, :], ALU.mult))

            dve.wait_ge(rank_done, 1)
            link(v.tensor_copy(count, bank[3][:, T * E:(T + 1) * E]))
            link(v.tensor_scalar(starts, count, float(C), 1.0, ALU.is_gt, ALU.add))
            for more in range(2, -(-S // C)):
                link(v.scalar_tensor_tensor(starts, count, float(more * C), starts, ALU.is_gt, ALU.add))
            link(v.tensor_copy(ends, starts))
            for shift in (1, 2, 4):
                link(v.tensor_copy(tmp8, ends))
                link(v.tensor_tensor(ends[:, shift:], tmp8[:, shift:], tmp8[:, 0:E - shift], ALU.add))
            link(v.tensor_tensor(starts, ends, starts, ALU.subtract))
            link(v.tensor_scalar(starts, starts, float(C), None, ALU.mult))
            link(v.tensor_tensor(spare, bank[3][:, 0:T * E].rearrange("p (t e) -> p t e", t=T), per_expert(starts), ALU.add))
            for n, onehot in enumerate((first, second)):
                link(v.tensor_tensor(eq, onehot, spare, ALU.mult))
                link(v.tensor_reduce(place_f[:, n * T:(n + 1) * T], eq, AX.X, ALU.add))
            link(v.tensor_copy(dest[:, :], place_f))
            link(v.tensor_copy(job_end, ends[0:1, :].unsqueeze(1).broadcast_to([1, 16, E])))
            link(v.tensor_copy(job_no, iota_j[0:1, :].unsqueeze(2).broadcast_to([1, 16, E])))
            link(v.tensor_tensor(job_end, job_end, job_no, ALU.is_le))
            link(v.tensor_reduce(job_exp, job_end, AX.X, ALU.add))
            link(v.tensor_scalar(job_exp, job_exp, float(E - 1), None, ALU.min))
            link(v.tensor_copy(table[0:1, 0:1], ends[0:1, E - 1:E]))
            v.tensor_copy(table[0:1, 1:17], job_exp).then_inc(routed, 1)

            def x_out(at):
                dve.wait_ge(xT_done, at)
                for b, k0, k1 in ((1, 0, 3), (7, 3, 6), (3, 6, 8)):
                    last = v.tensor_copy(xT[:, k0:k1, :], bank[b][:, 0:(k1 - k0) * C].rearrange("p (k n) -> p k n", n=C))
                last.then_inc(xT_ready, 1)

            x_out(1)
            dve.wait_ge(routed, 1)
            jobs = dve.value_load(table[0:1, 0:1], min_val=E, max_val=JMAX)
            with dve.Fori(0, jobs) as job:
                def product(f, par):
                    dve.wait_ge(silu_ready, job * MACTS + f + (FT + 1))
                    v.tensor_tensor(e_act[:, par, :], e_silu[:, par, :], bank[2 * par + 1][:, 0:C], ALU.mult
                                    ).then_inc(prod_ready, 1)

                with dve.Fori(0, FEF // 2) as i:
                    for q in range(2):
                        product(i * 2 + q, q)
                dve.wait_ge(silu_ready, job * MACTS + (FT + MACTS))
                v.tensor_tensor(e_act[0:FTAIL, 0, :], e_silu[0:FTAIL, 0, :], e_up[0:FTAIL, :], ALU.mult
                                ).then_inc(prod_ready, 1)
                x_out(job + 2)

            for t in range(T):
                dve.wait_ge(y_gathered[t % 2], 32 * (t // 2 + 1))
                link(v.scalar_tensor_tensor(h[:, t, :], y_in[:, 2 * (t % 2), :], gate0[:, t:t + 1], h[:, t, :],
                                            ALU.mult, ALU.add))
                v.scalar_tensor_tensor(h[:, t, :], y_in[:, 2 * (t % 2) + 1, :], gate1[:, t:t + 1], h[:, t, :],
                                       ALU.mult, ALU.add).then_inc(h_final, 1)
                dve.wait_ge(std_ready, 4 * T + t + 1)
                link(v.reciprocal(rms[:, t:t + 1], rms[:, t:t + 1]))
                dve.wait_ge(gain_landed, 16 * 5)
                if t >= 2:
                    dve.wait_ge(out_stored[t % 2], 16 * (t // 2))
                v.scalar_tensor_tensor(final[:, t % 2, :], h[:, t, :], rms[:, t:t + 1], gain, ALU.mult, ALU.mult
                                       ).then_inc(out_ready, 1)


_INS = ["x", "positions", "attn_norm", "ffn_norm", "mla_w_down", "mla_q_norm", "mla_w_uq", "mla_kv_norm", "mla_w_ukv",
        "mla_w_o", "pool_w", "pool_scale", "ffn_w_gate", "ffn_w_up", "ffn_w_down", "moe_router", "moe_w_gate", "moe_w_up",
        "moe_w_down", "final_norm"]


def kernel(**inputs):
    import concourse.bacc as _bacc
    from concourse.bass_utils import run_bass_kernel_spmd as _run

    nc = _bacc.Bacc("TRN2", target_bir_lowering=False, num_devices=1)
    arrays = {name: np.ascontiguousarray(inputs[name]) for name in _INS}
    arrays["rope_freq"] = (THETA ** (-np.arange(0, ROPE, 2, dtype=np.float64) / ROPE)).astype(np.float32)[None, :]
    args = {name: nc.dram_tensor(f"in_{name}", v.shape, mybir.dt.from_np(v.dtype), kind="ExternalInput").ap()
            for name, v in arrays.items()}
    out = nc.dram_tensor("out_0", (1, S, D), F32, kind="ExternalOutput").ap()
    trunk(nc, args, out)
    r = _run(nc, [{f"in_{name}": v for name, v in arrays.items()}], core_ids=[0])
    return r.results[0]["out_0"]
```

```python
from contextlib import ExitStack

import concourse.bass as bass
import numpy as np
from concourse import mybir

F32 = mybir.dt.float32
F32R = mybir.dt.float32r
BF16 = mybir.dt.bfloat16
I32 = mybir.dt.int32
ACT = mybir.ActivationFunctionType
ALU = mybir.AluOpType
AX = mybir.AxisListType

P = 128
D = 1024
S = 512
T = S // P
KD = D // P
H = 8
NOPE = 128
ROPE = 64
VD = 128
QR = 512
KVR = 256
DOWN = QR + KVR + ROPE
FF = 2688
FT = FF // P
FG = 3
FI = FT // FG
E = 8
FE = 1344
FEF = FE // P
FTAIL = FE - FEF * P
WINDOWS = (2, 4, 8, 16)
WMAX = max(WINDOWS)
GD = D // len(WINDOWS)
EPS = 1e-6
SCALE = (NOPE + ROPE) ** -0.5
NEG = -1e30
THETA = 10000.0

C = 144
CH = C // 2
NARROW = 128
JMAX = E + 2 * S // (C + 1) + 1
NJ = JMAX + 1
XROWS = (JMAX + 2) * C
ZP = CH
MACTS = FEF + 1
JUNITS = 3 * FEF + 2
AHEAD = 8

ROUND = 1.5 * 2.0 ** 23
TWO_PI = (6.28125, 0.00193500518798828125, 2 * np.pi - 6.28125 - 0.00193500518798828125)
PI_IN = 3.1415925

UNIT = 1024
SLOTS = 8
STAGES = 8
STAGES_OWN = 6


class plan_weights:

    def __init__(self):
        self.at = {}
        flat = []

        def add(name, slots, stages, twice=()):
            for j, (slot, stage) in enumerate(zip(slots, stages)):
                flat.append(((name, j), slot, stage, 2 if j in twice else 1))

        add("down", range(8), (0, 1, 2, 3, 4, 5, 0, 1))
        add("rope", (0, 1), (2, 3), twice=(0, 1))
        for _ in range(H // 2):
            add("pair", (2, 3), (4, 5), twice=(0,))
        add("wo", (4, 5, 6, 7, 0, 1, 2, 3), (0, 1, 2, 3, 4, 5, 0, 1))
        for _ in range(FI):
            add("ffn", (0, 1, 2, 3, 0, 1, 4, 5, 6), (2, 3, 4, 5, 0, 1, 2, 3, 4))
        add("pool", (7, 2), (5, 0))
        self.split = len(flat)
        add("pre", (None,) * 4, (2, 3, 4, 5))
        for _ in range(3):
            for _ in range((FEF - 2) // 2):
                add("step", (None,) * 6, range(6))
            add("tail", (None,) * 8, (0, 1, 6, 7, 2, 3, 4, 5), twice=(1,))
        last, uses, seen = {}, [0] * STAGES, {}
        for n, (place, slot, stage, dmas) in enumerate(flat):
            uses[stage] += dmas
            back = n - last[stage] if stage in last else None
            last[stage] = n
            seen.setdefault(place, []).append((n, uses[stage], back, slot, stage))
        for place, times in seen.items():
            inner = (FEF - 2) // 2 if place[0] == "step" else 1
            backs = [b for _, _, b, _, _ in times if b is not None]
            n0, u0, _, slot, stage = times[0]
            dn, du = (times[1][0] - n0, times[1][1] - u0) if len(times) > 1 else (0, 0)
            jn, ju = (times[inner][0] - n0, times[inner][1] - u0) if len(times) > inner else (0, 0)
            if place[0] == "tail":
                dn = du = 0
            self.at[place] = (n0, u0, dn, du, jn, ju, min(backs) if backs else None, slot, stage)

    def unit(self, name, j, i=0, job=0):
        n0, _, dn, _, jn, _, _, _, _ = self.at[name, j]
        return i * dn + job * jn + n0

    def landed(self, name, j, i=0, job=0):
        _, u0, _, du, _, ju, _, _, _ = self.at[name, j]
        return (i * du + job * ju + u0) * 16

    def back(self, name, j):
        return self.at[name, j][6]

    def slot(self, name, j):
        return self.at[name, j][7]

    def stage(self, name, j):
        return self.at[name, j][8]


def trunk(nc, a, out):
    plan = plan_weights()
    with ExitStack() as ctx:
        def sb(name, shape, dt=F32):
            return ctx.enter_context(nc.sbuf_tensor(name, shape, dt))

        def sem(name):
            return ctx.enter_context(nc.semaphore(name))

        bank = [ctx.enter_context(nc.psum_tensor(f"bank{b}", [P, 512], F32)) for b in range(8)]
        w_hi = sb("w_hi", [P, SLOTS, UNIT], F32R)
        w_lo = sb("w_lo", [P, SLOTS, UNIT], F32R)
        stage_own = sb("stage_own", [P, STAGES_OWN, UNIT])
        big_hi = sb("big_hi", [P, 8 * S], F32R)
        big_lo = sb("big_lo", [P, 8 * S], F32R)
        act_hi_mem = sb("act_hi_mem", [P, 6 * S], F32R)
        act_lo_mem = sb("act_lo_mem", [P, 6 * S], F32R)
        h = sb("h", [P, T, D])
        scratch = sb("scratch", [P, 9216])
        cos_t = sb("cos_t", [P, T, ROPE])
        sin_t = sb("sin_t", [P, T, ROPE])
        ident = sb("ident", [P, P])
        ident_b = sb("ident_b", [P, P], BF16)
        causal = sb("causal", [P, P], BF16)
        ones_b = sb("ones_b", [P, P], BF16)
        before_b = sb("before_b", [P, P], BF16)
        zeros = sb("zeros", [P, P])
        band = sb("band", [P, 4, P + WMAX])
        band0 = sb("band0", [P, 4, WMAX])
        krT = sb("krT", [P, S])
        qr_now = sb("qr_now", [P, S])
        router = sb("router", [P, KD, E])
        eps_t = sb("eps_t", [P, 1])
        warm = sb("warm", [P, 1])
        sumsq = sb("sumsq", [P, 24])
        rms = sb("rms", [P, 24])
        neg_max = sb("neg_max", [P, 8])
        row_sum = sb("row_sum", [P, 8])
        row_inv = sb("row_inv", [P, 8])
        picked = sb("picked", [P, T, E], BF16)
        gate0 = sb("gate0", [P, T])
        gate1 = sb("gate1", [P, T])
        dest = sb("dest", [P, 2 * T], I32)
        table = sb("table", [1, 32], I32)
        posi = sb("posi", [P, T], I32)
        iota_e = sb("iota_e", [P, E])
        iota_j = sb("iota_j", [1, NJ])

        hnT_hi, hnT_lo = (m[:, :].rearrange("p (k s) -> p k s", k=8) for m in (big_hi, big_lo))
        oT_hi, oT_lo, zT_hi, zT_lo = hnT_hi, hnT_lo, hnT_hi, hnT_lo
        cqT_hi, cqT_lo = (m[:, 0:4 * S].rearrange("p (k s) -> p k s", k=4) for m in (act_hi_mem, act_lo_mem))
        ckvT_hi, ckvT_lo = (m[:, 4 * S:6 * S].rearrange("p (k s) -> p k s", k=2) for m in (act_hi_mem, act_lo_mem))
        f_hi, f_lo = (m[:, 0:FG * S].rearrange("p (k s) -> p k s", k=FG) for m in (act_hi_mem, act_lo_mem))

        def view(at, n, k=None):
            v = scratch[:, at:at + n]
            return v if k is None else v.rearrange("p (k n) -> p k n", k=k)

        xn = view(0, T * D, T)
        cn = view(5120, 1792, 2)
        krope_tmp = view(6912, 128, 2)
        gain_c = view(7040, QR + KVR)
        freq = view(5120, ROPE // 2)
        posf = view(5152, T)
        angle, turns, folded, over = (view(5184 + P * n, P, T) for n in range(4))
        trig_arg = view(7808, 384).rearrange("p (a t n) -> p a t n", a=3, t=T)
        gain = view(8192, D)
        qn = view(0, 1024, 2)
        kn = view(1024, 1024, 2)
        v_nat = view(2048, 1024, T)
        qrT = view(3072, 2048, H // 2)
        rope_bank = (0, 1, 4, 0)
        rotated, rope_tmp = ([view(1024 + (t % 2) * 1024 + 512 * n, 512) for t in range(T)] for n in range(2))
        probs = view(5120, 2560, 2)
        probsT = view(7680, 1280)
        f_silu = view(4096, 1024, 2)
        f_act = view(5120, 1024, 2)
        xnT = [view(4096 + 1024 * n, 1024, 8) for n in range(2)]
        pscale = view(6144, 1024)
        logitsT = qr_now[0:E, :]
        iota_c = cos_t[:, :, :].rearrange("p t n -> p (t n)")[:, 0:C]
        chosen_x = view(4096, T * C, T)
        route = view(7168, 1024)
        band_first = view(7168, 4 * (P + WMAX), 4)
        stage_more = view(0, 2048, 2)
        yn = scratch[0:CH, 2048:4096].rearrange("p (k n) -> p k n", k=2)
        xg = scratch[0:CH, 4096:6144].rearrange("p (k n) -> p k n", k=2)
        yT = view(6144, KD * C, KD)
        xT = view(6144 + KD * C, KD * C, KD)
        e_silu = krT[:, 0:2 * C].rearrange("p (k n) -> p k n", k=2)
        e_act = qr_now[:, 0:2 * C].rearrange("p (k n) -> p k n", k=2)
        e_up = e_silu[:, 1, :]
        y_in = view(0, 8 * D, 8)

        def stage(s):
            return stage_own[:, s, :] if s < STAGES_OWN else stage_more[:, s - STAGES_OWN, :]

        xbuf = nc.dram_tensor("xbuf", (XROWS, D), F32, kind="Internal").ap()
        ybuf = nc.dram_tensor("ybuf", (JMAX * C, D), F32, kind="Internal").ap()

        landed = [sem(f"landed{s}") for s in range(STAGES)]
        x_landed = [sem(f"x_landed{t}") for t in range(T)]
        attn_gain_landed = sem("attn_gain_landed")
        gain_landed = sem("gain_landed")
        gainc_landed = sem("gainc_landed")
        freq_landed = sem("freq_landed")
        pos_landed = sem("pos_landed")
        router_landed = sem("router_landed")
        pscale_landed = sem("pscale_landed")
        xg_landed = sem("xg_landed")
        zero_stored = sem("zero_stored")
        scattered = sem("scattered")
        y_stored = sem("y_stored")
        y_gathered = [sem(f"y_gathered{n}") for n in range(2 * T)]
        out_stored = sem("out_stored")
        final_landed = sem("final_landed")
        eps_ready = sem("eps_ready")
        consts_ready = sem("consts_ready")
        counts_ready = sem("counts_ready")
        counts_inv = sem("counts_inv")
        pool_step = sem("pool_step")
        yn_free = sem("yn_free")

        weight_hi = sem("weight_hi")
        weight_lo = sem("weight_lo")
        std_ready = sem("std_ready")
        act_step = sem("act_step")
        xnT_hi = sem("xnT_hi")
        xnT_lo = sem("xnT_lo")
        xn_ready = sem("xn_ready")
        dve_step = sem("dve_step")
        trig_ready = sem("trig_ready")
        trig_done = sem("trig_done")
        iotas_ready = sem("iotas_ready")
        xnT_done = sem("xnT_done")
        c_done = sem("c_done")
        c_std = sem("c_std")
        c_ready = sem("c_ready")
        cT_done = sem("cT_done")
        cT_hi = sem("cT_hi")
        cT_lo = sem("cT_lo")
        down_freed = sem("down_freed")
        rope_done = sem("rope_done")
        rope_ready = sem("rope_ready")
        ropeT_done = sem("ropeT_done")
        qr_ready = sem("qr_ready")
        q_done = sem("q_done")
        k_done = sem("k_done")
        v_done = sem("v_done")
        q_ready = sem("q_ready")
        k_ready = sem("k_ready")
        v_ready = sem("v_ready")
        scores_done = sem("scores_done")
        max_ready = sem("max_ready")
        exp_ready = sem("exp_ready")
        inv_ready = sem("inv_ready")
        probs_ready = sem("probs_ready")
        pT_done = sem("pT_done")
        pT_act = sem("pT_act")
        pT_dve = sem("pT_dve")
        pv_done = sem("pv_done")
        o_hi = sem("o_hi")
        o_lo = sem("o_lo")
        wo_done = sem("wo_done")
        wo_freed = sem("wo_freed")
        h_attn = sem("h_attn")
        gu_done = sem("gu_done")
        silu_ready = sem("silu_ready")
        prod_ready = sem("prod_ready")
        act_hi = sem("act_hi")
        act_lo = sem("act_lo")
        ffn_done = sem("ffn_done")
        h_ffn = sem("h_ffn")
        z_done = sem("z_done")
        z_hi = sem("z_hi")
        z_lo = sem("z_lo")
        mix_done = sem("mix_done")
        h_mix = sem("h_mix")
        pool_scaled = sem("pool_scaled")
        logitsT_done = sem("logitsT_done")
        logitsT_ready = sem("logitsT_ready")
        logits_done = sem("logits_done")
        sel_ready = sem("sel_ready")
        chosen = sem("chosen")
        exp_gate = sem("exp_gate")
        rank_done = sem("rank_done")
        placed = sem("placed")
        routed = sem("routed")
        xT_done = sem("xT_done")
        xT_ready = sem("xT_ready")
        expert_used = sem("expert_used")
        yT_ready = sem("yT_ready")
        y_nat_done = sem("y_nat_done")
        xT_free = sem("xT_free")
        y_ready = sem("y_ready")
        y_ready_dve = sem("y_ready_dve")
        h_final = sem("h_final")
        out_ready = sem("out_ready")

        block = ctx.enter_context(nc.Block())

        gains = {"attn0": a["attn_norm"][0:1], "ffn0": a["ffn_norm"][0:1], "attn1": a["attn_norm"][1:2],
                 "ffn1": a["ffn_norm"][1:2], "final": a["final_norm"].rearrange("(o d) -> o d", o=1)}
        rows_of = {"down": a["mla_w_down"][0], "wo": a["mla_w_o"][0]}
        w_uq = a["mla_w_uq"][0].rearrange("(k p) n -> p k n", p=P)
        w_ukv = a["mla_w_ukv"][0].rearrange("(k p) n -> p k n", p=P)
        f_gate, f_up = (a[n][0].rearrange("(k p) n -> p k n", p=P) for n in ("ffn_w_gate", "ffn_w_up"))
        pool_w = a["pool_w"][0].rearrange("g (k p) n -> p (g k) n", p=P)
        m_gate, m_up = (a[n][0].rearrange("e (k p) n -> e p k n", p=P) for n in ("moe_w_gate", "moe_w_up"))
        m_down = a["moe_w_down"][0]

        @block.sync
        def _(sp):
            def load(name, j, pieces, i=0, job=0):
                back = plan.back(name, j)
                if name in ("step", "tail"):
                    sp.wait_ge(expert_used, plan.unit(name, j, i, job) - (back - 1) + (AHEAD - plan.split))
                elif name == "pre":
                    sp.wait_ge(weight_lo, plan.split)
                elif back is not None:
                    sp.wait_ge(weight_lo, plan.unit(name, j, i, job) - (back - 1))
                s = plan.stage(name, j)
                for dst, src in pieces(stage(s)):
                    sp.dma_start(dst, src).then_inc(landed[s], 16)

            def cols(st, k, n):
                return st[:, 0:k * n].rearrange("p (k n) -> p k n", k=k)

            def x_in(t):
                sp.dma_start(h[:, t, :], a["x"][0, t * P:(t + 1) * P, :]).then_inc(x_landed[t], 16)

            def rows(name, k):
                load(name, k, lambda st: [(st[:, 0:rows_of[name].shape[1]], rows_of[name][k * P:(k + 1) * P, :])])

            x_in(0)
            sp.dma_start(gain, gains["attn0"].partition_broadcast(P).rearrange("p o d -> p (o d)")).then_inc(attn_gain_landed, 16)
            for k in range(4):
                rows("down", k)
            x_in(1)
            for k in range(4, 6):
                rows("down", k)
            x_in(2)
            x_in(3)
            for k in range(6, 8):
                rows("down", k)

            for j in range(2):
                load("rope", j, lambda st: [(st[:, m * 512:m * 512 + 512].rearrange("p (h n) -> p h n", h=H),
                                             w_uq[:, 2 * j + m, :].rearrange("p (h n) -> p h n", h=H)[:, :, NOPE:])
                                            for m in range(2)])
            with sp.Fori(0, H // 2) as pair:
                load("pair", 0, lambda st: [(st.rearrange("p (k h n) -> p k h n", k=4, h=2)[:, :, hd, :],
                                             w_uq[:, :, bass.ds(pair * 384 + hd * 192, NOPE)]) for hd in range(2)], pair)
                load("pair", 1, lambda st: [(cols(st, 2, 512), w_ukv[:, :, bass.ds(pair * 512, 512)])], pair)
            for k in range(8):
                rows("wo", k)

            with sp.Fori(0, FI) as i:
                for j in range(FG):
                    for q, w in enumerate((f_gate, f_up)):
                        load("ffn", 2 * j + q, lambda st: [(cols(st, 8, P), w[:, :, bass.ds(i * (FG * P) + j * P, P)])], i)
                for j in range(FG):
                    load("ffn", 2 * FG + j,
                         lambda st: [(st, a["ffn_w_down"][0, bass.ds(i * (FG * P) + j * P, P), :])], i)
            for j in range(2):
                load("pool", j, lambda st: [(cols(st, 4, GD), pool_w[:, 4 * j:4 * j + 4, :])])

            def expert_cols(w, e, f, n=P):
                return w[bass.ds(e, 1), :, :, f * P:f * P + n].rearrange("o p k n -> p (o k) n")

            for j, (w, f) in enumerate(((m_gate, 0), (m_up, 0), (m_gate, 1), (m_up, 1))):
                load("pre", j, lambda st: [(cols(st, 8, P), w[0, :, :, f * P:(f + 1) * P])])

            sp.wait_ge(routed, 1)
            jobs = sp.value_load(table[0:1, 0:1], min_val=E, max_val=JMAX)
            with sp.Fori(0, jobs) as job:
                e = sp.value_load(table[0:1, bass.ds(job + 1, 1)], min_val=0, max_val=E - 1)
                e_next = sp.value_load(table[0:1, bass.ds(job + 2, 1)], min_val=0, max_val=E - 1)

                def columns(w, ee, off):
                    return w[bass.ds(ee, 1), :, :, bass.ds(off, P)].rearrange("o p k n -> p (o k) n")

                def down_rows(off, n=P):
                    return m_down[bass.ds(e, 1), bass.ds(off, n), :].rearrange("o p n -> p (o n)")

                with sp.Fori(0, (FEF - 2) // 2) as i:
                    for s in range(2):
                        off = i * (2 * P) + s * P
                        load("step", 3 * s, lambda st: [(st, down_rows(off))], i, job)
                        load("step", 3 * s + 1, lambda st: [(cols(st, 8, P), columns(m_gate, e, off + 2 * P))], i, job)
                        load("step", 3 * s + 2, lambda st: [(cols(st, 8, P), columns(m_up, e, off + 2 * P))], i, job)
                load("tail", 0, lambda st: [(st, down_rows((FEF - 2) * P))], 0, job)
                load("tail", 1, lambda st: [(cols(st, 8, P)[:, :, q * FTAIL:(q + 1) * FTAIL],
                                             expert_cols(w, e, FEF, FTAIL)) for q, w in enumerate((m_gate, m_up))], 0, job)
                sp.wait_ge(scattered, 16 * 2 * T)
                sp.wait_ge(xT_done, 1)
                load("tail", 2, lambda st: [(st, down_rows((FEF - 1) * P))], 0, job)
                load("tail", 3, lambda st: [(st[0:FTAIL, :], down_rows(FEF * P, FTAIL))], 0, job)
                for j, (w, f) in enumerate(((m_gate, 0), (m_up, 0), (m_gate, 1), (m_up, 1))):
                    load("tail", 4 + j, lambda st: [(cols(st, 8, P), expert_cols(w, e_next, f))], 0, job)
            sp.wait_ge(out_stored, 16 * T)

        @block.gpsimd
        def _(pool):
            steps = [0]

            def link(ins):
                steps[0] += 1
                ins.then_inc(pool_step, 1)
                pool.wait_ge(pool_step, steps[0])

            g = nc.gpsimd
            g.memset(eps_t[:, :], EPS).then_inc(eps_ready, 1)
            g.memset(ident[:, :], 0.0)
            link(g.memset(ident_b[:, :], 0.0))
            for m in (ident, ident_b):
                last = g.affine_select(out=m[:, :], in_=m[:, :], compare_op=ALU.not_equal, fill=1.0, base=0,
                                       pattern=[[-1, P]], channel_multiplier=1)
            last.then_inc(consts_ready, 1)
            g.memset(causal[:, :], 0.0)
            g.memset(zeros[:, :], 0.0)
            g.memset(ones_b[:, :], 1.0)
            link(g.memset(before_b[:, :], 1.0))
            g.affine_select(out=causal[:, :], in_=causal[:, :], compare_op=ALU.is_ge, fill=NEG, base=0,
                            pattern=[[-1, P]], channel_multiplier=1)
            g.affine_select(out=before_b[:, :], in_=before_b[:, :], compare_op=ALU.is_ge, fill=0.0, base=-1,
                            pattern=[[1, P]], channel_multiplier=-1).then_inc(consts_ready, 1)
            pool.dma_start(gain_c[:, 0:QR], a["mla_q_norm"].partition_broadcast(P).rearrange("p o d -> p (o d)")
                           ).then_inc(gainc_landed, 16)
            pool.dma_start(gain_c[:, QR:], a["mla_kv_norm"].partition_broadcast(P).rearrange("p o d -> p (o d)")
                           ).then_inc(gainc_landed, 16)
            pool.dma_start(router[:, :, :], a["moe_router"][0].rearrange("(k p) e -> p k e", p=P),
                           allow_slow_non_contiguous=True).then_inc(router_landed, 16)
            g.iota(iota_e[:, :], [[1, E]], base=0, channel_multiplier=0, allow_small_or_imprecise_dtypes=True
                   ).then_inc(iotas_ready, 1)
            g.iota(iota_j[:, :], [[1, NJ]], base=0, channel_multiplier=0, allow_small_or_imprecise_dtypes=True
                   ).then_inc(iotas_ready, 1)
            for n, w in enumerate(WINDOWS):
                g.memset(band[:, n, :], 1.0 / w)
                g.iota(band0[:, n, :], [[1, WMAX]], base=1, channel_multiplier=0, allow_small_or_imprecise_dtypes=True
                       ).then_inc(pool_step, 1)
                steps[0] += 1
            pool.wait_ge(pool_step, steps[0])
            for n, w in enumerate(WINDOWS):
                g.tensor_scalar(band0[:, n, :], band0[:, n, :], float(w), None, ALU.min).then_inc(counts_ready, 1)
            pool.wait_ge(counts_inv, 1)
            for n, w in enumerate(WINDOWS):
                for m, width in ((band, P + WMAX), (band0, WMAX)):
                    link(g.affine_select(out=m[:, n, :], in_=m[:, n, :], compare_op=ALU.is_ge, fill=0.0, base=0,
                                         pattern=[[1, width]], channel_multiplier=-1))
                    link(g.affine_select(out=m[:, n, :], in_=m[:, n, :], compare_op=ALU.is_ge, fill=0.0, base=w - 1,
                                         pattern=[[-1, width]], channel_multiplier=1))
                link(g.tensor_tensor(band[:, n, 0:P], band[:, n, 0:P], ident[:, :], ALU.subtract))
                link(g.tensor_tensor(band0[:, n, :], band0[:, n, :], ident[:, 0:WMAX], ALU.subtract))
            pool.sem_inc(consts_ready, 1)

            pool.wait_ge(weight_lo, plan.unit("pair", 1, 1) + 1)
            half = (JMAX + 2) // 2 * C
            for rows in (xbuf[0:half, :], xbuf[half:, :], ybuf[E * C:, :]):
                pool.dma_start(rows.rearrange("(p r) (c n) -> p (r c) n", p=ZP, n=P),
                               zeros[0:ZP, :].unsqueeze(1).broadcast_to([ZP, rows.shape[0] // ZP * (D // P), P])
                               ).then_inc(zero_stored, 16)

            pool.wait_ge(pv_done, H)
            pool.wait_ge(pT_dve, H)
            pool.wait_ge(xn_ready, T)
            g.iota(iota_c, [[1, C]], base=0, channel_multiplier=0, allow_small_or_imprecise_dtypes=True
                   ).then_inc(iotas_ready, 1)
            link(g.tensor_copy(band_first, band[:, :, :]))
            g.tensor_copy(band_first[:, :, 0:WMAX], band0[:, :, :]).then_inc(consts_ready, 1)
            pool.dma_start(gain, gains["ffn0"].partition_broadcast(P).rearrange("p o d -> p (o d)")).then_inc(gain_landed, 16)
            pool.wait_ge(xn_ready, 2 * T)
            pool.dma_start(gain, gains["attn1"].partition_broadcast(P).rearrange("p o d -> p (o d)")).then_inc(gain_landed, 16)
            pool.dma_start(pscale, a["pool_scale"].partition_broadcast(P).rearrange("p o d -> p (o d)")
                           ).then_inc(pscale_landed, 16)
            pool.wait_ge(xn_ready, 3 * T)
            pool.dma_start(gain, gains["ffn1"].partition_broadcast(P).rearrange("p o d -> p (o d)")).then_inc(gain_landed, 16)

            pool.wait_ge(placed, 1)
            pool.wait_ge(zero_stored, 48)
            for c in range(2 * T):
                pool.indirect_dma_start(out=xbuf, out_offset=bass.IndirectOffsetOnAxis(ap=dest[:, c:c + 1], axis=0),
                                        in_=xn[:, c % T, :], in_offset=None).then_inc(scattered, 16)
            pool.wait_ge(scattered, 16 * 2 * T)
            pool.sem_inc(yn_free, 1)
            pool.wait_ge(xT_done, 1)
            pool.dma_start(xg, xbuf[C:2 * C, :].rearrange("(k p) n -> p k n", p=CH)).then_inc(xg_landed, 16)
            pool.wait_ge(routed, 1)
            jobs = pool.value_load(table[0:1, 0:1], min_val=E, max_val=JMAX)
            with pool.Fori(0, jobs) as job:
                pool.wait_ge(xT_done, job + 2)
                pool.dma_start(xg, xbuf[bass.ds(job * C + 2 * C, C), :].rearrange("(k p) n -> p k n", p=CH)
                               ).then_inc(xg_landed, 16)
                pool.wait_ge(y_ready, job + 2)
                pool.wait_ge(y_ready_dve, job + 2)
                pool.dma_start(ybuf[bass.ds(job * C, C), :].rearrange("(k p) n -> p k n", p=CH), yn
                               ).then_inc(y_stored, 16)
                pool.wait_ge(xg_landed, job * 16 + 32)
                pool.wait_ge(y_stored, job * 16 + 16)
                pool.sem_inc(yn_free, 1)
            for t in range(T):
                if t == T - 1:
                    pool.wait_ge(xT_free, 1)
                for k in range(2):
                    pool.indirect_dma_start(out=y_in[:, 2 * t + k, :], out_offset=None, in_=ybuf,
                                            in_offset=bass.IndirectOffsetOnAxis(ap=dest[:, k * T + t:k * T + t + 1], axis=0)
                                            ).then_inc(y_gathered[2 * t + k], 16)

        @block.scalar
        def _(act):
            s = nc.scalar
            steps = [0]

            def link(ins):
                steps[0] += 1
                ins.then_inc(act_step, 1)
                act.wait_ge(act_step, steps[0])

            def split(name, j, i=0, n=UNIT):
                st, sl = plan.stage(name, j), plan.slot(name, j)
                act.wait_ge(landed[st], plan.landed(name, j, i))
                s.copy(w_hi[:, sl, 0:n], stage(st)[:, 0:n]).then_inc(weight_hi, 1)

            def norm_std(q, t):
                link(s.activation(xn[:, t, :], h[:, t, :], ACT.Square, scale=D ** -0.5, accum_out=sumsq[:, q:q + 1]))
                s.activation(rms[:, q:q + 1], sumsq[:, q:q + 1], ACT.Sqrt, bias=eps_t[:, 0:1]).then_inc(std_ready, 1)

            def norm_hi(q, t, banks=(0, 1)):
                act.wait_ge(xnT_done, q + 1)
                for b in range(2):
                    last = s.copy(hnT_hi[:, 4 * b:4 * b + 4, t * P:(t + 1) * P],
                                  bank[banks[b]][:, :].rearrange("p (k n) -> p k n", k=4))
                last.then_inc(xnT_hi, 1)

            act.dma_start(posi[:, :], a["positions"].rearrange("o (t p) -> p (o t)", p=P),
                          allow_slow_non_contiguous=True).then_inc(pos_landed, 16)
            act.dma_start(freq, a["rope_freq"].partition_broadcast(P).rearrange("p o d -> p (o d)")
                          ).then_inc(freq_landed, 16)
            act.wait_ge(eps_ready, 1)
            s.activation(warm[:, 0:1], eps_t[:, 0:1], ACT.Sqrt)
            def x_std(t):
                act.wait_ge(x_landed[t], 16)
                norm_std(t, t)

            def c_std_of(t):
                if t < T - 1:
                    act.wait_ge(c_done, t + 1)
                else:
                    act.wait_ge(down_freed, KD)
                b = 4 + 2 * (t % 2)
                s.activation(cn[:, t % 2, 0:QR], bank[b][:, :], ACT.Square, scale=QR ** -0.5, accum_out=sumsq[:, 16 + t:17 + t])
                link(s.activation(cn[:, t % 2, QR:QR + KVR], bank[b + 1][:, 0:KVR], ACT.Square, scale=KVR ** -0.5,
                                  accum_out=sumsq[:, 20 + t:21 + t]))
                s.activation(rms[:, 16 + t:17 + t], sumsq[:, 16 + t:17 + t], ACT.Sqrt, bias=eps_t[:, 0:1])
                s.activation(rms[:, 20 + t:21 + t], sumsq[:, 20 + t:21 + t], ACT.Sqrt, bias=eps_t[:, 0:1]).then_inc(c_std, 1)

            def c_hi(t):
                act.wait_ge(cT_done, t + 1)
                tok = slice(t * P, (t + 1) * P)
                s.copy(cqT_hi[:, :, tok], bank[2][:, :].rearrange("p (k n) -> p k n", k=4))
                s.copy(ckvT_hi[:, :, tok], bank[3][:, 0:2 * P].rearrange("p (k n) -> p k n", k=2)).then_inc(cT_hi, 1)

            x_std(0)
            for k in range(2):
                split("down", k, n=DOWN)
            norm_hi(0, 0)
            for k in range(2, 4):
                split("down", k, n=DOWN)
            x_std(1)
            for k in range(4, 8):
                split("down", k, n=DOWN)
            norm_hi(1, 1)
            x_std(2)
            x_std(3)
            act.wait_ge(trig_ready, 1)
            s.activation(sin_t[:, :, 32:64], trig_arg[:, 0], ACT.Sin)
            s.activation(cos_t[:, :, 0:32], trig_arg[:, 1], ACT.Sin)
            s.activation(cos_t[:, :, 32:64], trig_arg[:, 1], ACT.Sin)
            s.activation(sin_t[:, :, 0:32], trig_arg[:, 2], ACT.Sin).then_inc(trig_done, 1)
            c_std_of(0)
            norm_hi(2, 2)
            norm_hi(3, 3)
            c_hi(0)
            c_std_of(1)
            c_hi(1)
            c_std_of(2)
            for j, (name, n) in enumerate((("rope", 0), ("rope", 1), ("pair", 0))):
                act.wait_ge(down_freed, j + 1)
                split(name, n)

            def qr_out(t):
                act.wait_ge(ropeT_done, t + 1)
                s.mul(qrT[:, :, t * P:(t + 1) * P], bank[rope_bank[t]][:, :].rearrange("p (k n) -> p k n", k=4), SCALE
                      ).then_inc(qr_ready, 1)

            def q_out(pair, hd):
                act.wait_ge(q_done, 2 * pair + (hd + 1))
                s.mul(qn[:, hd, :], bank[4][:, :], SCALE).then_inc(q_ready, 1)

            c_hi(2)
            c_std_of(3)
            split("pair", 1)
            qr_out(0)
            c_hi(3)
            qr_out(1)
            qr_out(2)
            q_out(0, 0)
            qr_out(3)
            act.wait_ge(qr_ready, T)
            s.copy(qr_now[:, :], qrT[:, 0, :])
            q_out(0, 1)
            act.wait_ge(k_done, 2)
            for j in range(2):
                split("pair", j, 1)

            def attention(pair, more, between):
                def exps(hd):
                    for qb in range(T):
                        n = (qb + 1) * P
                        at = qb * (qb + 1) // 2 * P
                        col = 4 * hd + qb
                        act.wait_ge(max_ready, pair * 8 + col + 1)
                        s.activation(probs[:, hd, at:at + n], bank[qb][:, 0:n], ACT.Exp, bias=neg_max[:, col:col + 1],
                                     accum_out=row_sum[:, col:col + 1]).then_inc(exp_ready, 1)

                def turned(hd):
                    act.wait_ge(pT_done, pair * 2 + hd + 1)
                    s.copy(probsT[:, 0:512], bank[0][:, :])
                    s.copy(probsT[:, 896:1280], bank[2][:, 0:384]).then_inc(pT_act, 1)

                def head_out(hd):
                    act.wait_ge(pv_done, pair * 2 + hd + 1)
                    s.copy(oT_hi[:, bass.ds(pair * 2 + hd, 1), :], bank[3][:, :].unsqueeze(1)).then_inc(o_hi, 1)

                exps(0)
                between(0)
                if more:
                    q_out(pair + 1, 0)
                turned(0)
                head_out(0)
                exps(1)
                if more:
                    s.copy(qr_now[:, :].unsqueeze(1), qrT[:, bass.ds(pair + 1, 1), :])
                between(1)
                if more:
                    q_out(pair + 1, 1)
                turned(1)
                between(2)
                head_out(1)
                between(3)

            def next_pair(pair):
                def between(place):
                    if place >= 2:
                        act.wait_ge(k_done, pair * 2 + 4)
                        split("pair", place - 2, pair + 2)
                return between

            with act.Fori(0, H // 2 - 2) as pair:
                attention(pair, True, next_pair(pair))
            attention(H // 2 - 2, True, lambda place: [split("wo", k) for k in ((0,), (1, 2), (3,), (4, 5))[place]])
            act.wait_ge(k_done, H)
            attention(H // 2 - 1, False, lambda place: [split("wo", k) for k in ((6,), (7,), (), ())[place]])

            def ffn_split(j):
                act.wait_ge(wo_freed, 5 + j)
                split("ffn", j)

            for t in range(T):
                if t == T - 1:
                    ffn_split(0)
                    norm_hi(T + 2, 2)
                    ffn_split(1)
                act.wait_ge(h_attn, t + 1)
                norm_std(T + t, t)
                if 0 < t < T - 1:
                    norm_hi(T + t - 1, t - 1)
            norm_hi(2 * T - 1, T - 1, banks=(2, 3))
            ffn_split(2)
            ffn_split(3)

            def ffn_act(i, j):
                act.wait_ge(gu_done, i * FG + j + 1)
                s.activation(f_silu[:, j % 2, :], bank[2 * (j % 2)][:, :], ACT.Silu).then_inc(silu_ready, 1)
                act.wait_ge(prod_ready, i * FG + j + 1)
                s.copy(f_hi[:, j, :], f_act[:, j % 2, :]).then_inc(act_hi, 1)

            def ffn(i, following):
                ffn_act(i, 0)
                for j in range(4, 9):
                    split("ffn", j, i)
                ffn_act(i, 1)
                ffn_act(i, 2)
                following()

            with act.Fori(0, FI - 1) as i:
                ffn(i, lambda: [split("ffn", j, i + 1) for j in range(4)])

            def last_splits():
                s.activation(warm[:, 0:1], eps_t[:, 0:1], ACT.Sqrt)
                for j in range(2):
                    act.wait_ge(pool_scaled, j + 1)
                    split("pool", j)

            ffn(FI - 1, last_splits)

            for t in range(T):
                act.wait_ge(h_ffn, 8 * (FI - 1) + 4 + t + 1)
                norm_std(2 * T + t, t)
            for d in range(KD):
                act.wait_ge(z_done, d + 1)
                s.copy(zT_hi[:, d, :], bank[d][:, :]).then_inc(z_hi, 1)

            def rows_T(t):
                act.wait_ge(xnT_done, 2 * T + t + 1)
                s.copy(xnT[t % 2][:, 0:4, :], bank[6][:, :].rearrange("p (k n) -> p k n", k=4)).then_inc(xnT_hi, 1)

            for t in range(T):
                act.wait_ge(h_mix, t + 1)
                norm_std(3 * T + t, t)
                if t == 2:
                    rows_T(0)
            for t in range(1, T):
                rows_T(t)
            act.wait_ge(chosen, 1)
            s.activation(gate1[:, :], gate1[:, :], ACT.Exp).then_inc(exp_gate, 1)

            act.wait_ge(routed, 1)
            act.sem_inc(y_ready, 1)
            jobs = act.value_load(table[0:1, 0:1], min_val=E, max_val=JMAX)
            wide = act.value_load(table[0:1, NJ + 1:NJ + 2], min_val=1, max_val=JMAX)

            def expert_job(job, n):
                used = job * JUNITS + AHEAD

                def silu(par, count):
                    act.wait_ge(expert_used, used + count)
                    s.activation(e_silu[:, par, 0:n], bank[2 * par][:, 0:n], ACT.Silu).then_inc(silu_ready, 1)

                silu(0, 2)
                with act.Fori(0, (FEF - 2) // 2) as i:
                    silu(1, i * 6 + 4)
                    silu(0, i * 6 + 7)
                silu(1, JUNITS - 4)
                act.wait_ge(expert_used, used + (JUNITS - 2))
                act.wait_ge(prod_ready, job * MACTS + (FT + MACTS - 1))
                s.activation(e_silu[0:FTAIL, 0, 0:n], bank[0][0:FTAIL, 0:n], ACT.Silu)
                s.copy(e_up[0:FTAIL, 0:n], bank[0][FTAIL:P, 0:n]).then_inc(silu_ready, 1)
                act.wait_ge(expert_used, used + JUNITS)
                for b, k0, k1 in ((4, 0, 3), (5, 3, 6), (6, 6, 8)):
                    last = s.copy(yT[:, k0:k1, 0:n], bank[b][:, 0:(k1 - k0) * C].rearrange("p (k n) -> p k n", n=C)[:, :, 0:n])
                last.then_inc(yT_ready, 1)
                act.wait_ge(y_nat_done, job + 1)
                act.wait_ge(yn_free, job + 1)
                for b in range(2):
                    last = s.copy(yn[:, 0, b * 512:b * 512 + 512], bank[4 + b][0:CH, :])
                last.then_inc(y_ready, 1)

            with act.Fori(0, wide) as job:
                expert_job(job, C)
            with act.Fori(wide, jobs) as job:
                expert_job(job, NARROW)

            act.wait_ge(expert_used, jobs * JUNITS + (AHEAD + 2))
            s.activation(warm[:, 0:1], eps_t[:, 0:1], ACT.Sqrt).then_inc(xT_free, 1)
            act.dma_start(gain, gains["final"].partition_broadcast(P).rearrange("p o d -> p (o d)")).then_inc(final_landed, 16)
            for t in range(T):
                act.wait_ge(h_final, t + 1)
                link(s.activation(y_in[:, 2 * t + 1, :], h[:, t, :], ACT.Square, scale=D ** -0.5, accum_out=sumsq[:, t:t + 1]))
                s.activation(rms[:, t:t + 1], sumsq[:, t:t + 1], ACT.Sqrt, bias=eps_t[:, 0:1]).then_inc(std_ready, 1)
                if t:
                    act.wait_ge(out_ready, t)
                    act.dma_start(out[0, (t - 1) * P:t * P, :], y_in[:, 2 * t - 2, :]).then_inc(out_stored, 16)
            act.wait_ge(out_ready, T)
            act.dma_start(out[0, S - P:S, :], y_in[:, 2 * T - 2, :]).then_inc(out_stored, 16)
            act.wait_ge(out_stored, 16 * T)

        @block.tensor
        def _(pe):
            t_ = nc.tensor

            def mm3(dst, st_hi, st_lo, mv_hi, mv_lo, start, stop, check=False):
                t_.matmul(dst, st_lo, mv_hi, start=start, stop=False, skip_group_check=check)
                t_.matmul(dst, st_hi, mv_lo, start=False, stop=False, skip_group_check=check)
                return t_.matmul(dst, st_hi, mv_hi, start=False, stop=stop, skip_group_check=check)

            def weights(name, j, i=0):
                pe.wait_ge(weight_lo, plan.unit(name, j, i) + 1)
                return plan.slot(name, j)

            def transposes(src, banks):
                for k in range(8):
                    last = t_.transpose(bank[banks[k // 4]][:, k % 4 * P:k % 4 * P + P], src[:, k * P:(k + 1) * P], ident[:, :])
                return last

            def norm_T(q, t, banks=(0, 1)):
                pe.wait_ge(xn_ready, q + 1)
                if q:
                    pe.wait_ge(xnT_hi, q)
                    pe.wait_ge(xnT_lo, q)
                transposes(xn[:, t, :], banks).then_inc(xnT_done, 1)

            def tok(t):
                return slice(t * P, (t + 1) * P)

            def down(t, between=None):
                pe.wait_ge(xnT_lo, t + 1)
                if t >= 2:
                    pe.wait_ge(c_ready, t - 1)
                b = 4 + 2 * (t % 2)

                def part(k, half):
                    lo, hi = ((0, QR), (QR, DOWN))[half]
                    sl = weights("down", k)
                    return mm3(bank[b + half][:, 0:hi - lo], hnT_hi[:, k, tok(t)], hnT_lo[:, k, tok(t)],
                               w_hi[:, sl, lo:hi], w_lo[:, sl, lo:hi], k == 0, k == KD - 1)

                for k in range(KD):
                    if k == 6 and between:
                        between()
                    for half in range(2):
                        last = part(k, half)
                    if t == T - 1:
                        last.then_inc(down_freed, 1)
                if t < T - 1:
                    last.then_inc(c_done, 1)

            def latents_T(t):
                pe.wait_ge(c_ready, t + 1)
                if t:
                    pe.wait_ge(cT_lo, t)
                for k in range(7):
                    last = t_.transpose(bank[2 + k // 4][:, k % 4 * P:k % 4 * P + P], cn[:, t % 2, k * P:(k + 1) * P],
                                        ident[:, :])
                last.then_inc(cT_done, 1)

            pe.wait_ge(consts_ready, 2)
            norm_T(0, 0)
            down(0, lambda: norm_T(1, 1))
            down(1, lambda: norm_T(2, 2))
            norm_T(3, 3)
            latents_T(0)
            down(2)
            latents_T(1)

            def rope_q(t):
                pe.wait_ge(cT_lo, t + 1)
                if t == 3:
                    pe.wait_ge(qr_ready, 1)
                for k in range(4):
                    sl = weights("rope", k // 2)
                    at = slice(k % 2 * 512, k % 2 * 512 + 512)
                    last = mm3(bank[rope_bank[t]][:, :], cqT_hi[:, k, tok(t)], cqT_lo[:, k, tok(t)], w_hi[:, sl, at], w_lo[:, sl, at],
                               k == 0, k == 3)
                last.then_inc(rope_done, 1)

            def rope_T(t):
                pe.wait_ge(rope_ready, t + 1)
                for k in range(4):
                    last = t_.transpose(bank[rope_bank[t]][:, tok(k)], rotated[t][:, tok(k)], ident[:, :])
                last.then_inc(ropeT_done, 1)

            def wq(part, k, hd):
                m = (w_hi, w_lo)[part][:, plan.slot("pair", 0), :].rearrange("p (k h n) -> p k h n", k=4, h=2)
                return m[:, k, hd, :]

            def wkv(part, k):
                m = (w_hi, w_lo)[part][:, plan.slot("pair", 1), :].rearrange("p (k h n) -> p k h n", k=2, h=2)
                return m[:, k]

            def q_head(pair, hd, first=False):
                if not first:
                    pe.wait_ge(q_ready, 2 * pair + hd)
                weights("pair", 0, pair)
                for k in range(4):
                    last = mm3(bank[4][:, :], wq(0, k, hd), wq(1, k, hd), cqT_hi[:, k, :], cqT_lo[:, k, :], k == 0, k == 3)
                last.then_inc(q_done, 1)

            def k_head(pair, hd, first=False):
                if not first:
                    pe.wait_ge(k_ready, 2 * pair + hd)
                weights("pair", 1, pair)
                for k in range(2):
                    last = mm3(bank[5][:, :], wkv(0, k)[:, hd, 0:NOPE], wkv(1, k)[:, hd, 0:NOPE],
                               ckvT_hi[:, k, :], ckvT_lo[:, k, :], k == 0, k == 1)
                last.then_inc(k_done, 1)

            def values(pair, first=False):
                if not first:
                    pe.wait_ge(v_ready, 2 * pair)
                weights("pair", 1, pair)
                for t in range(T):
                    for k in range(2):
                        last = mm3(bank[6 + t // 2][:, t % 2 * 256:t % 2 * 256 + 256].rearrange("p (h n) -> p h n", h=2),
                                   ckvT_hi[:, k, tok(t)], ckvT_lo[:, k, tok(t)], wkv(0, k)[:, :, NOPE:], wkv(1, k)[:, :, NOPE:],
                                   k == 0, k == 1)
                last.then_inc(v_done, 1)

            down(3, lambda: rope_q(0))
            latents_T(2)
            rope_q(1)
            rope_q(2)
            rope_T(0)
            latents_T(3)
            rope_T(1)
            rope_q(3)
            rope_T(2)
            pe.wait_ge(qr_ready, 3)
            q_head(0, 0, True)
            k_head(0, 0, True)
            rope_T(3)
            values(0, True)
            q_head(0, 1)
            k_head(0, 1)

            def attention(pair, filler):
                def scores(hd):
                    if hd == 0:
                        pe.wait_ge(q_ready, pair * 2 + 2)
                        pe.wait_ge(k_ready, pair * 2 + 2)
                    r = slice(ROPE * hd, ROPE * hd + ROPE)
                    for qb in range(T):
                        if qb == T - 1:
                            pe.wait_ge(o_lo, pair * 2 + hd + 1)
                        dst, n = bank[qb], (qb + 1) * P
                        t_.matmul(dst[:, 0:n], qn[:, hd, tok(qb)], kn[:, hd, 0:n], start=True, stop=False)
                        t_.matmul(dst[:, 0:n], qr_now[r, tok(qb)], krT[r, 0:n], start=False, stop=False)
                        t_.matmul(dst[:, tok(qb)], ident_b[:, :], causal[:, :], start=False, stop=True
                                  ).then_inc(scores_done, 1)

                def turn(hd):
                    for qb in range(T):
                        pe.wait_ge(probs_ready, pair * 8 + 4 * hd + qb + 1)
                        at = qb * (qb + 1) // 2 * P
                        for kb in range(qb + 1):
                            col = (qb - kb) * P + (256 if kb == 3 else 0)
                            last = t_.transpose(bank[min(kb, 2)][:, col:col + P],
                                                probs[:, hd, at + kb * P:at + kb * P + P], ident[:, :])
                    last.then_inc(pT_done, 1)

                def head_out(hd):
                    pe.wait_ge(pT_act, pair * 2 + hd + 1)
                    pe.wait_ge(pT_dve, pair * 2 + hd + 1)
                    pe.wait_ge(v_ready, pair * 2 + hd + 1)
                    for kb, at in enumerate((0, 512, 896, 1152)):
                        last = t_.matmul(bank[3][:, kb * P:S], v_nat[:, kb, hd * VD:(hd + 1) * VD],
                                         probsT[:, at:at + S - kb * P], start=kb == 0, stop=kb == T - 1)
                    last.then_inc(pv_done, 1)

                for hd in range(2):
                    scores(hd)
                    filler(2 * hd)
                    turn(hd)
                    filler(2 * hd + 1)
                    head_out(hd)

            def next_pair(pair):
                def filler(place):
                    if place == 0:
                        q_head(pair + 1, 0)
                    elif place == 1:
                        k_head(pair + 1, 0)
                    elif place == 2:
                        values(pair + 1)
                        q_head(pair + 1, 1)
                    else:
                        k_head(pair + 1, 1)
                return filler

            with pe.Fori(0, H // 2 - 1) as pair:
                attention(pair, next_pair(pair))

            def wo_part(t, k):
                sl = weights("wo", k)
                for half in range(2):
                    at = slice(512 * half, 512 * half + 512)
                    last = mm3(bank[4 + 2 * (t % 2) + half][:, :], oT_hi[:, k, tok(t)], oT_lo[:, k, tok(t)],
                               w_hi[:, sl, at], w_lo[:, sl, at], k == 0, k == H - 1)
                if t == T - 1:
                    last.then_inc(wo_freed, 1)
                elif k == H - 1:
                    last.then_inc(wo_done, 1)

            def first_heads(place):
                if place == 2:
                    pe.wait_ge(v_ready, H)
                for t, k in (((0, 0), (0, 1), (0, 2)), ((0, 3), (0, 4)), ((0, 5), (1, 0), (1, 1)), ((1, 2), (1, 3)))[place]:
                    wo_part(t, k)

            attention(H // 2 - 1, first_heads)
            for k in (4, 5):
                wo_part(1, k)
            for k in (H - 2, H - 1):
                pe.wait_ge(o_lo, 1 + k + 1)
                for t in range(2):
                    wo_part(t, k)
            pe.wait_ge(h_attn, 1)
            for k in range(H):
                wo_part(2, k)
            norm_T(T, 0)
            pe.wait_ge(h_attn, 2)
            for k in range(H):
                if k in (2, 6):
                    norm_T(T + 1 + k // 4, 1 + k // 4)
                wo_part(3, k)

            def gate_or_up(i, j, q):
                sl = weights("ffn", 2 * j + q, i)
                for k in range(KD):
                    last = mm3(bank[2 * (j % 2) + q][:, :], w_hi[:, sl, k * P:(k + 1) * P], w_lo[:, sl, k * P:(k + 1) * P],
                               hnT_hi[:, k, :], hnT_lo[:, k, :], k == 0, k == KD - 1)
                return last

            def first_tile():
                for lo, hi in ((0, S - P), (S - P, S)):
                    if lo:
                        pe.wait_ge(xnT_lo, 2 * T)
                    for q in range(2):
                        sl = weights("ffn", q)
                        if lo == 0:
                            if q == 0:
                                pe.wait_ge(xnT_lo, 2 * T - 1)
                            else:
                                norm_T(2 * T - 1, T - 1, banks=(2, 3))
                        for k in range(KD):
                            last = mm3(bank[q][:, lo:hi], w_hi[:, sl, k * P:(k + 1) * P], w_lo[:, sl, k * P:(k + 1) * P],
                                       hnT_hi[:, k, lo:hi], hnT_lo[:, k, lo:hi], k == 0 and lo == 0, k == KD - 1 and hi == S,
                                       check=True)
                return last

            def ffn(i, first=False):
                for j in range(FG):
                    if j == 2:
                        pe.wait_ge(prod_ready, i * FG + 1)
                    if first and j == 0:
                        last = first_tile()
                    else:
                        for q in range(2):
                            last = gate_or_up(i, j, q)
                    last.then_inc(gu_done, 1)
                sl = [weights("ffn", 2 * FG + j, i) for j in range(FG)]
                pe.wait_ge(act_lo, i * FG + 2)
                for half in range(2):
                    at = slice(512 * half, 512 * half + 512)
                    for j in range(FG):
                        if j == 2 and half == 0:
                            pe.wait_ge(act_lo, i * FG + 3)
                        for t in range(T):
                            if j == 0 and half:
                                pe.wait_ge(h_ffn, i * 8 + t + 1)
                            elif j == 0 and first:
                                pe.wait_ge(h_attn, T)
                            last = mm3(bank[4 + t][:, :], f_hi[:, j, tok(t)], f_lo[:, j, tok(t)],
                                       w_hi[:, sl[j], at], w_lo[:, sl[j], at], j == 0, j == FG - 1)
                            if j == FG - 1:
                                last.then_inc(ffn_done, 1)

            ffn(0, first=True)
            with pe.Fori(0, FI - 1) as i:
                ffn(i + 1)

            pe.wait_ge(consts_ready, 4)
            for t, d in [(t, d) for t in range(2) for d in range(KD)] + [(t, d) for d in range(KD) for t in range(2, T)]:
                if d == 0:
                    pe.wait_ge(xn_ready, 2 * T + t + 1)
                n = P + WMAX if t < T - 1 else P
                bands = (band_first if t == 0 else band)[:, d // 2, 0:n]
                last = t_.matmul(bank[d][:, t * P:t * P + n], xn[:, t, d * P:(d + 1) * P], bands,
                                 start=t == 0, stop=t == T - 1, skip_group_check=True)
                if t == T - 1:
                    last.then_inc(z_done, 1)

            mix_bank = (0, 2, 4, 0)

            def mix(t, groups):
                for g in groups:
                    sl = weights("pool", g // 2)
                    for k in range(2):
                        at = ((g % 2) * 2 + k) * GD
                        last = mm3(bank[mix_bank[t] + g // 2][:, g % 2 * GD:g % 2 * GD + GD],
                                   zT_hi[:, 2 * g + k, tok(t)], zT_lo[:, 2 * g + k, tok(t)],
                                   w_hi[:, sl, at:at + GD], w_lo[:, sl, at:at + GD], k == 0, k == 1)
                if groups[-1] == 3:
                    last.then_inc(mix_done, 1)

            def rows_T(t):
                pe.wait_ge(xn_ready, 3 * T + t + 1)
                pe.wait_ge(xnT_hi, 2 * T + t)
                pe.wait_ge(xnT_lo, 2 * T + t)
                transposes(xn[:, t, :], (6, 7)).then_inc(xnT_done, 1)

            def logits(t):
                pe.wait_ge(xnT_hi, 2 * T + t + 1)
                pe.wait_ge(xnT_lo, 2 * T + t + 1)
                for k in range(KD):
                    last = t_.matmul(bank[2][0:E, tok(t)], router[:, k, :], xnT[t % 2][:, k, :], start=k == 0, stop=k == KD - 1)
                if t == T - 1:
                    last.then_inc(logitsT_done, 1)

            pe.wait_ge(router_landed, 16)
            pe.wait_ge(z_lo, 4)
            mix(0, (0, 1))
            mix(1, (0, 1))
            pe.wait_ge(z_lo, KD)
            mix(0, (2, 3))
            mix(1, (2, 3))
            mix(2, (0, 1, 2, 3))
            rows_T(0)
            pe.wait_ge(h_mix, 1)
            mix(3, (0, 1, 2, 3))
            pe.wait_ge(h_mix, 2)
            for t in range(1, T):
                rows_T(t)
                logits(t - 1)
            logits(T - 1)
            pe.wait_ge(logitsT_ready, 1)
            for t in range(T):
                last = t_.transpose(bank[2][:, t * E:(t + 1) * E], logitsT[:, tok(t)], ident[0:E, 0:E])
            last.then_inc(logits_done, 1)

            pe.wait_ge(chosen, 1)
            for t in range(T):
                for c in range(t + 1):
                    last = t_.matmul(bank[5][:, t * E:(t + 1) * E], (before_b if c == t else ones_b)[:, :], picked[:, c, :],
                                     start=c == 0, stop=c == t)
            for c in range(T):
                last = t_.matmul(bank[5][:, T * E:(T + 1) * E], ones_b[:, :], picked[:, c, :], start=c == 0, stop=c == T - 1)
            last.then_inc(rank_done, 1)

            x_banks = ((1, 0), (7, 3), (3, 6))

            def first_x():
                pe.wait_ge(sel_ready, 1)
                for k in range(KD):
                    b, k0 = x_banks[k // 3]
                    at = (k - k0) * C
                    for t in range(T):
                        last = t_.matmul(bank[b][:, at:at + C], xn[:, t, k * P:(k + 1) * P], chosen_x[:, t, :],
                                         start=t == 0, stop=t == T - 1)
                last.then_inc(xT_done, 1)

            def x_T(at):
                pe.wait_ge(xg_landed, at * 16 - 16)
                for k in range(KD):
                    b, k0 = x_banks[k // 3]
                    for q in range(2):
                        col = (k - k0) * C + q * CH
                        last = t_.transpose(bank[b][:, col:col + CH], xg[:, q, k * P:(k + 1) * P], ident[0:CH, 0:CH])
                last.then_inc(xT_done, 1)

            def landed_unit(name, j, i=0, job=0):
                st = plan.stage(name, j)
                pe.wait_ge(landed[st], plan.landed(name, j, i, job))
                return stage(st)

            def columns(dst, w, n=C):
                for k in range(KD):
                    last = t_.matmul(dst[:, 0:n], w[:, k * P:(k + 1) * P], xT[:, k, 0:n], start=k == 0, stop=k == KD - 1)
                return last.then_inc(expert_used, 1)

            def gate_up(name, j, par, i=0, job=0, n=C):
                for q in range(2):
                    columns(bank[2 * par + q], landed_unit(name, j + q, i, job), n)

            def down_tile(name, j, par, prod, i, job, n, first=False, final=False):
                pe.wait_ge(prod_ready, prod)
                w = landed_unit(name, j, i, job)
                parts = FTAIL if final else P
                for k in range(KD):
                    col = k % 3 * C
                    last = t_.matmul(bank[4 + k // 3][:, col:col + n], w[0:parts, k * P:(k + 1) * P], e_act[0:parts, par, 0:n],
                                     start=first and k % 3 == 0, stop=final, skip_group_check=True)
                last.then_inc(expert_used, 1)

            pe.sem_inc(expert_used, AHEAD)
            first_x()
            pe.wait_ge(xT_ready, 1)
            gate_up("pre", 0, 0)
            pe.wait_ge(routed, 1)
            for q in range(2):
                landed_unit("pre", 2 + q)
            jobs = pe.value_load(table[0:1, 0:1], min_val=E, max_val=JMAX)
            wide = pe.value_load(table[0:1, NJ + 1:NJ + 2], min_val=1, max_val=JMAX)

            def expert_job(job, n):
                acts = job * MACTS + FT
                turns = (FEF - 2) // 2 - 1
                for q in range(2):
                    columns(bank[2 + q], stage(plan.stage("pre", 2 + q)), n)
                pe.wait_ge(y_ready, job + 1)
                pe.wait_ge(y_ready_dve, job + 1)
                down_tile("step", 0, 0, acts + 1, 0, job, n, first=True)
                gate_up("step", 1, 0, 0, job, n)
                with pe.Fori(0, turns) as i:
                    down_tile("step", 3, 1, acts + i * 2 + 2, i, job, n)
                    gate_up("step", 4, 1, i, job, n)
                    down_tile("step", 0, 0, acts + i * 2 + 3, i + 1, job, n)
                    gate_up("step", 1, 0, i + 1, job, n)
                down_tile("step", 3, 1, acts + (2 * turns + 2), turns, job, n)
                gate_up("step", 4, 1, turns, job, n)
                down_tile("tail", 0, 0, acts + FEF - 1, 0, job, n)
                columns(bank[0], landed_unit("tail", 1, 0, job), n)
                pe.wait_ge(prod_ready, acts + FEF)
                x_T(job + 2)
                down_tile("tail", 2, 1, acts + FEF, 0, job, n)
                down_tile("tail", 3, 0, acts + MACTS, 0, job, n, final=True)
                pe.wait_ge(xT_ready, job + 2)
                columns(bank[0], landed_unit("tail", 4, 0, job), n)
                for q in range(2):
                    landed_unit("tail", 6 + q, 0, job)
                pe.wait_ge(yT_ready, job + 1)
                for q in range(2):
                    for k in range(KD):
                        last = t_.transpose(bank[4 + 2 * q + k // 4][0:CH, k % 4 * P:k % 4 * P + P], yT[:, k, q * CH:(q + 1) * CH],
                                            ident[:, :])
                last.then_inc(y_nat_done, 1)
                columns(bank[1], landed_unit("tail", 5, 0, job), n)

            with pe.Fori(0, wide) as job:
                expert_job(job, C)
            with pe.Fori(wide, jobs) as job:
                expert_job(job, NARROW)

        @block.vector
        def _(dve):
            v = nc.vector
            steps = [0]

            def link(ins):
                steps[0] += 1
                ins.then_inc(dve_step, 1)
                dve.wait_ge(dve_step, steps[0])

            def split(name, j, i=0, n=UNIT):
                st, sl = plan.stage(name, j), plan.slot(name, j)
                dve.wait_ge(weight_hi, plan.unit(name, j, i) + 1)
                v.tensor_tensor(w_lo[:, sl, 0:n], stage(st)[:, 0:n], w_hi[:, sl, 0:n], ALU.subtract).then_inc(weight_lo, 1)

            def norm_rows(q, t):
                dve.wait_ge(std_ready, q + 1)
                col = q if q < 4 * T else q - 4 * T
                link(v.reciprocal(rms[:, col:col + 1], rms[:, col:col + 1]))
                if q < T:
                    dve.wait_ge(attn_gain_landed, 16)
                else:
                    dve.wait_ge(gain_landed, 16 * (q // T))
                v.scalar_tensor_tensor(xn[:, t, :], h[:, t, :], rms[:, col:col + 1], gain, ALU.mult, ALU.mult
                                       ).then_inc(xn_ready, 1)

            def norm_lo(q, t, banks=(0, 1)):
                dve.wait_ge(xnT_hi, q + 1)
                for b in range(2):
                    at = (slice(None), slice(4 * b, 4 * b + 4), slice(t * P, (t + 1) * P))
                    last = v.tensor_tensor(hnT_lo[at], bank[banks[b]][:, :].rearrange("p (k n) -> p k n", k=4), hnT_hi[at],
                                           ALU.subtract)
                last.then_inc(xnT_lo, 1)

            def rotate(out_, tmp, q, heads, t):
                n = len(range(*t.indices(T)))
                shape = [P, n, heads, ROPE]
                half = [P, n, heads, ROPE // 2]
                v.tensor_tensor(out_, q, cos_t[:, t, :].unsqueeze(2).broadcast_to(shape), ALU.mult)
                v.tensor_tensor(tmp[..., 0:32], q[..., 32:64], sin_t[:, t, 0:32].unsqueeze(2).broadcast_to(half), ALU.mult)
                link(v.tensor_tensor(tmp[..., 32:64], q[..., 0:32], sin_t[:, t, 32:64].unsqueeze(2).broadcast_to(half),
                                     ALU.mult))
                return v.tensor_tensor(out_, out_, tmp, ALU.add)

            def latents(t):
                dve.wait_ge(c_std, t + 1)
                v.reciprocal(rms[:, 16 + t:17 + t], rms[:, 16 + t:17 + t])
                link(v.reciprocal(rms[:, 20 + t:21 + t], rms[:, 20 + t:21 + t]))
                b = 4 + 2 * (t % 2)
                c = cn[:, t % 2, :]
                v.scalar_tensor_tensor(c[:, 0:QR], bank[b][:, :], rms[:, 16 + t:17 + t], gain_c[:, 0:QR], ALU.mult, ALU.mult)
                v.scalar_tensor_tensor(c[:, QR:QR + KVR], bank[b + 1][:, 0:KVR], rms[:, 20 + t:21 + t], gain_c[:, QR:],
                                       ALU.mult, ALU.mult)
                kr = c[:, QR + KVR:DOWN]
                link(rotate(kr.unsqueeze(1).unsqueeze(1), krope_tmp[:, 0, :].unsqueeze(1).unsqueeze(1),
                            bank[b + 1][:, KVR:KVR + ROPE].unsqueeze(1).unsqueeze(1), 1, slice(t, t + 1)))
                v.tensor_copy(c[:, DOWN:DOWN + ROPE], kr).then_inc(c_ready, 1)

            def latents_lo(t):
                dve.wait_ge(cT_hi, t + 1)
                tok = slice(t * P, (t + 1) * P)
                v.tensor_tensor(cqT_lo[:, :, tok], bank[2][:, :].rearrange("p (k n) -> p k n", k=4), cqT_hi[:, :, tok],
                                ALU.subtract)
                v.tensor_copy(krT[:, tok], bank[3][:, 2 * P:3 * P])
                v.tensor_tensor(ckvT_lo[:, :, tok], bank[3][:, 0:2 * P].rearrange("p (k n) -> p k n", k=2),
                                ckvT_hi[:, :, tok], ALU.subtract).then_inc(cT_lo, 1)

            dve.wait_ge(pos_landed, 16)
            dve.wait_ge(freq_landed, 16)
            link(v.tensor_copy(posf, posi[:, :]))
            link(v.tensor_tensor(angle, posf.unsqueeze(2).broadcast_to([P, T, 32]),
                                 freq.unsqueeze(1).broadcast_to([P, T, 32]), ALU.mult))
            link(v.tensor_scalar(turns, angle, 1 / (2 * np.pi), ROUND, ALU.mult, ALU.add))
            link(v.tensor_scalar(turns, turns, ROUND, None, ALU.subtract))
            norm_rows(0, 0)
            for part in TWO_PI:
                link(v.scalar_tensor_tensor(angle, turns, -part, angle, ALU.mult, ALU.add))
            link(v.tensor_scalar(over, angle, np.pi / 2, 2 * np.pi, ALU.is_gt, ALU.mult))
            link(v.scalar_tensor_tensor(folded, angle, np.pi / 2, over, ALU.add, ALU.subtract))
            v.tensor_scalar(trig_arg[:, 0], angle, PI_IN, -PI_IN, ALU.min, ALU.max)
            v.tensor_scalar(trig_arg[:, 1], folded, PI_IN, -PI_IN, ALU.min, ALU.max)
            link(v.tensor_scalar(over, angle, -1.0, None, ALU.mult))
            v.tensor_scalar(trig_arg[:, 2], over, PI_IN, -PI_IN, ALU.min, ALU.max).then_inc(trig_ready, 1)
            split("down", 0, n=DOWN)
            norm_lo(0, 0)
            for k in range(1, 4):
                split("down", k, n=DOWN)
            norm_rows(1, 1)
            for k in range(4, 8):
                split("down", k, n=DOWN)
            norm_lo(1, 1)
            norm_rows(2, 2)
            norm_rows(3, 3)
            dve.wait_ge(counts_ready, len(WINDOWS))
            v.reciprocal(band0[:, :, :], band0[:, :, :]).then_inc(counts_inv, 1)
            dve.wait_ge(trig_done, 1)
            dve.wait_ge(gainc_landed, 32)
            latents(0)
            norm_lo(2, 2)
            norm_lo(3, 3)
            latents_lo(0)
            latents(1)
            latents_lo(1)
            latents(2)
            for name, n in (("rope", 0), ("rope", 1), ("pair", 0)):
                split(name, n)

            def rotate_q(t):
                dve.wait_ge(rope_done, t + 1)
                if t == 2:
                    dve.wait_ge(ropeT_done, 1)
                shape = "p (t h n) -> p t h n"
                q, out_, tmp = (m.rearrange(shape, t=1, h=H) for m in (bank[rope_bank[t]][:, :], rotated[t], rope_tmp[t]))
                rotate(out_, tmp, q, H, slice(t, t + 1)).then_inc(rope_ready, 1)

            def k_out(pair, hd):
                dve.wait_ge(k_done, 2 * pair + (hd + 1))
                v.tensor_copy(kn[:, hd, :], bank[5][:, :]).then_inc(k_ready, 1)

            def v_out(hd):
                for b in range(2):
                    last = v.tensor_copy(v_nat[:, 2 * b:2 * b + 2, hd * VD:(hd + 1) * VD],
                                         bank[6 + b][:, :].rearrange("p (t h n) -> p t h n", t=2, h=2)[:, :, hd, :])
                last.then_inc(v_ready, 1)

            rotate_q(0)
            latents_lo(2)
            latents(3)
            rotate_q(1)
            split("pair", 1)
            latents_lo(3)
            rotate_q(2)
            rotate_q(3)
            k_out(0, 0)
            dve.wait_ge(ropeT_done, T)
            dve.wait_ge(v_done, 1)
            v_out(0)
            v_out(1)
            k_out(0, 1)
            for j in range(2):
                split("pair", j, 1)
            dve.sem_inc(o_lo, 1)

            def attention(pair, more, between):
                def softmax(hd):
                    def largest(qb):
                        col = 4 * hd + qb
                        dve.wait_ge(scores_done, pair * 8 + col + 1)
                        v.tensor_reduce(neg_max[:, col:col + 1], bank[qb][:, 0:(qb + 1) * P], AX.X, ALU.max, negate=True
                                        ).then_inc(max_ready, 1)

                    def divide(qb):
                        col = 4 * hd + qb
                        at, n = qb * (qb + 1) // 2 * P, (qb + 1) * P
                        dve.wait_ge(exp_ready, pair * 8 + col + 1)
                        v.reciprocal(row_inv[:, col:col + 1], row_sum[:, col:col + 1]).then_inc(inv_ready, 1)
                        dve.wait_ge(inv_ready, pair * 8 + col + 1)
                        v.tensor_scalar(probs[:, hd, at:at + n], probs[:, hd, at:at + n], row_inv[:, col:col + 1], None,
                                        ALU.mult).then_inc(probs_ready, 1)

                    largest(0)
                    largest(1)
                    for qb in range(T):
                        divide(qb)
                        if qb + 2 < T:
                            largest(qb + 2)

                def turned(hd):
                    dve.wait_ge(pT_done, pair * 2 + hd + 1)
                    v.tensor_copy(probsT[:, 512:896], bank[1][:, 0:384]).then_inc(pT_dve, 1)

                def head_out(hd):
                    dve.wait_ge(o_hi, pair * 2 + hd + 1)
                    at = bass.ds(pair * 2 + hd, 1)
                    v.tensor_tensor(oT_lo[:, at, :], bank[3][:, :].unsqueeze(1), oT_hi[:, at, :],
                                    ALU.subtract).then_inc(o_lo, 1)

                softmax(0)
                between(0)
                turned(0)
                if more:
                    k_out(pair + 1, 0)
                head_out(0)
                softmax(1)
                if more:
                    dve.wait_ge(v_done, pair + 2)
                    v_out(0)
                between(1)
                turned(1)
                if more:
                    k_out(pair + 1, 1)
                between(2)
                head_out(1)
                if more:
                    v_out(1)
                between(3)

            def next_pair(pair):
                return lambda place: split("pair", place - 2, pair + 2) if place >= 2 else None

            with dve.Fori(0, H // 2 - 2) as pair:
                attention(pair, True, next_pair(pair))
            attention(H // 2 - 2, True, lambda place: [split("wo", k) for k in ((0,), (1, 2), (3,), (4, 5))[place]])
            attention(H // 2 - 1, False, lambda place: [split("wo", k) for k in ((6,), (7,), (), ())[place]])

            def add_attention(t):
                if t < T - 1:
                    dve.wait_ge(wo_done, t + 1)
                else:
                    dve.wait_ge(wo_freed, H)
                for half in range(2):
                    at = slice(512 * half, 512 * half + 512)
                    last = v.tensor_tensor(h[:, t, at], bank[4 + 2 * (t % 2) + half][:, :], h[:, t, at], ALU.add)
                last.then_inc(h_attn, 1)

            for t in range(T):
                if t == T - 1:
                    split("ffn", 0)
                    norm_lo(T + 2, 2)
                    split("ffn", 1)
                add_attention(t)
                norm_rows(T + t, t)
                if 0 < t < T - 1:
                    norm_lo(T + t - 1, t - 1)
            norm_lo(2 * T - 1, T - 1, banks=(2, 3))
            split("ffn", 2)
            split("ffn", 3)

            def ffn_act(i, j):
                n = i * FG + j + 1
                dve.wait_ge(silu_ready, n)
                v.tensor_tensor(f_act[:, j % 2, :], f_silu[:, j % 2, :], bank[2 * (j % 2) + 1][:, :], ALU.mult
                                ).then_inc(prod_ready, 1)
                dve.wait_ge(act_hi, n)
                v.tensor_tensor(f_lo[:, j, :], f_act[:, j % 2, :], f_hi[:, j, :], ALU.subtract).then_inc(act_lo, 1)

            def pool_scale():
                dve.wait_ge(pscale_landed, 16)
                for j in range(2):
                    dve.wait_ge(landed[plan.stage("pool", j)], plan.landed("pool", j))
                    w = stage(plan.stage("pool", j)).rearrange("p (g k n) -> p g k n", g=2, k=2)
                    scale = pscale[:, 512 * j:512 * j + 512].rearrange("p (g n) -> p g n", g=2)
                    v.tensor_tensor(w, w, scale.unsqueeze(2).broadcast_to([P, 2, 2, GD]), ALU.mult).then_inc(pool_scaled, 1)

            def ffn(i, following, scaling=None):
                ffn_act(i, 0)
                for j in range(4, 9):
                    split("ffn", j, i)
                ffn_act(i, 1)
                ffn_act(i, 2)
                if scaling:
                    scaling()
                for half in range(2):
                    following(half)
                    at = slice(512 * half, 512 * half + 512)
                    for t in range(T):
                        dve.wait_ge(ffn_done, i * 8 + 4 * half + t + 1)
                        v.tensor_tensor(h[:, t, at], bank[4 + t][:, :], h[:, t, at], ALU.add).then_inc(h_ffn, 1)

            with dve.Fori(0, FI - 1) as i:
                ffn(i, lambda half: [split("ffn", 2 * half + j, i + 1) for j in range(2)])
            ffn(FI - 1, lambda half: split("pool", half), pool_scale)

            for t in range(T):
                norm_rows(2 * T + t, t)
            for d in range(KD):
                dve.wait_ge(z_hi, d + 1)
                v.tensor_tensor(zT_lo[:, d, :], bank[d][:, :], zT_hi[:, d, :], ALU.subtract).then_inc(z_lo, 1)

            def rows_T(t):
                dve.wait_ge(xnT_done, 2 * T + t + 1)
                v.tensor_copy(xnT[t % 2][:, 4:8, :], bank[7][:, :].rearrange("p (k n) -> p k n", k=4)).then_inc(xnT_lo, 1)

            def add_mix(t):
                dve.wait_ge(mix_done, t + 1)
                for half in range(2):
                    at = slice(512 * half, 512 * half + 512)
                    last = v.tensor_tensor(h[:, t, at], bank[(0, 2, 4, 0)[t] + half][:, :], h[:, t, at], ALU.add)
                last.then_inc(h_mix, 1)

            add_mix(0)
            add_mix(1)
            norm_rows(3 * T, 0)
            add_mix(2)
            norm_rows(3 * T + 1, 1)
            rows_T(0)
            norm_rows(3 * T + 2, 2)
            add_mix(3)
            rows_T(1)
            norm_rows(3 * T + 3, 3)
            rows_T(2)
            rows_T(3)
            dve.wait_ge(logitsT_done, 1)
            v.tensor_copy(logitsT, bank[2][0:E, :]).then_inc(logitsT_ready, 1)

            def tab(n, width=T * E):
                return route[:, n * 32:n * 32 + width]

            def by_expert(n):
                return tab(n).rearrange("p (t e) -> p t e", t=T)

            def per_token(x):
                return x.unsqueeze(2).broadcast_to([P, T, E])

            def per_expert(x):
                return x.unsqueeze(1).broadcast_to([P, T, E])

            logit, eq, first, second, spare = (by_expert(n) for n in range(5))
            best = [tab(5 + n, T) for n in range(4)]
            index, count, is_wide, start_of, by_start = (tab(9 + n, E) for n in range(5))
            runs, ends, starts, spare16 = (tab(14 + n, 2 * E) for n in range(4))
            place_f = tab(18, 2 * T)
            job_exp, job_hi = (tab(19 + n, NJ)[0:1] for n in range(2))
            ended = route[0:1, 21 * 32:21 * 32 + NJ * 2 * E].rearrange("p (j e) -> p j e", e=2 * E)
            dve.wait_ge(logits_done, 1)
            dve.wait_ge(iotas_ready, 3)
            v.tensor_scalar(index, iota_e[:, :], -float(E), None, ALU.add)
            link(v.tensor_copy(tab(0), bank[2][:, 0:T * E]))

            def pick(logits, top, at, onehot):
                link(v.tensor_reduce(top, logits, AX.X, ALU.max))
                link(v.tensor_tensor(eq, logits, per_token(top), ALU.is_equal))
                link(v.tensor_tensor(eq, eq, per_expert(index), ALU.mult))
                link(v.tensor_reduce(at, eq, AX.X, ALU.min))
                link(v.tensor_tensor(onehot, per_expert(index), per_token(at), ALU.is_equal))

            pick(logit, best[0], best[1], first)
            link(v.scalar_tensor_tensor(spare, first, -1e38, logit, ALU.mult, ALU.add))
            pick(spare, best[2], best[3], second)
            link(v.tensor_tensor(gate1[:, :], best[2], best[0], ALU.subtract))
            v.tensor_tensor(picked[:, :, :], first, second, ALU.add).then_inc(chosen, 1)
            dve.wait_ge(rank_done, 1)
            rank = bank[5][:, 0:T * E].rearrange("p (t e) -> p t e", t=T)
            slot0 = best[0]
            link(v.tensor_tensor(slot0, first[:, :, 0], second[:, :, 0], ALU.add))
            link(v.tensor_scalar(slot0, slot0, -2.0 * S, 2.0 * S, ALU.mult, ALU.add))
            link(v.tensor_tensor(slot0, slot0, rank[:, :, 0], ALU.add))
            for t in range(T):
                last = v.tensor_scalar(chosen_x[:, t, :], iota_c, slot0[:, t:t + 1], None, ALU.is_equal)
            last.then_inc(sel_ready, 1)
            dve.wait_ge(exp_gate, 1)
            link(v.tensor_scalar(gate0[:, :], gate1[:, :], 1.0, None, ALU.add))
            link(v.reciprocal(gate0[:, :], gate0[:, :]))
            link(v.tensor_tensor(gate1[:, :], gate1[:, :], gate0[:, :], ALU.mult))

            link(v.tensor_copy(count, bank[5][:, T * E:(T + 1) * E]))
            link(v.tensor_scalar(start_of, count, float(C), 1.0, ALU.is_gt, ALU.add))
            for more in range(2, -(-S // C)):
                link(v.scalar_tensor_tensor(start_of, count, float(more * C), start_of, ALU.is_gt, ALU.add))
            link(v.tensor_scalar(is_wide, count, float(NARROW), None, ALU.is_gt))
            link(v.scalar_tensor_tensor(is_wide, iota_e[:, :], 0.5, is_wide, ALU.is_lt, ALU.max))
            link(v.tensor_tensor(runs[:, 0:E], start_of, is_wide, ALU.mult))
            link(v.tensor_tensor(runs[:, E:], start_of, runs[:, 0:E], ALU.subtract))
            link(v.tensor_copy(ends, runs))
            for shift in (1, 2, 4, 8):
                link(v.tensor_copy(spare16, ends))
                link(v.tensor_tensor(ends[:, shift:], spare16[:, shift:], spare16[:, 0:2 * E - shift], ALU.add))
            link(v.tensor_tensor(starts, ends, runs, ALU.subtract))
            link(v.tensor_tensor(start_of, starts[:, 0:E], starts[:, E:], ALU.subtract))
            link(v.tensor_tensor(start_of, start_of, is_wide, ALU.mult))
            link(v.tensor_tensor(start_of, start_of, starts[:, E:], ALU.add))
            link(v.tensor_scalar(by_start, start_of, float(C), None, ALU.mult))
            link(v.tensor_tensor(spare, rank, per_expert(by_start), ALU.add))
            for n, onehot in enumerate((first, second)):
                link(v.tensor_tensor(eq, onehot, spare, ALU.mult))
                link(v.tensor_reduce(place_f[:, n * T:(n + 1) * T], eq, AX.X, ALU.add))
            v.tensor_copy(dest[:, :], place_f).then_inc(placed, 1)
            link(v.tensor_tensor(ended, ends[0:1, :].unsqueeze(1).broadcast_to([1, NJ, 2 * E]),
                                 iota_j[0:1, :].unsqueeze(2).broadcast_to([1, NJ, 2 * E]), ALU.is_le))
            link(v.tensor_reduce(job_exp, ended, AX.X, ALU.add))
            link(v.tensor_scalar(job_hi, job_exp, float(E), -float(E), ALU.is_ge, ALU.mult))
            link(v.tensor_tensor(job_exp, job_exp, job_hi, ALU.add))
            link(v.tensor_scalar(job_exp, job_exp, float(E - 1), None, ALU.min))
            link(v.scalar_tensor_tensor(job_hi[:, 0:1], ends[0:1, E - 1:E], 1.0, ends[0:1, 2 * E - 1:], ALU.add, ALU.max))
            link(v.tensor_copy(table[0:1, 0:1], job_hi[:, 0:1]))
            link(v.tensor_copy(table[0:1, NJ + 1:NJ + 2], ends[0:1, E - 1:E]))
            v.tensor_copy(table[0:1, 1:NJ + 1], job_exp).then_inc(routed, 1)

            def x_out(at):
                dve.wait_ge(xT_done, at)
                for b, k0, k1 in ((1, 0, 3), (7, 3, 6), (3, 6, 8)):
                    last = v.tensor_copy(xT[:, k0:k1, :], bank[b][:, 0:(k1 - k0) * C].rearrange("p (k n) -> p k n", n=C))
                last.then_inc(xT_ready, 1)

            dve.wait_ge(routed, 1)
            x_out(1)
            dve.sem_inc(y_ready_dve, 1)
            jobs = dve.value_load(table[0:1, 0:1], min_val=E, max_val=JMAX)
            wide = dve.value_load(table[0:1, NJ + 1:NJ + 2], min_val=1, max_val=JMAX)

            def expert_job(job, n):
                def product(f, par):
                    dve.wait_ge(silu_ready, job * MACTS + f + (FT + 1))
                    v.tensor_tensor(e_act[:, par, 0:n], e_silu[:, par, 0:n], bank[2 * par + 1][:, 0:n], ALU.mult
                                    ).then_inc(prod_ready, 1)

                with dve.Fori(0, FEF // 2) as i:
                    for q in range(2):
                        product(i * 2 + q, q)
                dve.wait_ge(silu_ready, job * MACTS + (FT + MACTS))
                v.tensor_tensor(e_act[0:FTAIL, 0, 0:n], e_silu[0:FTAIL, 0, 0:n], e_up[0:FTAIL, 0:n], ALU.mult
                                ).then_inc(prod_ready, 1)
                x_out(job + 2)
                dve.wait_ge(y_nat_done, job + 1)
                dve.wait_ge(yn_free, job + 1)
                for b in range(2):
                    last = v.tensor_copy(yn[:, 1, b * 512:b * 512 + 512], bank[6 + b][0:CH, :])
                last.then_inc(y_ready_dve, 1)

            with dve.Fori(0, wide) as job:
                expert_job(job, C)
            with dve.Fori(wide, jobs) as job:
                expert_job(job, NARROW)

            def final_norm(t):
                dve.wait_ge(std_ready, 4 * T + t + 1)
                link(v.reciprocal(rms[:, t:t + 1], rms[:, t:t + 1]))
                dve.wait_ge(final_landed, 16)
                v.scalar_tensor_tensor(y_in[:, 2 * t, :], h[:, t, :], rms[:, t:t + 1], gain, ALU.mult, ALU.mult
                                       ).then_inc(out_ready, 1)

            for t in range(T):
                dve.wait_ge(y_gathered[2 * t], 16)
                link(v.scalar_tensor_tensor(h[:, t, :], y_in[:, 2 * t, :], gate0[:, t:t + 1], h[:, t, :], ALU.mult, ALU.add))
                dve.wait_ge(y_gathered[2 * t + 1], 16)
                v.scalar_tensor_tensor(h[:, t, :], y_in[:, 2 * t + 1, :], gate1[:, t:t + 1], h[:, t, :], ALU.mult, ALU.add
                                       ).then_inc(h_final, 1)
                if t:
                    final_norm(t - 1)
            final_norm(T - 1)


_INS = ["x", "positions", "attn_norm", "ffn_norm", "mla_w_down", "mla_q_norm", "mla_w_uq", "mla_kv_norm", "mla_w_ukv",
        "mla_w_o", "pool_w", "pool_scale", "ffn_w_gate", "ffn_w_up", "ffn_w_down", "moe_router", "moe_w_gate", "moe_w_up",
        "moe_w_down", "final_norm"]


def kernel(**inputs):
    import concourse.bacc as _bacc
    from concourse.bass_utils import run_bass_kernel_spmd as _run

    nc = _bacc.Bacc("TRN2", target_bir_lowering=False, num_devices=1)
    arrays = {name: np.ascontiguousarray(inputs[name]) for name in _INS}
    arrays["rope_freq"] = (THETA ** (-np.arange(0, ROPE, 2, dtype=np.float64) / ROPE)).astype(np.float32)[None, :]
    args = {name: nc.dram_tensor(f"in_{name}", v.shape, mybir.dt.from_np(v.dtype), kind="ExternalInput").ap()
            for name, v in arrays.items()}
    out = nc.dram_tensor("out_0", (1, S, D), F32, kind="ExternalOutput").ap()
    trunk(nc, args, out)
    r = _run(nc, [{f"in_{name}": v for name, v in arrays.items()}], core_ids=[0])
    return r.results[0]["out_0"]
```
